# Optimizing a Trainium2 kernel written in Bass

```python
import jax, jax.numpy as jnp
from jax import lax
import numpy as np

D_MODEL = 1024
BATCH = 1
SEQ = 256
DEPTH = 2

GRID_W = 64
CTX_LEN = 256
D_FF = ((8 * D_MODEL // 3 + 255) // 256) * 256
HALF_STEP = 0.5
N_MOD = 9
RMS_EPS = 1e-6
NEG_INF = -1e30

CONV_CH = D_MODEL // 4
CONV_K = 3
POOL_CH = D_MODEL // 4
POOL_WINDOWS = (2, 4, 8, 16)
POOL_GROUP = POOL_CH // 4
NA_HEAD_DIM = 64
NA_CH = D_MODEL // 2
NA_HEADS = NA_CH // NA_HEAD_DIM
NA_KH_MAX = 8
NA_KW = 16
NA_QC = 16
NA_KB = NA_QC + NA_KW - 1
D_MIX = CONV_CH + POOL_CH + NA_CH
OFF_B = CONV_CH
OFF_C = 2 * CONV_CH
OFF_P = 3 * CONV_CH
OFF_Q = 3 * CONV_CH + POOL_CH
OFF_K = OFF_Q + NA_CH
OFF_V = OFF_K + NA_CH
D_IN = OFF_V + NA_CH


def rms_norm(x, g):
    xf = x.astype(jnp.float32)
    y = xf * lax.rsqrt(jnp.mean(xf * xf, axis=-1, keepdims=True) + RMS_EPS)
    return (y * g.astype(jnp.float32)).astype(x.dtype)

def mod_norm(x, m, i, g):
    return rms_norm(x, g) * (1 + m[:, 3 * i + 1, None]) + m[:, 3 * i, None]

def swiglu(h, w1, w2):
    a, b = jnp.split(h @ w1, 2, axis=-1)
    return (jax.nn.silu(a) * b) @ w2

def ffn_sublayer(x, m, i, g, w1, w2):
    return x + HALF_STEP * m[:, 3 * i + 2, None] * swiglu(mod_norm(x, m, i, g), w1, w2)

def short_conv(u, w):
    return lax.conv_general_dilated(
        u, w[:, None, :].astype(u.dtype), window_strides=(1,),
        padding=[(CONV_K // 2, CONV_K // 2)],
        dimension_numbers=('NWC', 'WIO', 'NWC'), feature_group_count=u.shape[-1])

def gated_conv_mixer(h, b_gate, c_gate, conv_w):
    return b_gate * short_conv(c_gate * h, conv_w)

def multiscale_pool_mixer(v, pool_w, pool_scale):
    L = v.shape[1]
    vf = v.astype(jnp.float32)
    cs = jnp.concatenate([jnp.zeros_like(vf[:, :1]), jnp.cumsum(vf, axis=1)], axis=1)
    t = jnp.arange(L)
    outs = []
    for g, w in enumerate(POOL_WINDOWS):
        left = w // 2
        right = w - 1 - left
        lo = jnp.clip(t - left, 0, L)
        hi = jnp.clip(t + right + 1, 0, L)
        sl = slice(g * POOL_GROUP, (g + 1) * POOL_GROUP)
        mean = (cs[:, hi, sl] - cs[:, lo, sl]) / (hi - lo).astype(jnp.float32)[None, :, None]
        outs.append((mean - vf[..., sl]).astype(v.dtype) @ pool_w[g])
    return jnp.concatenate(outs, axis=-1) * pool_scale

def context_attention(q, k, v):
    B, L = q.shape[:2]
    s = jnp.einsum('bqhd,bkhd->bhqk', q, k, preferred_element_type=jnp.float32) * (NA_HEAD_DIM ** -0.5)
    p = jax.nn.softmax(s, axis=-1).astype(v.dtype)
    return jnp.einsum('bhqk,bkhd->bqhd', p, v).reshape(B, L, NA_CH)

def neighbourhood_attention(q, k, v, k_ctx, v_ctx, rpb):
    B, S = q.shape[:2]
    rows = S // GRID_W
    kh = min(NA_KH_MAX, rows)
    nj = GRID_W // NA_QC
    scale = NA_HEAD_DIM ** -0.5
    qg = q.reshape(B, rows, GRID_W, NA_HEADS, NA_HEAD_DIM)
    kg = k.reshape(B, rows, GRID_W, NA_HEADS, NA_HEAD_DIM)
    vg = v.reshape(B, rows, GRID_W, NA_HEADS, NA_HEAD_DIM)
    qcol = jnp.arange(GRID_W).reshape(nj, NA_QC)
    band0 = jnp.clip(jnp.arange(nj) * NA_QC - NA_KW // 2, 0, GRID_W - NA_KB)
    kcol = band0[:, None] + jnp.arange(NA_KB)
    cstart = jnp.clip(qcol - NA_KW // 2, 0, GRID_W - NA_KW)
    col_valid = (kcol[:, None, :] >= cstart[..., None]) & (kcol[:, None, :] < cstart[..., None] + NA_KW)
    col_off = kcol[:, None, :] - qcol[..., None] + NA_KW - 1
    n_loc = kh * NA_KB

    def row_block(r):
        rs = jnp.clip(r - kh // 2, 0, rows - kh)
        q_r = lax.dynamic_index_in_dim(qg, r, axis=1, keepdims=False).reshape(
            B, nj, NA_QC, NA_HEADS, NA_HEAD_DIM)
        k_b = lax.dynamic_slice_in_dim(kg, rs, kh, axis=1)[:, :, kcol]
        v_b = lax.dynamic_slice_in_dim(vg, rs, kh, axis=1)[:, :, kcol]
        row_off = rs + jnp.arange(kh) - r + NA_KH_MAX - 1
        bias = rpb[:, row_off[None, None, :, None], col_off[:, :, None, :]].astype(jnp.float32)
        bias = jnp.where(col_valid[None, :, :, None, :], bias, NEG_INF)
        s_loc = jnp.einsum('bjqhd,bijkhd->bhjqik', q_r, k_b,
                           preferred_element_type=jnp.float32) * scale + bias
        s_ctx = jnp.einsum('bjqhd,bchd->bhjqc', q_r, k_ctx,
                           preferred_element_type=jnp.float32) * scale
        s = jnp.concatenate([s_loc.reshape(B, NA_HEADS, nj, NA_QC, n_loc), s_ctx], axis=-1)
        p = jax.nn.softmax(s, axis=-1).astype(v.dtype)
        p_loc = p[..., :n_loc].reshape(B, NA_HEADS, nj, NA_QC, kh, NA_KB)
        o = (jnp.einsum('bhjqik,bijkhd->bjqhd', p_loc, v_b)
             + jnp.einsum('bhjqc,bchd->bjqhd', p[..., n_loc:], v_ctx))
        return o.reshape(B, GRID_W, NA_CH)

    out = lax.map(row_block, jnp.arange(rows))
    return out.transpose(1, 0, 2, 3).reshape(B, S, NA_CH)

def heads(t):
    return t.reshape(t.shape[0], t.shape[1], NA_HEADS, NA_HEAD_DIM)

def first_inputs(seed: int = 0) -> dict:
    key = jax.random.key(seed)
    ks = jax.random.split(key, 16)
    f32 = jnp.float32
    nrm = lambda k, shape, s: jax.random.normal(k, shape, f32) * s
    return {
        'x': nrm(ks[0], (BATCH, SEQ, D_MODEL), 1.0),
        'c': nrm(ks[1], (BATCH, D_MODEL), 1.0),
        'ctx': nrm(ks[2], (BATCH, CTX_LEN, D_MODEL), 1.0),
        'c_ctx': nrm(ks[3], (D_MODEL,), 1.0),
        'w_mod': nrm(ks[4], (DEPTH, D_MODEL, N_MOD * D_MODEL), 0.5 * D_MODEL ** -0.5),
        'b_mod': nrm(ks[5], (DEPTH, N_MOD * D_MODEL), 0.01),
        'norm_g': 1.0 + nrm(ks[6], (DEPTH, 3, D_MODEL), 0.02),
        'ffn_w_in': nrm(ks[7], (DEPTH, 2, D_MODEL, 2 * D_FF), D_MODEL ** -0.5),
        'ffn_w_out': nrm(ks[8], (DEPTH, 2, D_FF, D_MODEL), D_FF ** -0.5),
        'w_in': nrm(ks[9], (DEPTH, D_MODEL, D_IN), D_MODEL ** -0.5),
        'conv_w': nrm(ks[10], (DEPTH, CONV_K, CONV_CH), CONV_K ** -0.5),
        'pool_w': nrm(ks[11], (DEPTH, len(POOL_WINDOWS), POOL_GROUP, POOL_GROUP), POOL_GROUP ** -0.5),
        'pool_scale': 1.0 + nrm(ks[12], (DEPTH, POOL_CH), 0.1),
        'rpb': nrm(ks[13], (DEPTH, NA_HEADS, 2 * NA_KH_MAX - 1, 2 * NA_KW - 1), 0.1),
        'w_out': nrm(ks[14], (DEPTH, D_MIX, D_MODEL), D_MIX ** -0.5),
        'final_g': 1.0 + nrm(ks[15], (D_MODEL,), 0.02),
    }

def first_block(x, c, ctx, c_ctx, w_mod, b_mod, norm_g, ffn_w_in, ffn_w_out, w_in,
              conv_w, pool_w, pool_scale, rpb, w_out, final_g):
    B = x.shape[0]
    xc = ctx
    for l in range(DEPTH):
        last = l == DEPTH - 1
        m = (jax.nn.silu(c) @ w_mod[l] + b_mod[l]).reshape(B, N_MOD, D_MODEL)
        mc = (jax.nn.silu(c_ctx) @ w_mod[l] + b_mod[l]).reshape(1, N_MOD, D_MODEL)

        x = ffn_sublayer(x, m, 0, norm_g[l, 0], ffn_w_in[l, 0], ffn_w_out[l, 0])
        xc = ffn_sublayer(xc, mc, 0, norm_g[l, 0], ffn_w_in[l, 0], ffn_w_out[l, 0])

        h = mod_norm(x, m, 1, norm_g[l, 1])
        hc = mod_norm(xc, mc, 1, norm_g[l, 1])
        u = h @ w_in[l]
        if last:
            uc_kv = hc @ w_in[l][:, OFF_K:]
            kc, vc = heads(uc_kv[..., :NA_CH]), heads(uc_kv[..., NA_CH:])
        else:
            uc = hc @ w_in[l]
            kc, vc = heads(uc[..., OFF_K:OFF_V]), heads(uc[..., OFF_V:])
            yc = jnp.concatenate([
                gated_conv_mixer(uc[..., :OFF_B], uc[..., OFF_B:OFF_C], uc[..., OFF_C:OFF_P], conv_w[l]),
                multiscale_pool_mixer(uc[..., OFF_P:OFF_Q], pool_w[l], pool_scale[l]),
                context_attention(heads(uc[..., OFF_Q:OFF_K]), kc, vc),
            ], axis=-1) @ w_out[l]
            xc = xc + mc[:, 5, None] * yc
            xc = ffn_sublayer(xc, mc, 2, norm_g[l, 2], ffn_w_in[l, 1], ffn_w_out[l, 1])
        y = jnp.concatenate([
            gated_conv_mixer(u[..., :OFF_B], u[..., OFF_B:OFF_C], u[..., OFF_C:OFF_P], conv_w[l]),
            multiscale_pool_mixer(u[..., OFF_P:OFF_Q], pool_w[l], pool_scale[l]),
            neighbourhood_attention(heads(u[..., OFF_Q:OFF_K]), heads(u[..., OFF_K:OFF_V]),
                                    heads(u[..., OFF_V:]), kc, vc, rpb[l]),
        ], axis=-1) @ w_out[l]
        x = x + m[:, 5, None] * y

        x = ffn_sublayer(x, m, 2, norm_g[l, 2], ffn_w_in[l, 1], ffn_w_out[l, 1])
    return rms_norm(x, final_g)


DEPTH_2 = 1

D_MIX_2 = D_MODEL
RET_HEADS = 4
RET_DK = 128
RET_DV = 128
RET_CHUNK = 128
NSA_HEADS = 8
NSA_KV_GROUPS = 2
NSA_HPG = NSA_HEADS // NSA_KV_GROUPS
NSA_DH = 64
CMP_LEN = 32
CMP_STRIDE = 16
CMP_HID = 256
SEL_BLOCK = 64
SEL_TOPN = 16
WINDOW = 512
Q_BLOCK = 128
FORCED_SCORE = 1e9
ROPE_THETA = 10000.0
PEER_HEADS = 8
PEER_NKEYS = 128
PEER_EXPERTS = PEER_NKEYS * PEER_NKEYS
PEER_TOPK = 16
PEER_DQ = 256
PEER_DHALF = PEER_DQ // 2
PEER_TOK_BLOCK = 128
NORM_EPS = 1e-6
KV_COLS = NSA_KV_GROUPS * NSA_DH
IN_SPLITS = (RET_HEADS * RET_DK, RET_HEADS * RET_DK, RET_HEADS * RET_DV, RET_HEADS * RET_DV,
             NSA_HEADS * NSA_DH, KV_COLS, KV_COLS, KV_COLS, KV_COLS, KV_COLS, KV_COLS,
             NSA_HEADS * 3)
IN_COLS = sum(IN_SPLITS)


def _rms_norm(x, g):
    xf = x.astype(jnp.float32)
    y = xf * lax.rsqrt(jnp.mean(xf * xf, axis=-1, keepdims=True) + NORM_EPS)
    return (y * g.astype(jnp.float32)).astype(x.dtype)

def _modulate(h, shift, scale):
    return h * (1.0 + scale[:, None, :]) + shift[:, None, :]

def _rope(x, pos):
    d = x.shape[-1]
    inv = ROPE_THETA ** (-jnp.arange(0, d, 2, dtype=jnp.float32) / d)
    ang = pos.astype(jnp.float32)[:, None] * inv[None, :]
    cos = jnp.cos(ang)[None, :, None, :].astype(x.dtype)
    sin = jnp.sin(ang)[None, :, None, :].astype(x.dtype)
    x1, x2 = jnp.split(x, 2, axis=-1)
    return jnp.concatenate([x1 * cos - x2 * sin, x2 * cos + x1 * sin], axis=-1)

def _masked_softmax(s, mask):
    s = jnp.where(mask, s, -jnp.inf)
    m = jnp.max(s, axis=-1, keepdims=True)
    m = jnp.where(jnp.isfinite(m), m, 0.0)
    e = jnp.where(mask, jnp.exp(s - m), 0.0)
    return e / jnp.maximum(jnp.sum(e, axis=-1, keepdims=True), jnp.finfo(jnp.float32).tiny)

def _retention(q, k, v, g):
    B, S, H, DK = q.shape
    DV = v.shape[-1]
    C = RET_CHUNK
    nc = S // C
    f32 = jnp.float32
    log_g = jnp.log1p(-jnp.exp2(-5.0 - jnp.arange(H, dtype=f32)))
    n = jnp.arange(C, dtype=f32)
    diff = n[:, None] - n[None, :]
    causal = diff >= 0
    dmat = jnp.where(causal[None], jnp.exp(jnp.where(causal, diff, 0.0)[None] * log_g[:, None, None]), 0.0)
    qc = q.astype(f32).reshape(B, nc, C, H, DK)
    kc = (k.astype(f32) * DK ** -0.5).reshape(B, nc, C, H, DK)
    vc = v.astype(f32).reshape(B, nc, C, H, DV)
    scores = jnp.einsum('bcnhk,bcmhk->bchnm', qc, kc) * dmat[None, None]
    inner = jnp.einsum('bchnm,bcmhv->bcnhv', scores, vc)
    zeta = jnp.exp((C - 1 - n)[None, :] * log_g[:, None])
    kv = jnp.einsum('bcmhk,bcmhv,hm->cbhkv', kc, vc, zeta)
    cdecay = jnp.exp(C * log_g)[None, :, None, None]

    def step(state, kv_c):
        return cdecay * state + kv_c, state

    _, s_prev = lax.scan(step, jnp.zeros((B, H, DK, DV), f32), kv)
    xi = jnp.exp((n + 1.0)[None, :] * log_g[:, None])
    cross = jnp.einsum('bcnhk,cbhkv,hn->bcnhv', qc, s_prev, xi)
    y = (inner + cross).reshape(B, S, H, DV)
    mu = jnp.mean(y, axis=-1, keepdims=True)
    var = jnp.mean((y - mu) ** 2, axis=-1, keepdims=True)
    y = (y - mu) * lax.rsqrt(var + NORM_EPS)
    y = jax.nn.silu(g.astype(f32)) * y
    return y.reshape(B, S, H * DV).astype(q.dtype)

def _compress(kraw, pe, w1, b1, w2):
    B, S, G, DH = kraw.shape
    ncb = (S - CMP_LEN) // CMP_STRIDE + 1
    idx = jnp.arange(ncb)[:, None] * CMP_STRIDE + jnp.arange(CMP_LEN)[None, :]
    blk = kraw[:, idx] + pe[None, None, :, None, :]
    blk = blk.transpose(0, 1, 3, 2, 4).reshape(B, ncb, G, CMP_LEN * DH)
    return jax.nn.gelu(blk @ w1 + b1) @ w2

def _nsa(q, k_c, v_c, k_s, v_s, k_w, v_w, gate_logits, pe_k, pe_v, wk1, bk1, wk2, wv1, bv1, wv2):
    B, S = q.shape[:2]
    G, HPG, DH = NSA_KV_GROUPS, NSA_HPG, NSA_DH
    f32 = jnp.float32
    kc = _compress(k_c, pe_k, wk1, bk1, wk2)
    vc = _compress(v_c, pe_v, wv1, bv1, wv2)
    ncb = kc.shape[1]
    nsel = S // SEL_BLOCK
    n_top = min(SEL_TOPN, nsel)
    nqb = S // Q_BLOCK
    cmp_start = jnp.arange(ncb) * CMP_STRIDE
    cmp_end = cmp_start + CMP_LEN - 1
    sel_start = jnp.arange(nsel) * SEL_BLOCK
    overlap = jnp.clip(jnp.minimum(cmp_start[:, None] + CMP_LEN, sel_start[None, :] + SEL_BLOCK)
                       - jnp.maximum(cmp_start[:, None], sel_start[None, :]), 0).astype(f32) / CMP_STRIDE
    ks_g = k_s.reshape(B, nsel, SEL_BLOCK, G, DH).transpose(0, 3, 1, 2, 4)
    vs_g = v_s.reshape(B, nsel, SEL_BLOCK, G, DH).transpose(0, 3, 1, 2, 4)
    kw_pad = jnp.pad(k_w, ((0, 0), (WINDOW, 0), (0, 0), (0, 0)))
    vw_pad = jnp.pad(v_w, ((0, 0), (WINDOW, 0), (0, 0), (0, 0)))
    qg = q.reshape(B, nqb, Q_BLOCK, G, HPG, DH).swapaxes(0, 1)
    gg = gate_logits.reshape(B, nqb, Q_BLOCK, G, HPG, 3).swapaxes(0, 1)
    scale = DH ** -0.5
    gather = jax.vmap(jax.vmap(lambda tbl, ix: tbl[ix]))
    blk_ids = jnp.arange(nsel)

    def body(args):
        qb, qblk, gblk = args
        t = qb * Q_BLOCK + jnp.arange(Q_BLOCK)
        s_c = jnp.einsum('bqghd,bngd->bghqn', qblk, kc).astype(f32) * scale
        p_c = _masked_softmax(s_c, cmp_end[None, :] <= t[:, None])
        o_c = jnp.einsum('bghqn,bngd->bqghd', p_c.astype(vc.dtype), vc)
        imp = jnp.einsum('bghqn,nj->bgqj', p_c, overlap)
        cur = t // SEL_BLOCK
        forced = (blk_ids[None, :] == 0) | (blk_ids[None, :] == cur[:, None]) | (blk_ids[None, :] == cur[:, None] - 1)
        imp = jnp.where(forced, FORCED_SCORE, imp)
        imp = jnp.where(blk_ids[None, :] <= cur[:, None], imp, -jnp.inf)
        top_v, top_i = lax.top_k(imp, n_top)
        ksel = gather(ks_g, top_i)
        vsel = gather(vs_g, top_i)
        pos = top_i[..., None] * SEL_BLOCK + jnp.arange(SEL_BLOCK)
        m_s = jnp.isfinite(top_v)[..., None] & (pos <= t[None, None, :, None, None])
        s_s = jnp.einsum('bqghd,bgqnkd->bghqnk', qblk, ksel).astype(f32) * scale
        p_s = _masked_softmax(s_s.reshape(B, G, HPG, Q_BLOCK, n_top * SEL_BLOCK),
                              m_s.reshape(B, G, 1, Q_BLOCK, n_top * SEL_BLOCK))
        o_s = jnp.einsum('bghqm,bgqmd->bqghd', p_s.astype(vsel.dtype),
                         vsel.reshape(B, G, Q_BLOCK, n_top * SEL_BLOCK, DH))
        kwb = lax.dynamic_slice_in_dim(kw_pad, qb * Q_BLOCK, Q_BLOCK + WINDOW, axis=1)
        vwb = lax.dynamic_slice_in_dim(vw_pad, qb * Q_BLOCK, Q_BLOCK + WINDOW, axis=1)
        sp = qb * Q_BLOCK - WINDOW + jnp.arange(Q_BLOCK + WINDOW)
        m_w = (sp[None, :] >= 0) & (sp[None, :] <= t[:, None]) & (sp[None, :] > t[:, None] - WINDOW)
        s_w = jnp.einsum('bqghd,bkgd->bghqk', qblk, kwb).astype(f32) * scale
        p_w = _masked_softmax(s_w, m_w)
        o_w = jnp.einsum('bghqk,bkgd->bqghd', p_w.astype(vwb.dtype), vwb)
        gate = jax.nn.sigmoid(gblk.astype(f32))
        out = gate[..., 0:1] * o_c + gate[..., 1:2] * o_s + gate[..., 2:3] * o_w
        return out.astype(qblk.dtype)

    out = lax.map(body, (jnp.arange(nqb), qg, gg))
    return out.swapaxes(0, 1).reshape(B, S, NSA_HEADS * DH)

def _peer(h, w_q, subkeys, w_down, w_up):
    B, S, D = h.shape
    TB = PEER_TOK_BLOCK
    nb = S // TB
    hb = h.reshape(B, nb, TB, D).swapaxes(0, 1)

    def body(hblk):
        q = (hblk @ w_q).reshape(B, TB, PEER_HEADS, 2, PEER_DHALF)
        s = jnp.einsum('btphd,phnd->btphn', q, subkeys).astype(jnp.float32)
        v, i = lax.top_k(s, PEER_TOPK)
        cand = (v[..., 0, :, None] + v[..., 1, None, :]).reshape(B, TB, PEER_HEADS, PEER_TOPK * PEER_TOPK)
        cidx = (i[..., 0, :, None] * PEER_NKEYS + i[..., 1, None, :]).reshape(B, TB, PEER_HEADS, PEER_TOPK * PEER_TOPK)
        tv, tj = lax.top_k(cand, PEER_TOPK)
        eidx = jnp.take_along_axis(cidx, tj, axis=-1)
        w = jax.nn.softmax(tv, axis=-1)
        u = w_down[eidx]
        a = jax.nn.gelu(jnp.einsum('btd,btpkd->btpk', hblk, u).astype(jnp.float32))
        vv = w_up[eidx]
        return jnp.einsum('btpk,btpkd->btd', (w * a).astype(hblk.dtype), vv)

    out = lax.map(body, hb)
    return out.swapaxes(0, 1).reshape(B, S, D)

def second_inputs(seed: int = 0) -> dict:
    key = jax.random.key(seed)
    ks = jax.random.split(key, 24)
    L = DEPTH_2

    def nrm(k, shape, s):
        return jax.random.normal(k, shape, jnp.float32) * s

    return {
        "x": nrm(ks[0], (BATCH, SEQ, D_MODEL), 1.0),
        "c": nrm(ks[1], (BATCH, D_MODEL), 1.0),
        "w_ada": nrm(ks[2], (L, D_MODEL, 6 * D_MODEL), 0.5 * D_MODEL ** -0.5),
        "b_ada": nrm(ks[3], (L, 6 * D_MODEL), 0.02),
        "g_norm_mix": 1.0 + nrm(ks[4], (L, D_MODEL), 0.02),
        "w_in": nrm(ks[5], (L, D_MODEL, IN_COLS), D_MODEL ** -0.5),
        "pe_cmp_k": nrm(ks[6], (L, CMP_LEN, NSA_DH), 0.1),
        "pe_cmp_v": nrm(ks[7], (L, CMP_LEN, NSA_DH), 0.1),
        "w_cmp_k1": nrm(ks[8], (L, CMP_LEN * NSA_DH, CMP_HID), (CMP_LEN * NSA_DH) ** -0.5),
        "b_cmp_k1": nrm(ks[9], (L, CMP_HID), 0.02),
        "w_cmp_k2": nrm(ks[10], (L, CMP_HID, NSA_DH), CMP_HID ** -0.5),
        "w_cmp_v1": nrm(ks[11], (L, CMP_LEN * NSA_DH, CMP_HID), (CMP_LEN * NSA_DH) ** -0.5),
        "b_cmp_v1": nrm(ks[12], (L, CMP_HID), 0.02),
        "w_cmp_v2": nrm(ks[13], (L, CMP_HID, NSA_DH), CMP_HID ** -0.5),
        "w_out": nrm(ks[14], (L, D_MIX_2, D_MODEL), D_MIX_2 ** -0.5),
        "g_norm_ffn": 1.0 + nrm(ks[15], (L, D_MODEL), 0.02),
        "w_peer_q": nrm(ks[16], (L, D_MODEL, PEER_HEADS * PEER_DQ), D_MODEL ** -0.5),
        "peer_subkeys": nrm(ks[17], (L, PEER_HEADS, 2, PEER_NKEYS, PEER_DHALF), PEER_DHALF ** -0.5),
        "peer_down": nrm(ks[18], (L, PEER_EXPERTS, D_MODEL), D_MODEL ** -0.5),
        "peer_up": nrm(ks[19], (L, PEER_EXPERTS, D_MODEL), PEER_HEADS ** -0.5),
        "g_norm_final": 1.0 + nrm(ks[20], (D_MODEL,), 0.02),
    }

def second_block(x, c, w_ada, b_ada, g_norm_mix, w_in, pe_cmp_k, pe_cmp_v, w_cmp_k1, b_cmp_k1, w_cmp_k2,
              w_cmp_v1, b_cmp_v1, w_cmp_v2, w_out, g_norm_ffn, w_peer_q, peer_subkeys, peer_down, peer_up,
              g_norm_final):
    B, S, D = x.shape
    pos = jnp.arange(S)
    split_points = [int(v) for v in np.cumsum(IN_SPLITS)[:-1]]
    for l in range(DEPTH_2):
        mod = jax.nn.silu(c) @ w_ada[l] + b_ada[l]
        sh1, sc1, ga1, sh2, sc2, ga2 = jnp.split(mod, 6, axis=-1)
        h = _modulate(_rms_norm(x, g_norm_mix[l]), sh1, sc1)
        proj = h @ w_in[l]
        (r_q, r_k, r_v, r_g, n_q, n_kc, n_vc, n_ks, n_vs, n_kw, n_vw, n_gate) = jnp.split(proj, split_points, axis=-1)
        r_q = _rope(r_q.reshape(B, S, RET_HEADS, RET_DK), pos)
        r_k = _rope(r_k.reshape(B, S, RET_HEADS, RET_DK), pos)
        ret_out = _retention(r_q, r_k, r_v.reshape(B, S, RET_HEADS, RET_DV), r_g.reshape(B, S, RET_HEADS, RET_DV))
        kvshape = (B, S, NSA_KV_GROUPS, NSA_DH)
        nsa_out = _nsa(_rope(n_q.reshape(B, S, NSA_HEADS, NSA_DH), pos),
                       _rope(n_kc.reshape(kvshape), pos), n_vc.reshape(kvshape),
                       _rope(n_ks.reshape(kvshape), pos), n_vs.reshape(kvshape),
                       _rope(n_kw.reshape(kvshape), pos), n_vw.reshape(kvshape),
                       n_gate, pe_cmp_k[l], pe_cmp_v[l], w_cmp_k1[l], b_cmp_k1[l], w_cmp_k2[l],
                       w_cmp_v1[l], b_cmp_v1[l], w_cmp_v2[l])
        mix = jnp.concatenate([ret_out, nsa_out], axis=-1) @ w_out[l]
        x = x + ga1[:, None, :] * mix
        h = _modulate(_rms_norm(x, g_norm_ffn[l]), sh2, sc2)
        x = x + ga2[:, None, :] * _peer(h, w_peer_q[l], peer_subkeys[l], peer_down[l], peer_up[l])
    return _rms_norm(x, g_norm_final)


def setup_inputs(seed=0):
    out = dict(first_inputs(seed))
    for name, value in second_inputs(seed + 1).items():
        if name != "x":
            out[name + "_2"] = value
    return out


def reference(
    x, c, ctx, c_ctx, w_mod, b_mod, norm_g, ffn_w_in, ffn_w_out, w_in, conv_w, pool_w,
    pool_scale, rpb, w_out, final_g, c_2, w_ada_2, b_ada_2, g_norm_mix_2, w_in_2, pe_cmp_k_2,
    pe_cmp_v_2, w_cmp_k1_2, b_cmp_k1_2, w_cmp_k2_2, w_cmp_v1_2, b_cmp_v1_2, w_cmp_v2_2, w_out_2,
    g_norm_ffn_2, w_peer_q_2, peer_subkeys_2, peer_down_2, peer_up_2, g_norm_final_2,
):
    x = first_block(
        x, c, ctx, c_ctx, w_mod, b_mod, norm_g, ffn_w_in, ffn_w_out, w_in, conv_w, pool_w,
        pool_scale, rpb, w_out, final_g,
    )
    return second_block(
        x, c_2, w_ada_2, b_ada_2, g_norm_mix_2, w_in_2, pe_cmp_k_2, pe_cmp_v_2, w_cmp_k1_2,
        b_cmp_k1_2, w_cmp_k2_2, w_cmp_v1_2, b_cmp_v1_2, w_cmp_v2_2, w_out_2, g_norm_ffn_2,
        w_peer_q_2, peer_subkeys_2, peer_down_2, peer_up_2, g_norm_final_2,
    )


_drawn_inputs = setup_inputs


def setup_inputs(seed=0):
    import zlib

    import numpy as np

    out = dict(_drawn_inputs(seed))
    spreads = {}
    factors = {'b_mod': 3.187,
     'norm_g': 4.059,
     'rpb': 8.0,
     'b_ada_2': 3.094,
     'g_norm_mix_2': 7.786,
     'pe_cmp_k_2': 8.0,
     'pe_cmp_v_2': 7.004,
     'w_cmp_k1_2': 3.443,
     'b_cmp_k1_2': 8.0,
     'w_cmp_k2_2': 3.182,
     'b_cmp_v1_2': 41.377,
     'g_norm_ffn_2': 6.626,
     'g_norm_final_2': 7.736}
    for name, (base, spread) in spreads.items():
        noise = np.random.default_rng([zlib.crc32(name.encode()), seed]).standard_normal(out[name].shape)
        drawn = base * np.exp(spread * noise) if base else spread * noise
        out[name] = __import__('jax').numpy.asarray(drawn.astype(out[name].dtype))
    for name, factor in factors.items():
        out[name] = (out[name] * factor).astype(out[name].dtype)
    return out
```

```python
from contextlib import ExitStack

import numpy as np

import concourse.bass as bass
from concourse import mybir

F32 = mybir.dt.float32
U32 = mybir.dt.uint32
ALU = mybir.AluOpType
ACT = mybir.ActivationFunctionType
AX = mybir.AxisListType.X

P = 128
D = 1024
KT = D // P
S = 256
T2 = 2 * S
LAYERS = 2
D_FF = 2816
FT = D_FF // P
N_MOD = 9
EPS = 1e-6
NEG = -1e30
TINY = float(np.finfo(np.float32).tiny)
NS = 4
UNIT = 2048
FFN_OUT_UNIT = FT * P

CH_B, CH_C, CH_POOL, CH_Q, CH_K = 2, 4, 6, 8, 12
NA_H, DH = 8, 64
GRID = 64
BIAS_ROWS = 6
R_Q, R_K, N_Q, N_KC, N_KS, N_KW, N_VC, R_G = 0, 4, 8, 12, 13, 14, 15, 16
N_PROJ = 20
ROPE_WIDE, ROPE_ALL = 8, 15
RET_H = 4
NSA_H, NSA_G = 8, 2
CMP_LEN, CMP_STRIDE = 32, 16
NCB = (S - CMP_LEN) // CMP_STRIDE + 1
PH, TOPK, NK = 8, 16, 128
SLOTS = PH * TOPK

COLS = {}


def _columns():
    at = 0
    for name, n in [("cc", KT * 2), ("c2", KT), ("b_mod", LAYERS * N_MOD * KT), ("norm_g", LAYERS * 3 * KT),
                    ("final_g", KT), ("conv_w", LAYERS * 3 * 2), ("pool_scale", LAYERS * 2),
                    ("b_ada", 6 * KT), ("g_mix", KT), ("g_ffn", KT), ("g_final", KT),
                    ("b_cmp_k", 2), ("b_cmp_v", 2), ("pe_k", CMP_LEN // 2), ("pe_v", CMP_LEN // 2)]:
        COLS[name] = (at, n)
        at += n
    return at


N_COLS = _columns()
TAB = {}


def _tables():
    at = 0
    for name, n in [("cos128", S), ("sin128", S), ("cos64", S), ("sin64", S), ("perm128", P), ("perm64", P),
                    ("decay", RET_H * S), ("causal", S), ("cmp_add", 2 * 16), ("cmp_mask", 2 * 16)]:
        TAB[name] = (at, n)
        at += n
    return at


N_TAB = _tables()


class Signal:

    def __init__(self, ctx, nc, name):
        self.sem = ctx.enter_context(nc.semaphore(name))
        self.base = 0

    def at(self, n):
        return n + self.base

    def passed(self, n):
        self.base += n


class Stream:

    def __init__(self, ring, loaded, used, segments):
        self.ring, self.loaded, self.used, self.segments = ring, loaded, used, segments
        self.total = sum(n for _, n, _ in segments)
        self.g0 = 0

    def slot(self, j):
        return self.ring[:, (self.g0 + j) % NS, :]

    def wait_loaded(self, eng, c, j):
        g = self.g0 + j
        eng.wait_ge(self.loaded[g % NS], 16 * (c + (g // NS + 1)))

    def used_at(self, k):
        return k + (self.g0 + 1)

    def load(self, eng, lo, hi):
        hi = min(hi, self.total)
        first = 0
        for src, n, width in self.segments:
            a, b = max(lo, first), min(hi, first + n)
            if a < b:
                cycles = (b - a) // NS if a >= NS and (b - a) // NS >= 3 else 0
                if cycles:
                    with eng.Fori(0, cycles) as i:
                        for j in range(NS):
                            eng.wait_ge(self.used, NS * i + (a + j - NS + 1))
                            eng.dma_start(self.ring[:, (a + j) % NS, 0:width], src[NS * i + (a + j - first)])\
                               .then_inc(self.loaded[(a + j) % NS], 16)
                for g in range(a + NS * cycles, b):
                    if g >= NS:
                        eng.wait_ge(self.used, g - NS + 1)
                    eng.dma_start(self.ring[:, g % NS, 0:width], src[g - first])\
                       .then_inc(self.loaded[g % NS], 16)
            first += n

    def load_ahead(self, eng, n):
        self.load(eng, 0 if self.g0 == 0 else self.g0 + NS, self.g0 + n + NS)


def over_units(eng, n, body):
    for j in range(min(NS, n)):
        body(0, j)
    whole = n // NS
    if whole > 1:
        with eng.Fori(1, whole) as c:
            for j in range(NS):
                body(c, j)
    if whole:
        for j in range(n - whole * NS):
            body(whole, j)


def static(c):
    return isinstance(c, int)


class Chip:

    def __init__(self, ctx, nc, dram):
        def sb(name, shape, dt=F32):
            return ctx.enter_context(nc.sbuf_tensor(name, shape, dt))

        def sig(name):
            return Signal(ctx, nc, name)

        self.nc, self.dram = nc, dram
        self.bank = [ctx.enter_context(nc.psum_tensor(f"bank{b}", [P, 512], F32)) for b in range(8)]
        self.ring = sb("ring", [P, NS, FFN_OUT_UNIT])
        self.arena = sb("arena", [P, 32768])
        self.x2 = sb("x2", [P, KT, S])
        self.h2 = sb("h2", [P, KT, S])
        self.cols = sb("cols", [P, N_COLS])
        self.silu_c = sb("silu_c", [P, KT, 2])
        self.silu_c2 = sb("silu_c2", [P, KT])
        self.mod = sb("mod", [P, N_MOD * KT, 2])
        self.gain = sb("gain", [P, 3, KT, 2])
        self.half_gate = sb("half_gate", [P, 2, KT, 2])
        self.mod2 = sb("mod2", [P, 6 * KT])
        self.gain2 = sb("gain2", [P, 2, KT])
        self.ident = sb("ident", [P, P])
        self.ones = sb("ones", [P, P])

        self.eps = sb("eps", [P, 1])

        self.unit_used = ctx.enter_context(nc.semaphore("unit_used"))
        self.unit_loaded = [ctx.enter_context(nc.semaphore(f"unit_loaded{s}")) for s in range(NS)]
        self.squared, self.summed, self.rooted = sig("squared"), sig("summed"), sig("rooted")
        self.scaled, self.h_ready = sig("scaled"), sig("h_ready")
        self.dve_step, self.act_step, self.pool_step = sig("dve_step"), sig("act_step"), sig("pool_step")
        self.table = sig("table")
        self.product, self.copied, self.added = sig("product"), sig("copied"), sig("added")
        self.silu_done, self.gated = sig("silu_done"), sig("gated")
        self.pool_w = sb("pool_w", [P, 2, P])
        self.pool_inv = sb("pool_inv", [P, 2, S])
        self.nmax, self.rsum = sb("nmax", [P, 2]), sb("rsum", [P, 2])
        self.gates = sb("gates", [P, 2, 24])
        self.nmax4, self.rsum4 = sb("nmax4", [P, 2, 2]), sb("rsum4", [P, 2, 2])
        self.iota = sb("iota", [P, P])
        self.slot_t = sb("slot_t", [P, 3, S])
        self.work = sb("work", [P, 4, S])
        self.gelu_done = sig("gelu_done")
        self.scored, self.scores_read, self.maxed = sig("scored"), sig("scores_read"), sig("maxed")
        self.exped, self.probs, self.turned = sig("exped"), sig("probs"), sig("turned")
        self.moved, self.mixed = sig("moved"), sig("mixed")

    def col(self, name, at=0, n=None):
        lo, size = COLS[name]
        return self.cols[:, lo + at:lo + (size if n is None else at + n)]

    def part(self, at, *shape):
        n = int(np.prod(shape))
        assert at + n <= 32768
        flat = self.arena[:, at:at + n]
        if len(shape) == 1:
            return flat
        if len(shape) == 2:
            return flat.rearrange("p (a b) -> p a b", b=shape[1])
        return flat.rearrange("p (a b c) -> p a b c", b=shape[1], c=shape[2])


A_X, A_H = 0, 4096
A_G = 8192
A_U, A_V, A_Y, A_BIAS = 8192, 16384, 18432, 22528
A_SC, A_PT, A_POOL = 25600, 26624, 28672
A_RSTD = 31232


def in_order(eng, signal, instruction):
    signal.passed(1)
    instruction.then_inc(signal.sem, 1)
    eng.wait_ge(signal.sem, signal.base)


class Norm:
    def __init__(self, chip, x, h, root, rstd, gain, shift, groups, width):
        self.chip, self.x, self.h, self.root, self.rstd = chip, x, h, root, rstd
        self.gain, self.shift, self.groups, self.t = gain, shift, groups, width

    def scalar(self, act):
        c, nc, t = self.chip, self.chip.nc, self.t
        for kt in range(KT):
            nc.scalar.activation(self.h[:, kt, 0:t], self.x[:, kt, 0:t], ACT.Square).then_inc(c.squared.sem, 1)
        act.wait_ge(c.summed.sem, c.summed.at(1))
        nc.scalar.activation(self.root[:, 0:t], c.bank[7][:, 0:t], ACT.Sqrt, bias=self.chip.eps[:, 0:1], scale=1.0 / D)\
            .then_inc(c.rooted.sem, 1)
        for kt in range(KT):
            act.wait_ge(c.scaled.sem, c.scaled.at(kt + 1))
            for g, (lo, hi) in enumerate(self.groups):
                shift = 0.0 if self.shift is None else self.shift(kt, g)
                last = nc.scalar.activation(self.h[:, kt, lo:hi], self.h[:, kt, lo:hi], ACT.Identity,
                                            bias=shift, scale=self.gain(kt, g))
            last.then_inc(c.h_ready.sem, 1)

    def tensor(self, pe):
        c, nc, t = self.chip, self.chip.nc, self.t
        for kt in range(KT):
            pe.wait_ge(c.squared.sem, c.squared.at(kt + 1))
            last = nc.tensor.matmul(c.bank[7][:, 0:t], c.ones[:, :], self.h[:, kt, 0:t],
                                    start=(kt == 0), stop=(kt == KT - 1))
        last.then_inc(c.summed.sem, 1)

    def vector(self, dve):
        c, nc, t = self.chip, self.chip.nc, self.t
        dve.wait_ge(c.rooted.sem, c.rooted.at(1))
        in_order(dve, c.dve_step, nc.vector.reciprocal(self.rstd[:, 0:t], self.root[:, 0:t]))
        for kt in range(KT):
            nc.vector.tensor_tensor(self.h[:, kt, 0:t], self.x[:, kt, 0:t], self.rstd[:, 0:t], ALU.mult)\
                .then_inc(c.scaled.sem, 1)

    def end(self):
        c = self.chip
        c.squared.passed(KT)
        c.summed.passed(1)
        c.rooted.passed(1)
        c.scaled.passed(KT)
        c.h_ready.passed(KT)


def stage_setup(chip):
    nc, d = chip.nc, chip.dram
    x = chip.part(A_X, KT, T2)
    with nc.Block() as block:
        @block.sync
        def _(sp):
            sp.dma_start(chip.cols[:, :], d["cols"]).then_inc(chip.table.sem, 16)
            sp.dma_start(x, d["x"]).then_inc(chip.table.sem, 16)
            sp.wait_ge(chip.table.sem, 32)

        @block.gpsimd
        def _(pool):
            nc.gpsimd.memset(chip.ones[:, :], 1.0)
            nc.gpsimd.memset(chip.eps[:, :], EPS)
            in_order(pool, chip.pool_step, nc.gpsimd.memset(chip.ident[:, :], 0.0))
            in_order(pool, chip.pool_step, nc.gpsimd.affine_select(
                out=chip.ident[:, :], in_=chip.ident[:, :], compare_op=ALU.not_equal, fill=1.0, base=0,
                pattern=[[-1, P]], channel_multiplier=1))

        @block.scalar
        def _(act):
            act.wait_ge(chip.table.sem, 32)
            nc.scalar.activation(chip.silu_c[:, :, :].rearrange("p a b -> p (a b)"), chip.col("cc"), ACT.Silu)\
                .then_inc(chip.act_step.sem, 1)
            nc.scalar.activation(chip.silu_c2[:, :], chip.col("c2"), ACT.Silu).then_inc(chip.act_step.sem, 1)
            act.wait_ge(chip.act_step.sem, 2)
    chip.table.passed(32)
    chip.act_step.passed(2)


def stage_mod(chip, stream, layer):
    nc = chip.nc
    first = layer is not None
    chunks, width = (N_MOD * KT, 2) if first else (6 * KT, 1)
    units = chunks // 2
    rhs = (lambda kt: chip.silu_c[:, kt, :]) if first else (lambda kt: chip.silu_c2[:, kt:kt + 1])
    out = chip.bank[0][:, 0:chunks * width].rearrange("p (n w) -> p n w", w=width)
    with nc.Block() as block:
        @block.sync
        def _(sp):
            stream.load_ahead(sp, units)

        @block.tensor
        def _(pe):
            def unit(c, j):
                stream.wait_loaded(pe, c, j)
                w = stream.slot(j)
                for b in range(2):
                    for kt in range(KT):
                        last = nc.tensor.matmul(out[:, 2 * (NS * c + j) + b, :],
                                                w[:, kt * 256 + b * P:kt * 256 + (b + 1) * P], rhs(kt),
                                                start=(kt == 0), stop=(kt == KT - 1))
                last.then_inc(stream.used, 1)
            with pe.Fori(0, units // NS) as c:
                for j in range(NS):
                    unit(c, j)

        @block.vector
        def _(dve):
            dve.wait_ge(stream.used, stream.used_at(units - 1))
            if first:
                b = chip.col("b_mod", layer * N_MOD * KT, N_MOD * KT).unsqueeze(2).to_broadcast([P, N_MOD * KT, 2])
                in_order(dve, chip.dve_step, nc.vector.tensor_tensor(chip.mod[:, :, :], out, b, ALU.add))
                for i in range(3):
                    g = chip.col("norm_g", (layer * 3 + i) * KT, KT).unsqueeze(2).to_broadcast([P, KT, 2])
                    nc.vector.scalar_tensor_tensor(chip.gain[:, i, :, :], chip.mod[:, (3 * i + 1) * KT:(3 * i + 2) * KT, :],
                                                   1.0, g, ALU.add, ALU.mult)
                for i in range(2):
                    last = nc.vector.tensor_scalar(chip.half_gate[:, i, :, :],
                                                   chip.mod[:, (6 * i + 2) * KT:(6 * i + 3) * KT, :], 0.5, None, ALU.mult)
                in_order(dve, chip.dve_step, last)
            else:
                in_order(dve, chip.dve_step, nc.vector.tensor_tensor(chip.mod2[:, :], out[:, :, 0], chip.col("b_ada"), ALU.add))
                for i, g in enumerate(("g_mix", "g_ffn")):
                    in_order(dve, chip.dve_step, nc.vector.scalar_tensor_tensor(
                        chip.gain2[:, i, :], chip.mod2[:, (3 * i + 1) * KT:(3 * i + 2) * KT], 1.0, chip.col(g),
                        ALU.add, ALU.mult))
    stream.g0 += units


def norm1(chip, i, width):
    groups = [(0, S), (S, T2)][:width // S]
    return Norm(chip, chip.part(A_X, KT, T2), chip.part(A_H, KT, T2), chip.part(A_RSTD + 512, 512), chip.part(A_RSTD, 512),
                lambda kt, g: chip.gain[:, i, kt, g:g + 1], lambda kt, g: chip.mod[:, 3 * i * KT + kt, g:g + 1],
                groups, width)


def stage_ffn(chip, stream, which, width):
    nc = chip.nc
    norm = norm1(chip, 2 * which, width)
    x, h, hid = chip.part(A_X, KT, T2), chip.part(A_H, KT, T2), chip.part(A_G, FT, T2)
    t = width
    groups = norm.groups
    with nc.Block() as block:
        @block.sync
        def _(sp):
            stream.load_ahead(sp, FT + KT)

        @block.tensor
        def _(pe):
            norm.tensor(pe)
            pe.wait_ge(chip.h_ready.sem, chip.h_ready.at(KT))

            def up(c, j):
                stream.wait_loaded(pe, c, j)
                if not (static(c) and NS * c + j < 2):
                    pe.wait_ge(chip.gated.sem, chip.gated.at(NS * c + (j - 1)))
                w = stream.slot(j)
                for half in range(2):
                    for kt in range(KT):
                        last = nc.tensor.matmul(chip.bank[2 * (j % 2) + half][:, 0:t],
                                                w[:, kt * 256 + half * P:kt * 256 + (half + 1) * P], h[:, kt, 0:t],
                                                start=(kt == 0), stop=(kt == KT - 1))
                last.then_inc(stream.used, 1)
            over_units(pe, FT, up)
            pe.wait_ge(chip.gated.sem, chip.gated.at(FT))

            for n in range(KT):
                j = FT + n
                stream.wait_loaded(pe, 0, j)
                if n >= 2:
                    pe.wait_ge(chip.added.sem, chip.added.at(n - 1))
                w = stream.slot(j)
                for kt in range(FT):
                    last = nc.tensor.matmul(chip.bank[4 + n % 2][:, 0:t], w[:, kt * P:(kt + 1) * P], hid[:, kt, 0:t],
                                            start=(kt == 0), stop=(kt == FT - 1))
                last.then_inc(stream.used, 1)

        @block.scalar
        def _(act):
            norm.scalar(act)

            def silu(c, j):
                act.wait_ge(stream.used, stream.used_at(NS * c + j))
                nc.scalar.activation(hid[:, NS * c + j, 0:t], chip.bank[2 * (j % 2)][:, 0:t], ACT.Silu)\
                    .then_inc(chip.silu_done.sem, 1)
            over_units(act, FT, silu)

        @block.vector
        def _(dve):
            norm.vector(dve)

            def gate(c, j):
                dve.wait_ge(chip.silu_done.sem, chip.silu_done.at(NS * c + (j + 1)))
                nc.vector.tensor_tensor(hid[:, NS * c + j, 0:t], hid[:, NS * c + j, 0:t],
                                        chip.bank[2 * (j % 2) + 1][:, 0:t], ALU.mult).then_inc(chip.gated.sem, 1)
            over_units(dve, FT, gate)
            for n in range(KT):
                dve.wait_ge(stream.used, stream.used_at(FT + n))
                for g, (lo, hi) in enumerate(groups):
                    last = nc.vector.scalar_tensor_tensor(x[:, n, lo:hi], chip.bank[4 + n % 2][:, lo:hi],
                                                          chip.half_gate[:, which, n, g:g + 1], x[:, n, lo:hi],
                                                          ALU.mult, ALU.add)
                last.then_inc(chip.added.sem, 1)
    norm.end()
    chip.silu_done.passed(FT)
    chip.gated.passed(FT)
    chip.added.passed(KT)
    stream.g0 += FT + KT


def stage_mix_in(chip, stream, layer, last):
    nc, d = chip.nc, chip.dram
    norm = norm1(chip, 1, T2)
    h, u, v = chip.part(A_H, KT, T2), chip.part(A_U, 16, T2), chip.part(A_V, 4, 512)
    bias = chip.part(A_BIAS, NA_H * BIAS_ROWS * GRID)
    width = [S if last and n < CH_K else T2 for n in range(16)]
    with nc.Block() as block:
        @block.sync
        def _(sp):
            sp.dma_start(bias, d["rel_bias"][layer]).then_inc(chip.table.sem, 16)
            sp.dma_start(chip.pool_w[:, :, :], d["pool_w"][layer]).then_inc(chip.table.sem, 16)
            sp.dma_start(chip.pool_inv[:, :, :], d["pool_inv"]).then_inc(chip.table.sem, 16)
            stream.load_ahead(sp, 10)

        @block.gpsimd
        def _(pool):
            pool.wait_ge(chip.table.sem, chip.table.at(48))
            for half in range(2):
                b = bias[half * GRID:(half + 1) * GRID, :].rearrange("p (r k) -> p r k", k=GRID)
                lo, hi = b[:, :, 0:GRID - 16], b[:, :, 16:GRID]
                in_order(pool, chip.pool_step, nc.gpsimd.affine_select(
                    out=lo, in_=lo, compare_op=ALU.is_ge, fill=NEG, base=8,
                    pattern=[[0, NA_H * BIAS_ROWS], [1, GRID - 16]], channel_multiplier=-1))
                in_order(pool, chip.pool_step, nc.gpsimd.affine_select(
                    out=hi, in_=hi, compare_op=ALU.is_ge, fill=NEG, base=7 - 16,
                    pattern=[[0, NA_H * BIAS_ROWS], [-1, GRID - 16]], channel_multiplier=1))

        @block.tensor
        def _(pe):
            norm.tensor(pe)
            pe.wait_ge(chip.h_ready.sem, chip.h_ready.at(KT))
            for k in range(8):
                stream.wait_loaded(pe, 0, k)
                w = stream.slot(k)
                for b in range(2):
                    n = 2 * k + b
                    if n >= 4:
                        pe.wait_ge(chip.copied.sem, chip.copied.at(n - 3))
                    for kt in range(KT):
                        mm = nc.tensor.matmul(chip.bank[n % 4][:, 0:width[n]],
                                              w[:, kt * 256 + b * P:kt * 256 + (b + 1) * P], h[:, kt, 0:width[n]],
                                              start=(kt == 0), stop=(kt == KT - 1))
                    mm.then_inc(chip.product.sem, 1)
                pe.wait_ge(chip.product.sem, chip.product.at(2 * k + 2))
                pe.sem_inc(stream.used, 1)
            for k in range(2):
                stream.wait_loaded(pe, 0, 8 + k)
                w = stream.slot(8 + k)
                for tt in range(4):
                    for kt in range(KT):
                        mm = nc.tensor.matmul(chip.bank[4 + tt][:, k * 256:(k + 1) * 256],
                                              h[:, kt, tt * P:(tt + 1) * P], w[:, kt * 256:(kt + 1) * 256],
                                              start=(kt == 0), stop=(kt == KT - 1))
                mm.then_inc(stream.used, 1)

        @block.scalar
        def _(act):
            norm.scalar(act)
            for n in range(16):
                act.wait_ge(chip.product.sem, chip.product.at(n + 1))
                nc.scalar.activation(u[:, n, 0:width[n]], chip.bank[n % 4][:, 0:width[n]], ACT.Copy)\
                    .then_inc(chip.copied.sem, 1)
            act.wait_ge(stream.used, stream.used_at(9))
            for tt in range(4):
                nc.scalar.activation(v[:, tt, :], chip.bank[4 + tt][:, :], ACT.Copy)

        @block.vector
        def _(dve):
            norm.vector(dve)
    norm.end()
    chip.table.passed(48)
    chip.product.passed(16)
    chip.copied.passed(16)
    stream.g0 += 10


def stage_mix(chip, stream, layer, last):
    nc = chip.nc
    u, v, y = chip.part(A_U, 16, T2), chip.part(A_V, 4, 512), chip.part(A_Y, KT, T2)
    bias = chip.part(A_BIAS, NA_H, BIAS_ROWS * GRID)
    sc, pt = chip.part(A_SC, 2, 512), chip.part(A_PT, 2, 4, S)
    ng = 1 if last else 2
    t = ng * S
    items = [(g, h, qt) for g in range(ng) for h in range(NA_H) for qt in range(2)]
    keys = lambda g: (0, T2) if g == 0 else (S, T2)

    with nc.Block() as block:
        @block.sync
        def _(sp):
            pass

        @block.gpsimd
        def _(pool):
            eng = nc.gpsimd
            step = lambda ins: in_order(pool, chip.pool_step, ins)
            z = chip.part(A_POOL, ng, S + 2)
            acc, tmp = chip.part(A_POOL + 544, ng, S), chip.part(A_POOL + 1088, ng, S)
            step(eng.memset(z, 0.0))
            for b in range(2):
                uu = lambda n: u[:, n + b, 0:t].rearrange("p (g s) -> p g s", s=S)
                w = lambda k: chip.col("conv_w", (layer * 3 + k) * 2 + b, 1)
                step(eng.tensor_tensor(z[:, :, 1:S + 1], uu(CH_C), uu(0), ALU.mult))
                step(eng.tensor_scalar(acc, z[:, :, 0:S], w(0), None, ALU.mult))
                for k in (1, 2):
                    step(eng.tensor_scalar(tmp, z[:, :, k:k + S], w(k), None, ALU.mult))
                    step(eng.tensor_tensor(acc, acc, tmp, ALU.add))
                step(eng.tensor_tensor(y[:, b, 0:t].rearrange("p (g s) -> p g s", s=S), acc, uu(CH_B), ALU.mult))
            wide = S + 16
            a, c = chip.part(A_POOL, ng, wide), chip.part(A_POOL + 544, ng, wide)
            for b in range(2):
                vv = u[:, CH_POOL + b, 0:t].rearrange("p (g s) -> p g s", s=S)
                out = y[:, 2 + b, 0:t].rearrange("p (g s) -> p g s", s=S)
                step(eng.memset(a, 0.0))
                step(eng.tensor_copy(a[:, :, 8:8 + S], vv))
                src, dst = a, c
                for n in range(2 + 2 * b):
                    gap, at = 1 << n, (2 << n) - 1
                    step(eng.tensor_tensor(dst[:, :, at:wide], src[:, :, at:wide], src[:, :, at - gap:wide - gap], ALU.add))
                    src, dst = dst, src
                    if n >= 2 * b:
                        half, lo = n - 2 * b, 8 + gap - 1
                        q = slice(64 * half, 64 * half + 64)
                        inv = chip.pool_inv[q, b, :].unsqueeze(1).to_broadcast([64, ng, S])
                        step(eng.tensor_tensor(out[q, :, :], src[q, :, lo:lo + S], inv, ALU.mult))
                step(eng.tensor_tensor(out, out, vv, ALU.subtract))
            eng.sem_inc(chip.mixed.sem, 1)

        @block.tensor
        def _(pe):
            def scores(w):
                g, h, qt = items[w]
                lo, hi = keys(g)
                po, q0 = 64 * (h % 2), g * S + qt * P
                if w >= 2:
                    pe.wait_ge(chip.scores_read.sem, chip.scores_read.at(w - 1))
                nc.tensor.matmul(chip.bank[w % 2][:, 0:hi - lo], u[po:po + 64, CH_Q + h // 2, q0:q0 + P],
                                 u[po:po + 64, CH_K + h // 2, lo:hi], start=True, stop=True)\
                    .then_inc(chip.scored.sem, 1)

            def transposes(w):
                g, h, qt = items[w]
                pe.wait_ge(chip.probs.sem, chip.probs.at(w + 1))
                if w >= 2:
                    pe.wait_ge(chip.copied.sem, chip.copied.at(w - 1))
                for kt in range((keys(g)[1] - keys(g)[0]) // P):
                    mm = nc.tensor.transpose(chip.bank[2 + w % 2][:, kt * P:(kt + 1) * P],
                                             sc[:, w % 2, kt * P:(kt + 1) * P], chip.ident[:, :])
                mm.then_inc(chip.turned.sem, 1)

            def values(n):
                g, h, _ = items[2 * n]
                po = 64 * (h % 2)
                pe.wait_ge(chip.copied.sem, chip.copied.at(2 * n + 2))
                if n >= 2:
                    pe.wait_ge(chip.moved.sem, chip.moved.at(n - 1))
                nkt = (keys(g)[1] - keys(g)[0]) // P
                for kt in range(nkt):
                    mm = nc.tensor.matmul(chip.bank[4 + n % 2][po:po + 64, 0:S],
                                          v[:, kt + 4 - nkt, h * DH:(h + 1) * DH], pt[:, n % 2, kt, :],
                                          start=(kt == 0), stop=(kt == nkt - 1))
                mm.then_inc(chip.product.sem, 1)

            scores(0)
            scores(1)
            for w in range(len(items)):
                transposes(w)
                if w + 2 < len(items):
                    scores(w + 2)
                if w >= 2 and w % 2 == 0:
                    values(w // 2 - 1)
            values(len(items) // 2 - 1)
            pe.wait_ge(chip.mixed.sem, chip.mixed.at(1))
            for b in range(2):
                mm = nc.tensor.matmul(chip.bank[6 + b][:, 0:t], chip.pool_w[:, b, :], y[:, 2 + b, 0:t],
                                      start=True, stop=True)
            mm.then_inc(chip.product.sem, 1)

        @block.scalar
        def _(act):
            def exps(w):
                g, h, qt = items[w]
                n = keys(g)[1] - keys(g)[0]
                act.wait_ge(chip.maxed.sem, chip.maxed.at(w + 1))
                nc.scalar.activation(sc[:, w % 2, 0:n], sc[:, w % 2, 0:n], ACT.Exp, bias=chip.nmax[:, w % 2:w % 2 + 1],
                                     accum_out=chip.rsum[:, w % 2:w % 2 + 1]).then_inc(chip.exped.sem, 1)

            def copies(w):
                g, h, qt = items[w]
                nkt = (keys(g)[1] - keys(g)[0]) // P
                n = w // 2
                act.wait_ge(chip.turned.sem, chip.turned.at(w + 1))
                if n >= 2:
                    act.wait_ge(chip.product.sem, chip.product.at(n - 1))
                nc.scalar.activation(pt[:, n % 2, 0:nkt, qt * P:(qt + 1) * P],
                                     chip.bank[2 + w % 2][:, 0:nkt * P].rearrange("p (k q) -> p k q", q=P), ACT.Copy)\
                    .then_inc(chip.copied.sem, 1)

            def move(n):
                g, h, _ = items[2 * n]
                po = 64 * (h % 2)
                act.wait_ge(chip.product.sem, chip.product.at(n + 1))
                nc.scalar.activation(y[po:po + 64, 4 + h // 2, g * S:(g + 1) * S], chip.bank[4 + n % 2][po:po + 64, 0:S],
                                     ACT.Copy).then_inc(chip.moved.sem, 1)

            exps(0)
            for w in range(len(items)):
                if w + 1 < len(items):
                    exps(w + 1)
                copies(w)
                if w >= 3 and w % 2 == 1:
                    move(w // 2 - 1)
            move(len(items) // 2 - 1)
            act.wait_ge(chip.product.sem, chip.product.at(len(items) // 2 + 1))
            for b in range(2):
                nc.scalar.activation(y[:, 2 + b, 0:t], chip.bank[6 + b][:, 0:t], ACT.Copy,
                                     scale=chip.col("pool_scale", layer * 2 + b, 1))

        @block.vector
        def _(dve):
            def scale(w):
                g, h, qt = items[w]
                n = keys(g)[1] - keys(g)[0]
                s, bank = sc[:, w % 2, :], chip.bank[w % 2]
                dve.wait_ge(chip.scored.sem, chip.scored.at(w + 1))
                if w >= 2:
                    dve.wait_ge(chip.turned.sem, chip.turned.at(w - 1))
                if g == 0:
                    r0 = (2 - 2 * qt) * GRID
                    nc.vector.scalar_tensor_tensor(s[:, 0:S], bank[:, 0:S], 0.125, bias[:, h, r0:r0 + S], ALU.mult, ALU.add)
                    nc.vector.tensor_scalar(s[:, S:T2], bank[:, S:T2], 0.125, None, ALU.mult)\
                        .then_inc(chip.scores_read.sem, 1)
                else:
                    nc.vector.tensor_scalar(s[:, 0:n], bank[:, 0:n], 0.125, None, ALU.mult)\
                        .then_inc(chip.scores_read.sem, 1)
                dve.wait_ge(chip.scores_read.sem, chip.scores_read.at(w + 1))
                nc.vector.tensor_reduce(chip.nmax[:, w % 2:w % 2 + 1], s[:, 0:n], AX.X, ALU.max, negate=True)\
                    .then_inc(chip.maxed.sem, 1)

            def normalise(w):
                g, h, qt = items[w]
                n = keys(g)[1] - keys(g)[0]
                dve.wait_ge(chip.exped.sem, chip.exped.at(w + 1))
                r = chip.rsum[:, w % 2:w % 2 + 1]
                in_order(dve, chip.dve_step, nc.vector.reciprocal(r, r))
                nc.vector.tensor_scalar(sc[:, w % 2, 0:n], sc[:, w % 2, 0:n], r, None, ALU.mult).then_inc(chip.probs.sem, 1)

            scale(0)
            for w in range(len(items)):
                if w + 1 < len(items):
                    scale(w + 1)
                normalise(w)
    n = len(items)
    for sig in (chip.scored, chip.scores_read, chip.maxed, chip.exped, chip.probs, chip.turned, chip.copied):
        sig.passed(n)
    chip.product.passed(n // 2 + 1)
    chip.moved.passed(n // 2)
    chip.mixed.passed(1)


def stage_add_product(chip, stream, x, y, gate, groups):
    nc, t = chip.nc, groups[-1][1]
    with nc.Block() as block:
        @block.sync
        def _(sp):
            stream.load_ahead(sp, 4)

        @block.tensor
        def _(pe):
            for k in range(4):
                stream.wait_loaded(pe, 0, k)
                w = stream.slot(k)
                for b in range(2):
                    n = 2 * k + b
                    if n >= 4:
                        pe.wait_ge(chip.added.sem, chip.added.at(n - 3))
                    for kt in range(KT):
                        mm = nc.tensor.matmul(chip.bank[n % 4][:, 0:t], w[:, kt * 256 + b * P:kt * 256 + (b + 1) * P],
                                              y[:, kt, 0:t], start=(kt == 0), stop=(kt == KT - 1))
                    mm.then_inc(chip.product.sem, 1)
                pe.wait_ge(chip.product.sem, chip.product.at(2 * k + 2))
                pe.sem_inc(stream.used, 1)

        @block.vector
        def _(dve):
            for n in range(KT):
                dve.wait_ge(chip.product.sem, chip.product.at(n + 1))
                for g, (lo, hi) in enumerate(groups):
                    last = nc.vector.scalar_tensor_tensor(x[:, n, lo:hi], chip.bank[n % 4][:, lo:hi], gate(n, g),
                                                          x[:, n, lo:hi], ALU.mult, ALU.add)
                last.then_inc(chip.added.sem, 1)
    chip.product.passed(KT)
    chip.added.passed(KT)
    stream.g0 += 4


B_U, B_TAB = 0, 5120
B_RV = B_TAB + N_TAB
B_VS = B_RV + 1024
B_Y = B_VS + 512
B_SR = B_Y + 2048
B_RY, B_T1, B_T2 = B_SR + 768, B_SR + 768 + 1024, B_SR + 768 + 2048
B_W1 = B_T2 + 1024
B_W2 = B_W1 + 8192
B_K2 = B_W2 + 256
B_BLK = B_K2 + 1024
B_HID = B_BLK + 960
B_SC, B_PTS, B_PTC = B_HID + 128, B_HID + 128 + 1024, B_HID + 128 + 1024 + 1536
B_C = B_PTC + 2048
E_Q, E_SC, E_SC2, E_V, E_I, E_IF, E_TV, E_TJ = 0, 4096, 8192, 8704, 9216, 9728, 10240, 10496
E_J, E_JF, E_EQ, E_N, E_W, E_CAND = 10752, 11264, 11776, 13824, 14592, 15104


def stage_final_norm(chip):
    norm = Norm(chip, chip.part(A_X, KT, T2), chip.x2, chip.part(A_RSTD + 512, 512), chip.part(A_RSTD, 512),
                lambda kt, g: chip.col("final_g", kt, 1), None, [(0, S)], S)
    with chip.nc.Block() as block:
        block.tensor(norm.tensor)
        block.scalar(norm.scalar)
        block.vector(norm.vector)
    norm.end()


def norm2(chip, i, at):
    return Norm(chip, chip.x2, chip.h2, chip.part(at, S), chip.part(at + S, S),
                lambda kt, g: chip.gain2[:, i, kt:kt + 1], lambda kt, g: chip.mod2[:, 3 * i * KT + kt:3 * i * KT + kt + 1],
                [(0, S)], S)


def stage_proj(chip, stream):
    nc, d = chip.nc, chip.dram
    norm = norm2(chip, 0, B_T2)
    h, u = chip.h2, chip.part(B_U, N_PROJ, S)
    rv, vs = chip.part(B_RV, 2, 512), chip.part(B_VS, 2, S)
    with nc.Block() as block:
        @block.sync
        def _(sp):
            sp.dma_start(chip.part(B_TAB, N_TAB), d["tables"]).then_inc(chip.table.sem, 16)
            for n, k in enumerate("kv"):
                sp.dma_start(chip.part(B_W1 + 4096 * n, 16, 256), d[f"cmp_{k}1"]).then_inc(chip.table.sem, 16)
                sp.dma_start(chip.part(B_W2 + 128 * n, 2, 64), d[f"cmp_{k}2"]).then_inc(chip.table.sem, 16)
            stream.load_ahead(sp, 14)
            sp.wait_ge(chip.table.sem, chip.table.at(80))

        @block.tensor
        def _(pe):
            norm.tensor(pe)
            pe.wait_ge(chip.h_ready.sem, chip.h_ready.at(KT))
            for k in range(N_PROJ // 2):
                stream.wait_loaded(pe, 0, k)
                w = stream.slot(k)
                if k >= 2:
                    pe.wait_ge(chip.copied.sem, chip.copied.at(k - 1))
                for b in range(2):
                    for kt in range(KT):
                        mm = nc.tensor.matmul(chip.bank[k % 2][:, b * S:(b + 1) * S],
                                              w[:, kt * 256 + b * P:kt * 256 + (b + 1) * P], h[:, kt, :],
                                              start=(kt == 0), stop=(kt == KT - 1))
                mm.then_inc(stream.used, 1)
            for k in range(4):
                stream.wait_loaded(pe, 0, N_PROJ // 2 + k)
                w = stream.slot(N_PROJ // 2 + k)
                lo, n = ((0, 256), (256, 256), (0, 256), (256, 24))[k]
                for tt in range(2):
                    for kt in range(KT):
                        mm = nc.tensor.matmul(chip.bank[(2 if k < 2 else 4) + tt][:, lo:lo + n],
                                              h[:, kt, tt * P:(tt + 1) * P], w[:, kt * 256:kt * 256 + n],
                                              start=(kt == 0), stop=(kt == KT - 1))
                mm.then_inc(stream.used, 1)

        @block.scalar
        def _(act):
            norm.scalar(act)
            for k in range(N_PROJ // 2):
                act.wait_ge(stream.used, stream.used_at(k))
                nc.scalar.activation(u[:, 2 * k:2 * k + 2, :].rearrange("p a b -> p (a b)"), chip.bank[k % 2][:, :], ACT.Copy)\
                    .then_inc(chip.copied.sem, 1)
            act.wait_ge(stream.used, stream.used_at(13))
            for tt in range(2):
                nc.scalar.activation(rv[:, tt, :], chip.bank[2 + tt][:, :], ACT.Copy)
                nc.scalar.activation(vs[:, tt, :], chip.bank[4 + tt][:, 0:S], ACT.Copy)
                nc.scalar.activation(chip.gates[:, tt, :], chip.bank[4 + tt][:, S:S + 24], ACT.Sigmoid)

        @block.vector
        def _(dve):
            norm.vector(dve)
    norm.end()
    chip.table.passed(80)
    chip.copied.passed(N_PROJ // 2)
    stream.g0 += 14


def table(chip, name, *shape):
    at, n = TAB[name]
    return chip.part(B_TAB + at, *(shape or (n,)))


def stage_rope(chip):
    nc, u = chip.nc, chip.part(B_U, N_PROJ, S)
    pairs = [(n, min(n + 2, ROPE_ALL)) for n in range(0, ROPE_ALL, 2)]
    with nc.Block() as block:
        @block.tensor
        def _(pe):
            for k, (lo, hi) in enumerate(pairs):
                perm = table(chip, "perm128" if lo < ROPE_WIDE else "perm64")
                mm = nc.tensor.matmul(chip.bank[k][:, 0:(hi - lo) * S], perm,
                                      u[:, lo:hi, :].rearrange("p a b -> p (a b)"), start=True, stop=True)
                mm.then_inc(chip.turned.sem, 1)

        @block.vector
        def _(dve):
            for k, (lo, hi) in enumerate(pairs):
                size = "128" if lo < ROPE_WIDE else "64"
                n = hi - lo
                cos, sin = (table(chip, x + size).unsqueeze(1).to_broadcast([P, n, S]) for x in ("cos", "sin"))
                tmp = chip.part(B_RY if k % 2 else B_T1, n, S)
                rot = chip.bank[k][:, 0:n * S].rearrange("p (a b) -> p a b", b=S)
                dve.wait_ge(chip.turned.sem, chip.turned.at(k + 1))
                nc.vector.tensor_tensor(tmp, rot, sin, ALU.mult)
                in_order(dve, chip.dve_step, nc.vector.tensor_tensor(u[:, lo:hi, :], u[:, lo:hi, :], cos, ALU.mult))
                nc.vector.tensor_tensor(u[:, lo:hi, :], u[:, lo:hi, :], tmp, ALU.add)
    chip.turned.passed(len(pairs))


def stage_retention(chip):
    nc = chip.nc
    u, rv, y = chip.part(B_U, N_PROJ, S), chip.part(B_RV, 2, 512), chip.part(B_Y, KT, S)
    sr, ry = chip.part(B_SR, 2, 384), chip.part(B_RY, RET_H * S)
    t1, t2 = chip.part(B_T1, RET_H * S), chip.part(B_T2, RET_H * S)
    decay = table(chip, "decay", RET_H, S)
    halves = [slice(0, 512), slice(512, 1024)]
    with nc.Block() as block:
        @block.tensor
        def _(pe):
            def scores(h):
                if h >= 2:
                    pe.wait_ge(chip.probs.sem, chip.probs.at(h - 1))
                q, k, b = u[:, R_Q + h, :], u[:, R_K + h, :], chip.bank[h % 2]
                nc.tensor.matmul(b[:, 0:S], k[:, 0:P], q, start=True, stop=True)
                nc.tensor.matmul(b[:, S:384], k[:, P:S], q[:, P:S], start=True, stop=True).then_inc(chip.scored.sem, 1)

            scores(0)
            for h in range(RET_H):
                if h + 1 < RET_H:
                    scores(h + 1)
                pe.wait_ge(chip.probs.sem, chip.probs.at(h + 1))
                o = chip.bank[2 + h // 2][:, (h % 2) * S:(h % 2 + 1) * S]
                nc.tensor.matmul(o, rv[:, 0, h * P:(h + 1) * P], sr[:, h % 2, 0:S], start=True, stop=False)
                nc.tensor.matmul(o[:, P:S], rv[:, 1, h * P:(h + 1) * P], sr[:, h % 2, S:384], start=False, stop=True)\
                    .then_inc(chip.product.sem, 1)
            pe.wait_ge(chip.copied.sem, chip.copied.at(2))
            for n, part in enumerate(halves):
                nc.tensor.matmul(chip.bank[4 + n][:, :], chip.ones[:, :], ry[:, part], start=True, stop=True)\
                    .then_inc(chip.summed.sem, 1)
            pe.wait_ge(chip.squared.sem, chip.squared.at(1))
            for n, part in enumerate(halves):
                nc.tensor.matmul(chip.bank[6 + n][:, :], chip.ones[:, :], t1[:, part], start=True, stop=True)\
                    .then_inc(chip.summed.sem, 1)

        @block.scalar
        def _(act):
            nc.scalar.activation(u[:, R_G:R_G + RET_H, :], u[:, R_G:R_G + RET_H, :], ACT.Silu).then_inc(chip.silu_done.sem, 1)
            for n, part in enumerate(halves):
                act.wait_ge(chip.product.sem, chip.product.at(2 * n + 2))
                nc.scalar.activation(ry[:, part], chip.bank[2 + n][:, :], ACT.Copy).then_inc(chip.copied.sem, 1)
            act.wait_ge(chip.scaled.sem, chip.scaled.at(1))
            nc.scalar.activation(t1, ry, ACT.Square).then_inc(chip.squared.sem, 1)
            for n, part in enumerate(halves):
                act.wait_ge(chip.summed.sem, chip.summed.at(3 + n))
                last = nc.scalar.activation(t2[:, part], chip.bank[6 + n][:, :], ACT.Sqrt, bias=chip.eps[:, 0:1], scale=1.0 / P)
            last.then_inc(chip.rooted.sem, 1)

        @block.vector
        def _(dve):
            for h in range(RET_H):
                dve.wait_ge(chip.scored.sem, chip.scored.at(h + 1))
                if h >= 2:
                    dve.wait_ge(chip.product.sem, chip.product.at(h - 1))
                b = chip.bank[h % 2]
                nc.vector.tensor_tensor(sr[:, h % 2, 0:S], b[:, 0:S], decay[:, h, :], ALU.mult)
                nc.vector.tensor_tensor(sr[:, h % 2, S:384], b[:, S:384], decay[:, h, 0:P], ALU.mult).then_inc(chip.probs.sem, 1)
            dve.wait_ge(chip.copied.sem, chip.copied.at(2))
            dve.wait_ge(chip.summed.sem, chip.summed.at(2))
            for n, part in enumerate(halves):
                last = nc.vector.scalar_tensor_tensor(ry[:, part], chip.bank[4 + n][:, :], -1.0 / P, ry[:, part], ALU.mult, ALU.add)
            last.then_inc(chip.scaled.sem, 1)
            dve.wait_ge(chip.rooted.sem, chip.rooted.at(1))
            dve.wait_ge(chip.silu_done.sem, chip.silu_done.at(1))
            in_order(dve, chip.dve_step, nc.vector.reciprocal(t2, t2))
            in_order(dve, chip.dve_step, nc.vector.tensor_tensor(ry, ry, t2, ALU.mult))
            nc.vector.tensor_tensor(y[:, 0:RET_H, :].rearrange("p a b -> p (a b)"), ry,
                                    u[:, R_G:R_G + RET_H, :].rearrange("p a b -> p (a b)"), ALU.mult)
    for sig, n in ((chip.scored, 4), (chip.probs, 4), (chip.product, 4), (chip.copied, 2), (chip.summed, 4),
                   (chip.squared, 1), (chip.rooted, 1), (chip.scaled, 1), (chip.silu_done, 1)):
        sig.passed(n)


def stage_compress(chip):
    nc = chip.nc
    u = chip.part(B_U, N_PROJ, S)
    w1 = [chip.part(B_W1 + 4096 * n, 16, 256) for n in range(2)]
    w2 = [chip.part(B_W2 + 128 * n, 2, 64) for n in range(2)]
    k2 = [chip.part(B_K2 + 512 * n, 2, S) for n in range(2)]
    blk = [chip.part(B_BLK + 480 * n, 16, 30) for n in range(2)]
    hid = [chip.part(B_HID + 60 * n, 2, 30) for n in range(2)]
    ptc = chip.part(B_PTC, NSA_H, S)
    s_c, mask01, add = chip.part(B_C, 16, 16), table(chip, "cmp_mask", 2, 16), table(chip, "cmp_add", 2, 16)
    top, tot = chip.part(B_C + 256, 16), chip.part(B_C + 272, 16)
    kc, vc = chip.part(B_C + 288, 16), chip.part(B_C + 304, 2, 64)
    sc = s_c[:, :, 0:NCB]
    with nc.Block() as block:
        @block.vector
        def _(dve):
            for n, chunk in enumerate((N_KC, N_VC)):
                for g in range(2):
                    src = u[64 * g:64 * g + 64, chunk, :]
                    nc.vector.tensor_copy(k2[n][0:64, g, :], src)
                    last = nc.vector.tensor_copy(k2[n][64:128, g, 0:S - 1], src[:, 1:S])
            nc.vector.memset(k2[0][64:128, :, S - 1:S], 0.0)
            in_order(dve, chip.dve_step, nc.vector.memset(k2[1][64:128, :, S - 1:S], 0.0))
            for n, pe_col in enumerate(("pe_k", "pe_v")):
                for g in range(2):
                    v = k2[n][:, g, :].rearrange("p (n l) -> p l n", l=CMP_STRIDE)
                    for j0 in (0, 8):
                        out = blk[n][:, j0:j0 + 8, g * NCB:(g + 1) * NCB]
                        pos = chip.col(pe_col, j0, 8).unsqueeze(2).to_broadcast([P, 8, NCB])
                        at = j0 // 8
                        last = nc.vector.tensor_tensor(out, v[:, 0:CMP_STRIDE:2, at:at + NCB], pos, ALU.add)
            last.then_inc(chip.gated.sem, 1)
            dve.wait_ge(chip.scored.sem, chip.scored.at(1))
            for qt in range(2):
                for g in range(2):
                    last = nc.vector.scalar_tensor_tensor(
                        s_c[:, 8 * qt + g:8 * qt + 8:2, 0:NCB],
                        chip.bank[6 + g][:, 64 * qt:64 * qt + 64].rearrange("p (h n) -> p h n", n=16)[:, :, 0:NCB], 0.125,
                        add[:, qt, 0:NCB].unsqueeze(1).to_broadcast([P, 4, NCB]), ALU.mult, ALU.add)
            in_order(dve, chip.dve_step, last)
            in_order(dve, chip.dve_step, nc.vector.tensor_reduce(top, sc, AX.X, ALU.max))
            nc.vector.tensor_tensor(sc, sc, top.unsqueeze(2).to_broadcast([P, 16, NCB]), ALU.subtract).then_inc(chip.maxed.sem, 1)
            dve.wait_ge(chip.exped.sem, chip.exped.at(1))
            for qt in range(2):
                last = nc.vector.tensor_tensor(s_c[:, 8 * qt:8 * qt + 8, 0:NCB], s_c[:, 8 * qt:8 * qt + 8, 0:NCB],
                                               mask01[:, qt, 0:NCB].unsqueeze(1).to_broadcast([P, 8, NCB]), ALU.mult)
            in_order(dve, chip.dve_step, last)
            in_order(dve, chip.dve_step, nc.vector.tensor_reduce(tot, sc, AX.X, ALU.add))
            in_order(dve, chip.dve_step, nc.vector.tensor_scalar(tot, tot, TINY, None, ALU.max))
            in_order(dve, chip.dve_step, nc.vector.reciprocal(tot, tot))
            gate = chip.gates[:, :, :].rearrange("p t (h b) -> p (t h) b", b=3)[:, :, 0]
            in_order(dve, chip.dve_step, nc.vector.tensor_tensor(tot, tot, gate, ALU.mult))
            nc.vector.tensor_tensor(sc, sc, tot.unsqueeze(2).to_broadcast([P, 16, NCB]), ALU.mult).then_inc(chip.probs.sem, 1)

        @block.tensor
        def _(pe):
            pe.wait_ge(chip.gated.sem, chip.gated.at(1))
            for n in range(2):
                for m in range(2):
                    for j in range(16):
                        mm = nc.tensor.matmul(chip.bank[2 * n + m][:, 0:2 * NCB], w1[n][:, j, m * P:(m + 1) * P],
                                              blk[n][:, j, :], start=(j == 0), stop=(j == 15))
                    mm.then_inc(chip.product.sem, 1)
            pe.wait_ge(chip.silu_done.sem, chip.silu_done.at(4))
            for g in range(2):
                for m in range(2):
                    nc.tensor.matmul(chip.bank[4][64 * g:64 * g + 64, 0:NCB], w2[0][:, m, :],
                                     hid[0][:, m, g * NCB:(g + 1) * NCB], start=(m == 0), stop=(m == 1))
                for m in range(2):
                    mm = nc.tensor.matmul(chip.bank[5][0:NCB, 64 * g:64 * g + 64], hid[1][:, m, g * NCB:(g + 1) * NCB],
                                          w2[1][:, m, :], start=(m == 0), stop=(m == 1))
            mm.then_inc(chip.product.sem, 1)
            pe.wait_ge(chip.copied.sem, chip.copied.at(1))
            for qt in range(2):
                for hh in range(NSA_H):
                    po, n = 64 * (hh % 2), 4 * qt + hh // 2
                    mm = nc.tensor.matmul(chip.bank[6 + hh % 2][:, n * 16:n * 16 + NCB], u[po:po + 64, N_Q + hh // 2, qt * P:(qt + 1) * P],
                                          kc[po:po + 64, 0:NCB], start=True, stop=True)
            mm.then_inc(chip.scored.sem, 1)
            pe.wait_ge(chip.probs.sem, chip.probs.at(1))
            for hh in range(NSA_H):
                for qt in range(2):
                    n = 2 * hh + qt
                    mm = nc.tensor.matmul(chip.bank[n // 4][0:NCB, (n % 4) * P:(n % 4 + 1) * P], s_c[:, 8 * qt + hh, 0:NCB],
                                          chip.ident[:, :], start=True, stop=True)
            mm.then_inc(chip.turned.sem, 1)

        @block.scalar
        def _(act):
            for n in range(2):
                for m in range(2):
                    act.wait_ge(chip.product.sem, chip.product.at(2 * n + m + 1))
                    nc.scalar.activation(hid[n][:, m, :], chip.bank[2 * n + m][:, 0:2 * NCB], ACT.Gelu_apprx_tanh,
                                         bias=chip.col(("b_cmp_k", "b_cmp_v")[n], m, 1)).then_inc(chip.silu_done.sem, 1)
            act.wait_ge(chip.product.sem, chip.product.at(5))
            nc.scalar.activation(kc[:, 0:NCB], chip.bank[4][:, 0:NCB], ACT.Copy)
            nc.scalar.activation(vc[0:NCB, :, :].rearrange("p a b -> p (a b)"), chip.bank[5][0:NCB, 0:P], ACT.Copy).then_inc(chip.copied.sem, 1)
            act.wait_ge(chip.maxed.sem, chip.maxed.at(1))
            nc.scalar.activation(sc, sc, ACT.Exp).then_inc(chip.exped.sem, 1)
            act.wait_ge(chip.turned.sem, chip.turned.at(1))
            for b in range(4):
                nc.scalar.activation(ptc[0:NCB, 2 * b:2 * b + 2, :].rearrange("p a b -> p (a b)"), chip.bank[b][0:NCB, :], ACT.Copy)
    for sig, n in ((chip.gated, 1), (chip.scored, 1), (chip.maxed, 1), (chip.exped, 1), (chip.probs, 1), (chip.product, 5),
                   (chip.silu_done, 4), (chip.copied, 1), (chip.turned, 1)):
        sig.passed(n)


def stage_sparse(chip):
    nc = chip.nc
    u, vs, y = chip.part(B_U, N_PROJ, S), chip.part(B_VS, 2, S), chip.part(B_Y, KT, S)
    sc, pts, ptc = chip.part(B_SC, 2, 2, S), chip.part(B_PTS, 2, 2, 384), chip.part(B_PTC, NSA_H, S)
    vc, causal = chip.part(B_C + 304, 2, 64), table(chip, "causal")
    items = [(hh, qt) for hh in range(NSA_H) for qt in range(2)]

    with nc.Block() as block:
        @block.tensor
        def _(pe):
            def scores(w):
                hh, qt = items[w]
                po, nk = 64 * (hh % 2), P * (qt + 1)
                if w >= 2:
                    pe.wait_ge(chip.scores_read.sem, chip.scores_read.at(w - 1))
                for br, chunk in enumerate((N_KS, N_KW)):
                    mm = nc.tensor.matmul(chip.bank[w % 2][:, br * S:br * S + nk], u[po:po + 64, N_Q + hh // 2, qt * P:(qt + 1) * P],
                                          u[po:po + 64, chunk, 0:nk], start=True, stop=True)
                mm.then_inc(chip.scored.sem, 1)

            def transposes(w):
                hh, qt = items[w]
                pe.wait_ge(chip.probs.sem, chip.probs.at(w + 1))
                if w >= 2:
                    pe.wait_ge(chip.copied.sem, chip.copied.at(w - 1))
                for br in range(2):
                    for kt in range(qt + 1):
                        mm = nc.tensor.transpose(chip.bank[2 + w % 2][:, (2 * br + kt) * P:(2 * br + kt + 1) * P],
                                                 sc[:, w % 2, br, kt * P:(kt + 1) * P], chip.ident[:, :])
                mm.then_inc(chip.turned.sem, 1)

            def values(hh):
                g = hh % 2
                pe.wait_ge(chip.copied.sem, chip.copied.at(2 * hh + 2))
                if hh >= 2:
                    pe.wait_ge(chip.moved.sem, chip.moved.at(hh - 1))
                o = chip.bank[4 + hh % 2][64 * g:64 * g + 64, :]
                for br in range(2):
                    v = slice(br * P + g * 64, br * P + g * 64 + 64)
                    nc.tensor.matmul(o[:, 0:S], vs[:, 0, v], pts[:, hh % 2, br, 0:S], start=(br == 0), stop=False)
                    nc.tensor.matmul(o[:, P:S], vs[:, 1, v], pts[:, hh % 2, br, S:384], start=False, stop=False)
                nc.tensor.matmul(o[:, 0:S], vc[0:NCB, g, :], ptc[0:NCB, hh, :], start=False, stop=True).then_inc(chip.product.sem, 1)

            scores(0)
            scores(1)
            for w in range(len(items)):
                transposes(w)
                if w + 2 < len(items):
                    scores(w + 2)
                if w >= 2 and w % 2 == 0:
                    values(w // 2 - 1)
            values(NSA_H - 1)

        @block.scalar
        def _(act):
            def exps(w):
                hh, qt = items[w]
                nk = P * (qt + 1)
                act.wait_ge(chip.maxed.sem, chip.maxed.at(w + 1))
                for br in range(2):
                    last = nc.scalar.activation(sc[:, w % 2, br, 0:nk], sc[:, w % 2, br, 0:nk], ACT.Exp,
                                                bias=chip.nmax4[:, w % 2, br:br + 1], accum_out=chip.rsum4[:, w % 2, br:br + 1])
                last.then_inc(chip.exped.sem, 1)

            def copies(w):
                hh, qt = items[w]
                act.wait_ge(chip.turned.sem, chip.turned.at(w + 1))
                if hh >= 2:
                    act.wait_ge(chip.product.sem, chip.product.at(hh - 1))
                src = chip.bank[2 + w % 2][:, :].rearrange("p (b k) -> p b k", b=2)
                nc.scalar.activation(pts[:, hh % 2, :, P * qt:P * qt + P * (qt + 1)], src[:, :, 0:P * (qt + 1)], ACT.Copy)\
                    .then_inc(chip.copied.sem, 1)

            def move(hh):
                po = 64 * (hh % 2)
                act.wait_ge(chip.product.sem, chip.product.at(hh + 1))
                nc.scalar.activation(y[po:po + 64, 4 + hh // 2, :], chip.bank[4 + hh % 2][po:po + 64, 0:S], ACT.Copy)\
                    .then_inc(chip.moved.sem, 1)

            exps(0)
            for w in range(len(items)):
                if w + 1 < len(items):
                    exps(w + 1)
                copies(w)
                if w >= 3 and w % 2 == 1:
                    move(w // 2 - 1)
            move(NSA_H - 1)

        @block.vector
        def _(dve):
            def scale(w):
                hh, qt = items[w]
                nk = P * (qt + 1)
                s = sc[:, w % 2, :, 0:nk]
                dve.wait_ge(chip.scored.sem, chip.scored.at(w + 1))
                if w >= 2:
                    dve.wait_ge(chip.turned.sem, chip.turned.at(w - 1))
                nc.vector.scalar_tensor_tensor(s, chip.bank[w % 2][:, :].rearrange("p (b k) -> p b k", b=2)[:, :, 0:nk], 0.125,
                                               causal[:, S - nk:S].unsqueeze(1).to_broadcast([P, 2, nk]), ALU.mult, ALU.add)\
                    .then_inc(chip.scores_read.sem, 1)
                dve.wait_ge(chip.scores_read.sem, chip.scores_read.at(w + 1))
                nc.vector.tensor_reduce(chip.nmax4[:, w % 2, :], s, AX.X, ALU.max, negate=True).then_inc(chip.maxed.sem, 1)

            def normalise(w):
                hh, qt = items[w]
                nk = P * (qt + 1)
                s, r = sc[:, w % 2, :, 0:nk], chip.rsum4[:, w % 2, :]
                dve.wait_ge(chip.exped.sem, chip.exped.at(w + 1))
                in_order(dve, chip.dve_step, nc.vector.reciprocal(r, r))
                in_order(dve, chip.dve_step, nc.vector.tensor_tensor(r, r, chip.gates[:, qt, 3 * hh + 1:3 * hh + 3], ALU.mult))
                nc.vector.tensor_tensor(s, s, r.unsqueeze(2).to_broadcast([P, 2, nk]), ALU.mult).then_inc(chip.probs.sem, 1)

            scale(0)
            for w in range(len(items)):
                if w + 1 < len(items):
                    scale(w + 1)
                normalise(w)
    n = len(items)
    for sig in (chip.scored, chip.scores_read, chip.maxed, chip.exped, chip.probs, chip.turned, chip.copied):
        sig.passed(n)
    chip.product.passed(NSA_H)
    chip.moved.passed(NSA_H)


def stage_expert_scores(chip, stream):
    nc = chip.nc
    norm = norm2(chip, 1, E_SC2)
    q, s = chip.part(E_Q, 16, S), chip.part(E_SC, 2, 16, NK)
    with nc.Block() as block:
        @block.sync
        def _(sp):
            stream.load_ahead(sp, 9)

        @block.tensor
        def _(pe):
            norm.tensor(pe)
            pe.wait_ge(chip.h_ready.sem, chip.h_ready.at(KT))
            for k in range(8):
                stream.wait_loaded(pe, 0, k)
                w = stream.slot(k)
                if k >= 2:
                    pe.wait_ge(chip.copied.sem, chip.copied.at(k - 1))
                for b in range(2):
                    for kt in range(KT):
                        mm = nc.tensor.matmul(chip.bank[k % 2][:, b * S:(b + 1) * S], w[:, kt * 256 + b * P:kt * 256 + (b + 1) * P],
                                              chip.h2[:, kt, :], start=(kt == 0), stop=(kt == KT - 1))
                mm.then_inc(stream.used, 1)
            stream.wait_loaded(pe, 0, 8)
            pe.wait_ge(chip.copied.sem, chip.copied.at(8))
            keys = stream.slot(8)
            for tt in range(2):
                for n in range(16):
                    mm = nc.tensor.matmul(chip.bank[4 * tt + n // 4][:, (n % 4) * NK:(n % 4 + 1) * NK],
                                          q[:, n, tt * P:(tt + 1) * P], keys[:, n * NK:(n + 1) * NK], start=True, stop=True)
            mm.then_inc(stream.used, 1)

        @block.scalar
        def _(act):
            norm.scalar(act)
            for k in range(8):
                act.wait_ge(stream.used, stream.used_at(k))
                nc.scalar.activation(q[:, 2 * k:2 * k + 2, :].rearrange("p a b -> p (a b)"), chip.bank[k % 2][:, :], ACT.Copy)\
                    .then_inc(chip.copied.sem, 1)
            act.wait_ge(stream.used, stream.used_at(8))
            for b in range(8):
                nc.scalar.activation(s[:, b // 4, 4 * (b % 4):4 * (b % 4) + 4, :].rearrange("p a b -> p (a b)"),
                                     chip.bank[b][:, :], ACT.Copy)

        @block.vector
        def _(dve):
            norm.vector(dve)
    norm.end()
    chip.copied.passed(8)
    stream.g0 += 9


def stage_retrieve(chip):
    nc = chip.nc
    s = chip.part(E_SC, 2, 16, NK)
    rest = [chip.part(E_SC2 + 256 * n, 256) for n in range(2)]
    v, ix = chip.part(E_V, 2, 16, TOPK), chip.part(E_I, 2, 16, TOPK).bitcast(U32)
    ixf = chip.part(E_IF, 2, 16, TOPK)
    tv, tj = chip.part(E_TV, 2, SLOTS), chip.part(E_TJ, 2, SLOTS).bitcast(U32)
    jj, jf = chip.part(E_J, 2, SLOTS).bitcast(U32), chip.part(E_JF, 2, SLOTS)
    eq = chip.part(E_EQ, PH * TOPK, TOPK)
    slots = chip.part(E_N, 3, SLOTS)
    small = chip.part(E_W, 64)
    cand = chip.part(E_CAND, 2, PH, TOPK * TOPK)
    iota16, iota = chip.iota[:, 0:TOPK], chip.iota

    with nc.Block() as block:
        @block.gpsimd
        def _(pool):
            nc.gpsimd.iota(iota[:, :], [[1, P]], base=0, channel_multiplier=0, allow_small_or_imprecise_dtypes=True)\
                .then_inc(chip.table.sem, 1)

        @block.vector
        def _(dve):
            step = lambda ins: in_order(dve, chip.dve_step, ins)

            def best(values, index, source, spare):
                both = list(zip(values, index, source, spare))
                for lo in (0, 8):
                    src = [x[2] if lo == 0 else x[3] for x in both]
                    for x, sr in zip(both, src):
                        last = nc.vector.max(x[0][:, lo:lo + 8], sr)
                    step(last)
                    for x, sr in zip(both, src):
                        last = nc.vector.max_index(x[1][:, lo:lo + 8], x[0][:, lo:lo + 8], sr)
                        if lo == 0:
                            last = nc.vector.match_replace(x[3], x[0][:, 0:8], sr, -3e38)
                    step(last)

            for tt in range(2):
                for n in range(0, 16, 2):
                    best([v[:, tt, n + i, :] for i in range(2)], [ix[:, tt, n + i, :] for i in range(2)],
                         [s[:, tt, n + i, :] for i in range(2)], [rest[i][:, 0:NK] for i in range(2)])
            step(nc.vector.tensor_copy(ixf, ix))
            for tt in range(2):
                vp = v[:, tt, :, :].rearrange("p (h two) k -> p h two k", two=2)
                for h in range(PH):
                    last = nc.vector.tensor_tensor(
                        cand[:, tt, h, :].rearrange("p (a b) -> p a b", b=TOPK),
                        vp[:, h, 0, :].unsqueeze(2).to_broadcast([P, TOPK, TOPK]),
                        vp[:, h, 1, :].unsqueeze(1).to_broadcast([P, TOPK, TOPK]), ALU.add)
            step(last)
            for tt in range(2):
                for h in range(0, PH, 2):
                    at = lambda x: [x[:, tt, (h + i) * TOPK:(h + i + 1) * TOPK] for i in range(2)]
                    best(at(tv), at(tj), [cand[:, tt, h + i, :] for i in range(2)], rest)
            dve.wait_ge(chip.table.sem, chip.table.at(1))
            for tt in range(2):
                for half in range(2):
                    step(nc.vector.tensor_scalar(jj[:, half, :], tj[:, tt, :], 4 if half == 0 else 15, None,
                                                 ALU.logical_shift_right if half == 0 else ALU.bitwise_and))
                    step(nc.vector.tensor_copy(jf[:, half, :], jj[:, half, :]))
                    step(nc.vector.tensor_tensor(eq, iota16.unsqueeze(1).to_broadcast([P, SLOTS, TOPK]),
                                                 jf[:, half, :].unsqueeze(2).to_broadcast([P, SLOTS, TOPK]), ALU.is_equal))
                    e4 = eq.rearrange("p (h k) i -> p h k i", h=PH)
                    sub = ixf[:, tt, :, :].rearrange("p (h two) k -> p h two k", two=2)[:, :, half, :]
                    step(nc.vector.tensor_tensor(e4, e4, sub.unsqueeze(2).to_broadcast([P, PH, TOPK, TOPK]), ALU.mult))
                    if tt == 1 and half == 0:
                        dve.wait_ge(chip.turned.sem, chip.turned.at(1))
                    step(nc.vector.tensor_reduce(slots[:, half, :], eq, AX.X, ALU.add))
                w = slots[:, 2, :].rearrange("p (h k) -> p h k", h=PH)
                t3 = tv[:, tt, :].rearrange("p (h k) -> p h k", h=PH)
                nc.vector.tensor_tensor(w, t3, t3[:, :, 0:1].to_broadcast([P, PH, TOPK]), ALU.subtract)\
                    .then_inc(chip.maxed.sem, 1)
                dve.wait_ge(chip.exped.sem, chip.exped.at(tt + 1))
                step(nc.vector.tensor_reduce(small[:, 0:PH], w, AX.X, ALU.add))
                step(nc.vector.reciprocal(small[:, 0:PH], small[:, 0:PH]))
                nc.vector.tensor_tensor(w, w, small[:, 0:PH].unsqueeze(2).to_broadcast([P, PH, TOPK]), ALU.mult)\
                    .then_inc(chip.probs.sem, 1)

        @block.scalar
        def _(act):
            for tt in range(2):
                act.wait_ge(chip.maxed.sem, chip.maxed.at(tt + 1))
                nc.scalar.activation(slots[:, 2, :], slots[:, 2, :], ACT.Exp).then_inc(chip.exped.sem, 1)
                act.wait_ge(chip.turned.sem, chip.turned.at(tt + 1))
                nc.scalar.activation(chip.slot_t[:, :, tt * P:(tt + 1) * P],
                                     chip.bank[tt][:, 0:3 * P].rearrange("p (a b) -> p a b", b=P), ACT.Copy)

        @block.tensor
        def _(pe):
            for tt in range(2):
                pe.wait_ge(chip.probs.sem, chip.probs.at(tt + 1))
                for n in range(3):
                    mm = nc.tensor.transpose(chip.bank[tt][:, n * P:(n + 1) * P], slots[:, n, :], chip.ident[:, :])
                mm.then_inc(chip.turned.sem, 1)
    for sig in (chip.maxed, chip.exped, chip.probs, chip.turned):
        sig.passed(2)
    chip.table.passed(1)


def stage_spread(chip):
    nc = chip.nc
    weight = chip.part(0, S, NK)
    a, b = chip.work[:, 0:4, 0:P], chip.work[:, 0:4, P:2 * P]
    with nc.Block() as block:
        @block.vector
        def _(dve):
            def onehots(c, j):
                t = NS * c + j
                if not static(c):
                    dve.wait_ge(chip.product.sem, chip.product.at(t - 3))
                col = lambda n: chip.slot_t[:, n, bass.ds(t, 1)]
                nc.vector.tensor_scalar(a[:, j, :], chip.iota[:, :], col(0), col(2), ALU.is_equal, ALU.mult)
                nc.vector.tensor_scalar(b[:, j, :], chip.iota[:, :], col(1), None, ALU.is_equal).then_inc(chip.probs.sem, 1)
            over_units(dve, S, onehots)

        @block.tensor
        def _(pe):
            def spread(c, j):
                t = NS * c + j
                if not static(c) and j % 2 == 0:
                    pe.wait_ge(chip.copied.sem, chip.copied.at(2 * c + (j // 2 - 1)))
                pe.wait_ge(chip.probs.sem, chip.probs.at(t + 1))
                nc.tensor.matmul(chip.bank[j // 2][:, (j % 2) * P:(j % 2 + 1) * P], a[:, j, :], b[:, j, :],
                                 start=True, stop=True).then_inc(chip.product.sem, 1)
            over_units(pe, S, spread)

        @block.scalar
        def _(act):
            with act.Fori(0, S // NS) as c:
                for j in range(2):
                    act.wait_ge(chip.product.sem, chip.product.at(NS * c + (2 * j + 2)))
                    nc.scalar.activation(weight[:, bass.ds(NS * c + 2 * j, 2), :].rearrange("p a b -> p (a b)"),
                                         chip.bank[j][:, 0:2 * P], ACT.Copy).then_inc(chip.copied.sem, 1)
    chip.product.passed(S)
    chip.probs.passed(S)
    chip.copied.passed(S // 2)


def stage_experts(chip, stream):
    nc = chip.nc
    weight, g = chip.part(0, S, NK), chip.work
    steps = NK
    with nc.Block() as block:
        @block.sync
        def _(sp):
            stream.load_ahead(sp, 128)

        @block.tensor
        def _(pe):
            def down(c, j, unit, at):
                if not static(c):
                    pe.wait_ge(chip.gelu_done.sem, chip.gelu_done.at(NS * c + (j - 3)))
                w = stream.ring[:, (stream.g0 + unit) % NS, at * 1024:(at + 1) * 1024]
                for kt in range(KT):
                    mm = nc.tensor.matmul(chip.bank[j][:, 0:S], w[:, kt * P:(kt + 1) * P], chip.h2[:, kt, :],
                                          start=(kt == 0), stop=(kt == KT - 1))
                return mm

            def up(c, j, unit, at, first=False, last=False):
                pe.wait_ge(chip.gated.sem, chip.gated.at(NS * c + (j + 1)))
                w = stream.ring[:, (stream.g0 + unit) % NS, at * 1024:(at + 1) * 1024]
                for tt in range(2):
                    for half in range(2):
                        mm = nc.tensor.matmul(chip.bank[4 + 2 * tt + half][:, :], g[:, j, tt * P:(tt + 1) * P],
                                              w[:, half * 512:(half + 1) * 512], start=first, stop=last)
                return mm

            def loaded(c, unit):
                x = stream.g0 + unit
                pe.wait_ge(stream.loaded[x % NS], 16 * (c + (x // NS + 1)))

            loaded(0, 0)
            down(0, 0, 0, 0).then_inc(chip.product.sem, 1)
            down(0, 1, 0, 1).then_inc(stream.used, 1)
            loaded(0, 1)
            down(0, 2, 1, 0).then_inc(chip.product.sem, 1)
            loaded(0, 2)
            up(0, 0, 2, 0, first=True)
            down(0, 3, 1, 1).then_inc(stream.used, 1)
            up(0, 1, 2, 1).then_inc(stream.used, 1)
            with pe.Fori(1, steps // NS) as c:
                loaded(c - 1, 3)
                down(c, 0, 3, 0).then_inc(chip.product.sem, 1)
                loaded(c - 1, 4)
                up(c - 1, 2, 4, 0)
                down(c, 1, 3, 1).then_inc(stream.used, 1)
                up(c - 1, 3, 4, 1).then_inc(stream.used, 1)
                loaded(c - 1, 5)
                down(c, 2, 5, 0).then_inc(chip.product.sem, 1)
                loaded(c - 1, 6)
                up(c, 0, 6, 0)
                down(c, 3, 5, 1).then_inc(stream.used, 1)
                up(c, 1, 6, 1).then_inc(stream.used, 1)
            end = steps // NS - 1
            loaded(end, 3)
            up(end, 2, 3, 0)
            up(end, 3, 3, 1, last=True).then_inc(stream.used, 1)

        @block.scalar
        def _(act):
            def gelu(c, j):
                if j % 2 == 0:
                    act.wait_ge(chip.product.sem, chip.product.at(2 * c + (j // 2 + 1)))
                elif static(c):
                    act.wait_ge(stream.used, stream.used_at((0, 0, 0, 1)[j]))
                else:
                    act.wait_ge(stream.used, stream.used_at(NS * c + (j - 2)))
                nc.scalar.activation(g[:, j, :], chip.bank[j][:, 0:S], ACT.Gelu_apprx_tanh).then_inc(chip.gelu_done.sem, 1)
            over_units(act, steps, gelu)

        @block.vector
        def _(dve):
            def weigh(c, j):
                k = NS * c + j
                dve.wait_ge(chip.gelu_done.sem, chip.gelu_done.at(k + 1))
                nc.vector.tensor_tensor(g[:, j, :], g[:, j, :], weight[:, :, k], ALU.mult).then_inc(chip.gated.sem, 1)
            over_units(dve, steps, weigh)
    chip.product.passed(steps // 2)
    chip.gelu_done.passed(steps)
    chip.gated.passed(steps)
    stream.g0 += 128


def stage_finish(chip, out):
    nc = chip.nc
    o = chip.part(0, 2, D)
    norm = Norm(chip, chip.x2, chip.h2, chip.part(4096, S), chip.part(4096 + S, S),
                lambda kt, g: chip.col("g_final", kt, 1), None, [(0, S)], S)
    with nc.Block() as block:
        @block.scalar
        def _(act):
            for n in range(4):
                nc.scalar.activation(o[:, n // 2, (n % 2) * 512:(n % 2 + 1) * 512], chip.bank[4 + n][:, :], ACT.Copy)\
                    .then_inc(chip.copied.sem, 1)

        @block.tensor
        def _(pe):
            pe.wait_ge(chip.copied.sem, chip.copied.at(4))
            for kt in range(KT):
                for tt in range(2):
                    mm = nc.tensor.transpose(chip.bank[kt // 2][:, (kt % 2) * S + tt * P:(kt % 2) * S + (tt + 1) * P],
                                             o[:, tt, kt * P:(kt + 1) * P], chip.ident[:, :])
                mm.then_inc(chip.turned.sem, 1)

        @block.vector
        def _(dve):
            for kt in range(KT):
                dve.wait_ge(chip.turned.sem, chip.turned.at(2 * (kt // 2) + 2))
                nc.vector.scalar_tensor_tensor(chip.x2[:, kt, :], chip.bank[kt // 2][:, (kt % 2) * S:(kt % 2 + 1) * S],
                                               chip.mod2[:, 5 * KT + kt:5 * KT + kt + 1], chip.x2[:, kt, :], ALU.mult, ALU.add)
    chip.copied.passed(4)
    chip.turned.passed(KT)
    with nc.Block() as block:
        block.tensor(norm.tensor)
        block.scalar(norm.scalar)
        block.vector(norm.vector)

        @block.sync
        def _(sp):
            sp.wait_ge(chip.h_ready.sem, chip.h_ready.at(KT))
            sp.dma_start(out, chip.h2[:, :, :]).then_inc(chip.table.sem, 16)
            sp.wait_ge(chip.table.sem, chip.table.at(16))


def build(nc, dram, out):
    with ExitStack() as ctx:
        chip = Chip(ctx, nc, dram)
        segments = []
        for l in range(LAYERS):
            segments += [(dram["w_mod"][l], 36, UNIT),
                         (dram["ffn_in"][l][0], FT, UNIT), (dram["ffn_out"][l][0], KT, FFN_OUT_UNIT),
                         (dram["w_mix"][l], 14, UNIT),
                         (dram["ffn_in"][l][1], FT, UNIT), (dram["ffn_out"][l][1], KT, FFN_OUT_UNIT)]
        segments += [(dram["w_ada"], 24, UNIT), (dram["w_second"], 27, UNIT), (dram["experts"], 128, UNIT)]
        stream = Stream(chip.ring, chip.unit_loaded, chip.unit_used, segments)
        stage_setup(chip)
        for l in range(LAYERS):
            last = l == LAYERS - 1
            width = S if last else T2
            groups = [(0, S)] if last else [(0, S), (S, T2)]
            stage_mod(chip, stream, l)
            stage_ffn(chip, stream, 0, T2)
            stage_mix_in(chip, stream, l, last)
            stage_mix(chip, stream, l, last)
            stage_add_product(chip, stream, chip.part(A_X, KT, T2), chip.part(A_Y, KT, T2),
                              lambda n, g: chip.mod[:, 5 * KT + n, g:g + 1], groups)
            stage_ffn(chip, stream, 1, width)
        stage_final_norm(chip)
        stage_mod(chip, stream, None)
        stage_proj(chip, stream)
        stage_rope(chip)
        stage_retention(chip)
        stage_compress(chip)
        stage_sparse(chip)
        stage_add_product(chip, stream, chip.x2, chip.part(B_Y, KT, S), lambda n, g: chip.mod2[:, 2 * KT + n:2 * KT + n + 1], [(0, S)])
        stage_expert_scores(chip, stream)
        stage_retrieve(chip)
        stage_spread(chip)
        stage_experts(chip, stream)
        stage_finish(chip, out)


def _layout(inp):
    def pack(w):
        k, n = w.shape
        return w.reshape(k // P, P, n // 256, 256).transpose(2, 1, 0, 3).reshape(n // 256, P, k // P * 256)

    def vec(v):
        return v.reshape(-1, P).T

    f = np.float32
    a = {}
    a["w_mod"] = np.stack([pack(w) for w in inp["w_mod"]])
    fi = inp["ffn_w_in"].reshape(LAYERS, 2, KT, P, 2, FT, P)
    a["ffn_in"] = fi.transpose(0, 1, 5, 3, 2, 4, 6).reshape(LAYERS, 2, FT, P, UNIT)
    fo = inp["ffn_w_out"].reshape(LAYERS, 2, FT, P, KT, P)
    a["ffn_out"] = fo.transpose(0, 1, 4, 3, 2, 5).reshape(LAYERS, 2, KT, P, FFN_OUT_UNIT)
    a["w_mix"] = np.stack([np.concatenate([pack(inp["w_in"][l]), pack(inp["w_out"][l])]) for l in range(LAYERS)])
    x = np.concatenate([inp["x"][0], inp["ctx"][0]])
    a["x"] = x.T.reshape(KT, P, T2).transpose(1, 0, 2)
    cc = np.stack([vec(inp["c"][0]), vec(inp["c_ctx"])], axis=2).reshape(P, KT * 2)
    parts = {"cc": cc, "c2": vec(inp["c_2"][0]), "b_mod": vec(inp["b_mod"]), "norm_g": vec(inp["norm_g"]),
             "final_g": vec(inp["final_g"]), "conv_w": vec(inp["conv_w"]), "pool_scale": vec(inp["pool_scale"]),
             "b_ada": vec(inp["b_ada_2"]), "g_mix": vec(inp["g_norm_mix_2"]), "g_ffn": vec(inp["g_norm_ffn_2"]),
             "g_final": vec(inp["g_norm_final_2"]), "b_cmp_k": vec(inp["b_cmp_k1_2"]), "b_cmp_v": vec(inp["b_cmp_v1_2"]),
             "pe_k": vec(inp["pe_cmp_k_2"]), "pe_v": vec(inp["pe_cmp_v_2"])}
    a["cols"] = np.concatenate([parts[n] for n in COLS], axis=1)
    assert a["cols"].shape[1] == N_COLS
    rpb = np.zeros((LAYERS, NA_H, 7, 2 * GRID - 1), inp["rpb"].dtype)
    rpb[..., GRID - 16:GRID + 15] = inp["rpb"][:, :, 4:11, :]
    t = np.stack([rpb[..., GRID - 1 - q:2 * GRID - 1 - q] for q in range(GRID)], axis=1)
    a["rel_bias"] = np.concatenate([t[:, :, :, 1:7], t[:, :, :, 0:6]], axis=1).reshape(LAYERS, P, NA_H * BIAS_ROWS * GRID)
    pw = np.zeros((LAYERS, 2, 2, 64, 2, 64), inp["pool_w"].dtype)
    for g in range(4):
        pw[:, g // 2, g % 2, :, g % 2, :] = inp["pool_w"][:, g]
    a["pool_w"] = pw.reshape(LAYERS, 2, P, P).transpose(0, 2, 1, 3)
    cnt = np.zeros((4, S), f)
    for g, w in enumerate((2, 4, 8, 16)):
        tt = np.arange(S)
        cnt[g] = np.clip(tt + w - w // 2, 0, S) - np.clip(tt - w // 2, 0, S)
    a["pool_inv"] = np.repeat((f(1) / cnt).reshape(2, 2, 1, S), 64, axis=2).reshape(2, P, S).transpose(1, 0, 2)

    a["w_ada"] = pack(inp["w_ada_2"][0])
    w = inp["w_in_2"][0]
    cut = np.split(w, np.cumsum([512, 512, 512, 512, 512, 128, 128, 128, 128, 128, 128, 24])[:-1], axis=1)
    rq, rk, rv, rg, nq, kc, vc, ks, vs, kw, vw, gate = cut
    nq = nq.reshape(D, 2, 4, 64).transpose(0, 2, 1, 3).reshape(D, 512)
    gate = np.concatenate([gate.reshape(D, 2, 4, 3).transpose(0, 2, 1, 3).reshape(D, 24), np.zeros((D, 232), w.dtype)], axis=1)
    w_in2 = np.concatenate([rq, rk, nq, kc, ks, kw, vc, rg, rv, vs, vw, gate], axis=1)
    wo = inp["w_out_2"][0]
    wo = np.concatenate([wo[:512], wo[512:].reshape(2, 4, 64, D).transpose(1, 0, 2, 3).reshape(512, D)])
    sk = inp["peer_subkeys_2"][0].reshape(16, NK, P).transpose(2, 0, 1).reshape(1, P, UNIT)
    a["w_second"] = np.concatenate([pack(w_in2), pack(wo), pack(inp["w_peer_q_2"][0]), sk])
    down = inp["peer_down_2"][0].reshape(NK, 64, 2, KT, P).transpose(1, 4, 2, 3, 0).reshape(64, P, UNIT)
    up = inp["peer_up_2"][0].reshape(NK, 64, 2, D).transpose(1, 0, 2, 3).reshape(64, P, UNIT)
    order = [down[0], down[1], up[0]]
    for i in range(1, 32):
        order += [down[2 * i], up[2 * i - 1], down[2 * i + 1], up[2 * i]]
    a["experts"] = np.stack(order + [up[63]])
    for k, nm in (("k", "w_cmp_k"), ("v", "w_cmp_v")):
        w1 = inp[f"{nm}1_2"][0].reshape(16, P, 256).transpose(1, 0, 2)
        w2 = inp[f"{nm}2_2"][0].reshape(2, P, 64).transpose(1, 0, 2)
        a[f"cmp_{k}1"], a[f"cmp_{k}2"] = w1, w2

    tab = {}
    for dim, name in ((128, "128"), (64, "64")):
        inv = f(10000.0) ** (-np.arange(0, dim, 2, dtype=f) / f(dim))
        ang = np.arange(S, dtype=f)[None, :] * inv[:, None]
        tab["cos" + name] = np.tile(np.cos(ang).astype(f), (P // (dim // 2), 1))
        tab["sin" + name] = np.tile(np.sin(ang).astype(f), (P // (dim // 2), 1))
        perm = np.zeros((P, P), f)
        for m in range(P):
            half = dim // 2
            if m % dim < half:
                perm[m + half, m] = -1
            else:
                perm[m - half, m] = 1
        tab["perm" + name] = perm
    log_g = np.log1p(-np.exp2(f(-5.0) - np.arange(RET_H, dtype=f))).astype(f)
    diff = np.arange(S, dtype=f)[None, :] - np.arange(P, dtype=f)[:, None]
    dec = np.where(diff >= 0, np.exp(np.where(diff >= 0, diff, 0)[None] * log_g[:, None, None]), 0).astype(f)
    tab["decay"] = (dec * f(128 ** -0.5)).transpose(1, 0, 2).reshape(P, RET_H * S)
    q = np.arange(P)
    tab["causal"] = np.concatenate([np.zeros((P, P), f), np.where(q[None, :] <= q[:, None], 0, NEG).astype(f)], axis=1)
    n = np.arange(16)
    ok = np.stack([(CMP_STRIDE * n[None, :] + CMP_LEN - 1 <= q[:, None] + P * qt) & (n[None, :] < NCB) for qt in range(2)], axis=1)
    tab["cmp_add"] = np.where(ok, 0, NEG).astype(f).reshape(P, 32)
    tab["cmp_mask"] = ok.astype(f).reshape(P, 32)
    a["tables"] = np.concatenate([tab[n] for n in TAB], axis=1)
    assert a["tables"].shape[1] == N_TAB
    return {k: np.ascontiguousarray(v) for k, v in a.items()}


def kernel(**inputs):
    import concourse.bacc as bacc
    from concourse.bass_utils import run_bass_kernel_spmd

    arrays = _layout({k: np.asarray(v) for k, v in inputs.items()})
    nc = bacc.Bacc("TRN2", target_bir_lowering=False, num_devices=1)
    dram = {k: nc.dram_tensor(f"in_{k}", v.shape, mybir.dt.from_np(v.dtype), kind="ExternalInput").ap()
            for k, v in arrays.items()}
    out = nc.dram_tensor("out_x", (P, KT, S), F32, kind="ExternalOutput").ap()
    build(nc, dram, out)
    r = run_bass_kernel_spmd(nc, [{f"in_{k}": v for k, v in arrays.items()}], core_ids=[0])
    return r.results[0]["out_x"].transpose(2, 1, 0).reshape(1, S, D)
```

```python
from contextlib import ExitStack

import numpy as np

import concourse.bass as bass
from concourse import mybir

F32 = mybir.dt.float32
F32R = mybir.dt.float32r
U32 = mybir.dt.uint32
ALU = mybir.AluOpType
ACT = mybir.ActivationFunctionType
AX = mybir.AxisListType.X

P = 128
D = 1024
KT = D // P
S = 256
T2 = 2 * S
LAYERS = 2
D_FF = 2816
FT = D_FF // P
N_MOD = 9
LAYER_UNITS = N_MOD * KT // 2
MOD_UNITS = LAYERS * LAYER_UNITS + 6 * KT // 2
EPS = 1e-6
NEG = -1e30
TINY = float(np.finfo(np.float32).tiny)
NS = 4
UNIT = KT * P
MOD_UNIT = 2 * UNIT
HIDDEN = (8, 8, 6)
FFN_UNITS = 2 * FT + KT * len(HIDDEN)

CH_B, CH_C, CH_POOL, CH_Q, CH_K = 2, 4, 6, 8, 12
NA_H, DH = 8, 64
GRID = 64
BIAS_ROWS = 6
R_Q, R_K, N_Q, N_KC, N_KS, N_KW, N_VC, R_G = 0, 4, 8, 12, 13, 14, 15, 16
N_PROJ = 20
ROPE_WIDE, ROPE_ALL = 8, 15
RET_H = 4
NSA_H, NSA_G = 8, 2
CMP_LEN, CMP_STRIDE = 32, 16
NCB = (S - CMP_LEN) // CMP_STRIDE + 1
PH, TOPK, NK = 8, 16, 128
SLOTS = PH * TOPK

COLS = {}


def _columns():
    at = 0
    for name, n in [("cc", KT * 2), ("c2", KT), ("b_mod", LAYERS * N_MOD * KT), ("norm_g", LAYERS * 3 * KT),
                    ("final_g", KT), ("conv_w", LAYERS * 3 * 2), ("pool_scale", LAYERS * 2),
                    ("b_ada", 6 * KT), ("g_mix", KT), ("g_ffn", KT), ("g_final", KT),
                    ("b_cmp_k", 2), ("b_cmp_v", 2), ("pe_k", CMP_LEN // 2), ("pe_v", CMP_LEN // 2)]:
        COLS[name] = (at, n)
        at += n
    return at


N_COLS = _columns()
TAB = {}


def _tables():
    at = 0
    for name, n in [("cos128", S), ("sin128", S), ("cos64", S), ("sin64", S), ("perm128", P), ("perm64", P),
                    ("decay", RET_H * S), ("causal", S), ("cmp_add", 2 * 16), ("cmp_mask", 2 * 16)]:
        TAB[name] = (at, n)
        at += n
    return at


N_TAB = _tables()


class Signal:

    def __init__(self, ctx, nc, name):
        self.sem = ctx.enter_context(nc.semaphore(name))
        self.base = 0

    def at(self, n):
        return n + self.base

    def passed(self, n):
        self.base += n


class Stream:

    def __init__(self, ctx, nc, segments):
        self.nc, self.segments = nc, segments
        self.ring = ctx.enter_context(nc.sbuf_tensor("weight_ring", [P, NS, UNIT], F32))
        self.hi = ctx.enter_context(nc.sbuf_tensor("weight_hi", [P, 2, UNIT], F32R))
        self.lo = ctx.enter_context(nc.sbuf_tensor("weight_lo", [P, 2, UNIT], F32R))
        self.loaded = [ctx.enter_context(nc.semaphore(f"unit_loaded{s}")) for s in range(NS)]
        self.rounded = ctx.enter_context(nc.semaphore("unit_rounded"))
        self.split = ctx.enter_context(nc.semaphore("unit_split"))
        self.used = ctx.enter_context(nc.semaphore("unit_used"))
        self.total = sum(n for _, n in segments)
        self.g0 = 0

    def used_at(self, k):
        return k + (self.g0 + 1)

    def round(self, act, c, j):
        g = self.g0 + j
        act.wait_ge(self.loaded[g % NS], 16 * (c + (g // NS + 1)))
        if not (static(c) and NS * c + g < 2):
            act.wait_ge(self.used, NS * c + (g - 1))
        self.nc.scalar.activation(self.hi[:, g % 2, :], self.ring[:, g % NS, :], ACT.Copy).then_inc(self.rounded, 1)

    def subtract(self, dve, c, j):
        g = self.g0 + j
        dve.wait_ge(self.rounded, NS * c + (g + 1))
        self.nc.vector.tensor_tensor(self.lo[:, g % 2, :], self.ring[:, g % NS, :], self.hi[:, g % 2, :].bitcast(F32),
                                     ALU.subtract).then_inc(self.split, 1)

    def operands(self, pe, c, j):
        g = self.g0 + j
        pe.wait_ge(self.split, NS * c + (g + 1))
        return self.hi[:, g % 2, :], self.lo[:, g % 2, :]

    def load(self, eng, lo, hi):
        hi = min(hi, self.total)
        first = 0
        for src, n in self.segments:
            a, b = max(lo, first), min(hi, first + n)
            if a < b:
                cycles = (b - a) // NS if a >= NS and (b - a) // NS >= 2 else 0
                if cycles:
                    with eng.Fori(0, cycles) as i:
                        for j in range(NS):
                            eng.wait_ge(self.split, NS * i + (a + j - NS + 1))
                            eng.dma_start(self.ring[:, (a + j) % NS, :], src[NS * i + (a + j - first)])\
                               .then_inc(self.loaded[(a + j) % NS], 16)
                for g in range(a + NS * cycles, b):
                    if g >= NS:
                        eng.wait_ge(self.split, g - NS + 1)
                    eng.dma_start(self.ring[:, g % NS, :], src[g - first]).then_inc(self.loaded[g % NS], 16)
            first += n

    def load_ahead(self, eng, n):
        self.load(eng, NS if self.g0 == 0 else self.g0 + NS + 2, self.g0 + n + NS + 2)


def product(nc, out, pairs, start=True, stop=True):
    for n, ((a_hi, a_lo), (b_hi, b_lo)) in enumerate(pairs):
        nc.tensor.matmul(out, a_hi, b_hi, start=start and n == 0, stop=False)
        nc.tensor.matmul(out, a_hi, b_lo, start=False, stop=False)
        last = nc.tensor.matmul(out, a_lo, b_hi, start=False, stop=stop and n == len(pairs) - 1)
    return last


def split_activations(nc, hi, lo, x):
    first = nc.vector.tensor_copy(hi, x)
    return first, lambda: nc.vector.tensor_tensor(lo, x, hi.bitcast(F32), ALU.subtract)


def over_units(eng, n, body):
    for j in range(min(NS, n)):
        body(0, j)
    whole = n // NS
    if whole > 1:
        with eng.Fori(1, whole) as c:
            for j in range(NS):
                body(c, j)
    if whole:
        for j in range(n - whole * NS):
            body(whole, j)


def static(c):
    return isinstance(c, int)


class Chip:

    def __init__(self, ctx, nc, dram):
        def sb(name, shape, dt=F32):
            return ctx.enter_context(nc.sbuf_tensor(name, shape, dt))

        def sig(name):
            return Signal(ctx, nc, name)

        self.nc, self.dram, self.extra = nc, dram, {}
        self.bank = [ctx.enter_context(nc.psum_tensor(f"bank{b}", [P, 512], F32)) for b in range(8)]
        self.x2 = sb("x2", [P, KT, S])
        self.cols = sb("cols", [P, N_COLS])
        self.silu_c = sb("silu_c", [P, KT, 2])
        self.silu_c2 = sb("silu_c2", [P, KT])
        self.mod_sums = sb("mod_sums", [P, MOD_UNITS, 4])
        self.mods = [sb(f"mod{l}", [P, N_MOD * KT, 2]) for l in range(LAYERS)]
        self.gains = [sb(f"gain{l}", [P, 3, KT, 2]) for l in range(LAYERS)]
        self.half_gates = [sb(f"half_gate{l}", [P, 2, KT, 2]) for l in range(LAYERS)]
        self.mod2 = sb("mod2", [P, 6 * KT])
        self.gain2 = sb("gain2", [P, 2, KT])
        self.ident = sb("ident", [P, P])
        self.ones = sb("ones", [P, P])

        self.eps = sb("eps", [P, 1])

        self.squared, self.summed, self.rooted = sig("squared"), sig("summed"), sig("rooted")
        self.scaled, self.h_ready = sig("scaled"), sig("h_ready")
        self.dve_step, self.act_step, self.pool_step = sig("dve_step"), sig("act_step"), sig("pool_step")
        self.table = sig("table")
        self.product, self.copied, self.added = sig("product"), sig("copied"), sig("added")
        self.silu_done, self.gated = sig("silu_done"), sig("gated")
        self.mod_loaded = [sig("mod_loaded0"), sig("mod_loaded1")]
        self.mod_step, self.mod_summed, self.mod_diag = sig("mod_step"), sig("mod_summed"), sig("mod_diag")
        self.pool_w = sb("pool_w", [P, 2, P])
        self.pool_inv = sb("pool_inv", [P, 2, S])
        self.nmax, self.rsum = sb("nmax", [P, 2]), sb("rsum", [P, 2])
        self.gates = sb("gates", [P, 2, 24])
        self.nmax4, self.rsum4 = sb("nmax4", [P, 2, 2]), sb("rsum4", [P, 2, 2])
        self.iota = sb("iota", [P, P])
        self.split_in = sig("split_in")
        self.ffn_step = sig("ffn_step")
        self.gelu_done = sig("gelu_done")
        self.scored, self.scores_read, self.maxed = sig("scored"), sig("scores_read"), sig("maxed")
        self.exped, self.probs, self.turned = sig("exped"), sig("probs"), sig("turned")
        self.moved, self.mixed = sig("moved"), sig("mixed")

    def col(self, name, at=0, n=None):
        lo, size = COLS[name]
        return self.cols[:, lo + at:lo + (size if n is None else at + n)]

    def take(self, ctx, width, words):
        sb = lambda name, shape, dt: ctx.enter_context(self.nc.sbuf_tensor(f"{name}_{width}", shape, dt))
        self.hi, self.lo = sb("operand_hi", [P, KT, width], F32R), sb("operand_lo", [P, KT, width], F32R)
        self.arena, self.words = sb("arena", [P, words], F32), words

    def take_more(self, ctx, name, words=0, **more):
        sb = lambda n, shape, dt: ctx.enter_context(self.nc.sbuf_tensor(f"{n}_{name}", shape, dt))
        if words:
            self.extension = sb("extension", [P, words], F32)
        for buffer, (shape, dt) in more.items():
            self.extra[buffer] = sb(buffer, shape, dt)

    def part(self, at, *shape):
        n = int(np.prod(shape))
        if at < self.words:
            assert at + n <= self.words
            flat = self.arena[:, at:at + n]
        else:
            flat = self.extension[:, at - self.words:at - self.words + n]
        if len(shape) == 1:
            return flat
        if len(shape) == 2:
            return flat.rearrange("p (a b) -> p a b", b=shape[1])
        return flat.rearrange("p (a b c) -> p a b c", b=shape[1], c=shape[2])


A_X, A_H, A_RSTD = 0, 4096, 8192
A_Y = A_H
A_WORDS = A_RSTD + 1024
A_U = A_WORDS
A_V = A_U + 8192
A_BIAS = A_V + 2048
A_SC = A_BIAS + NA_H * BIAS_ROWS * GRID
A_PT = A_SC + 1024
A_POOL = A_PT + 2048
A_MIXER = A_POOL + 2048 - A_WORDS
A_MOD = A_WORDS
A_GATE = A_MOD + 2 * MOD_UNIT + 1024 + 4 * P
A_FFN = A_GATE + 2 * T2 - A_WORDS


def in_order(eng, signal, instruction):
    signal.passed(1)
    instruction.then_inc(signal.sem, 1)
    eng.wait_ge(signal.sem, signal.base)


class Norm:
    def __init__(self, chip, x, h, root, rstd, gain, shift, groups, width, split=True):
        self.chip, self.x, self.h, self.root, self.rstd = chip, x, h, root, rstd
        self.gain, self.shift, self.groups, self.t = gain, shift, groups, width
        self.split = split

    def scalar(self, act):
        c, nc, t = self.chip, self.chip.nc, self.t
        for kt in range(KT):
            nc.scalar.activation(self.h[:, kt, 0:t], self.x[:, kt, 0:t], ACT.Square).then_inc(c.squared.sem, 1)
        act.wait_ge(c.summed.sem, c.summed.at(1))
        nc.scalar.activation(self.root[:, 0:t], c.bank[7][:, 0:t], ACT.Sqrt, bias=self.chip.eps[:, 0:1], scale=1.0 / D)\
            .then_inc(c.rooted.sem, 1)
        for kt in range(KT):
            act.wait_ge(c.scaled.sem, c.scaled.at(kt + 1))
            for g, (lo, hi) in enumerate(self.groups):
                shift = 0.0 if self.shift is None else self.shift(kt, g)
                last = nc.scalar.activation(self.h[:, kt, lo:hi], self.h[:, kt, lo:hi], ACT.Identity,
                                            bias=shift, scale=self.gain(kt, g))
            last.then_inc(c.h_ready.sem, 1)

    def tensor(self, pe):
        c, nc, t = self.chip, self.chip.nc, self.t
        for kt in range(KT):
            pe.wait_ge(c.squared.sem, c.squared.at(kt + 1))
            last = nc.tensor.matmul(c.bank[7][:, 0:t], c.ones[:, :], self.h[:, kt, 0:t],
                                    start=(kt == 0), stop=(kt == KT - 1))
        last.then_inc(c.summed.sem, 1)

    def vector(self, dve):
        c, nc, t = self.chip, self.chip.nc, self.t
        dve.wait_ge(c.rooted.sem, c.rooted.at(1))
        in_order(dve, c.dve_step, nc.vector.reciprocal(self.rstd[:, 0:t], self.root[:, 0:t]))
        for kt in range(KT):
            nc.vector.tensor_tensor(self.h[:, kt, 0:t], self.x[:, kt, 0:t], self.rstd[:, 0:t], ALU.mult)\
                .then_inc(c.scaled.sem, 1)
            if self.split and kt:
                self.parts(dve, kt - 1)
        if self.split:
            self.parts(dve, KT - 1)

    def parts(self, dve, kt):
        c, nc, t = self.chip, self.chip.nc, self.t
        dve.wait_ge(c.h_ready.sem, c.h_ready.at(kt + 1))
        first, rest = split_activations(nc, c.hi[:, kt, 0:t], c.lo[:, kt, 0:t], self.h[:, kt, 0:t])
        in_order(dve, c.dve_step, first)
        rest().then_inc(c.split_in.sem, 1)

    def end(self):
        c = self.chip
        c.squared.passed(KT)
        c.summed.passed(1)
        c.rooted.passed(1)
        c.scaled.passed(KT)
        c.h_ready.passed(KT)
        if self.split:
            c.split_in.passed(KT)


def stage_setup(chip, stream):
    nc, d = chip.nc, chip.dram
    x = chip.part(A_X, KT, T2)
    with nc.Block() as block:
        @block.sync
        def _(sp):
            sp.dma_start(chip.cols[:, :], d["cols"]).then_inc(chip.table.sem, 16)
            sp.dma_start(x, d["x"]).then_inc(chip.table.sem, 16)
            stream.load(sp, 0, NS)
            sp.wait_ge(chip.table.sem, 32)

        @block.gpsimd
        def _(pool):
            nc.gpsimd.memset(chip.ones[:, :], 1.0)
            nc.gpsimd.memset(chip.eps[:, :], EPS)
            in_order(pool, chip.pool_step, nc.gpsimd.memset(chip.ident[:, :], 0.0))
            in_order(pool, chip.pool_step, nc.gpsimd.affine_select(
                out=chip.ident[:, :], in_=chip.ident[:, :], compare_op=ALU.not_equal, fill=1.0, base=0,
                pattern=[[-1, P]], channel_multiplier=1))

        @block.scalar
        def _(act):
            act.wait_ge(chip.table.sem, 32)
            nc.scalar.activation(chip.silu_c[:, :, :].rearrange("p a b -> p (a b)"), chip.col("cc"), ACT.Silu)\
                .then_inc(chip.act_step.sem, 1)
            nc.scalar.activation(chip.silu_c2[:, :], chip.col("c2"), ACT.Silu).then_inc(chip.act_step.sem, 1)
            act.wait_ge(chip.act_step.sem, 2)
            for j in range(2):
                stream.round(act, 0, j)

        @block.vector
        def _(dve):
            for j in range(2):
                stream.subtract(dve, 0, j)
    chip.table.passed(32)
    chip.act_step.passed(2)


class Modulation:

    def __init__(self, chip, first, n, groups, at=A_MOD):
        self.chip, self.first, self.n, self.groups = chip, first, n, groups
        self.steps = KT * groups
        self.w = chip.part(at, 2, MOD_UNIT)
        self.acc = chip.part(at + 2 * MOD_UNIT, 2, 512)
        self.diag = chip.part(at + 2 * MOD_UNIT + 1024, 2 * groups, P)

    def load(self, eng):
        c = self.chip
        for l in range(2):
            eng.dma_start(self.w[:, l, :], c.dram["w_mods"][self.first + l]).then_inc(c.mod_loaded[l].sem, 16)
        with eng.Fori(1, self.n // 2) as i:
            for j in range(2):
                eng.wait_ge(c.mod_step.sem, c.mod_step.at(2 * self.steps * i + self.steps * (j - 1)))
                eng.dma_start(self.w[:, j, :], c.dram["w_mods"][2 * i + (self.first + j)]).then_inc(c.mod_loaded[j].sem, 16)

    def accumulate(self, dve, i, j, l, lo=0, hi=KT):
        c, nc = self.chip, self.chip.nc
        if lo == 0:
            dve.wait_ge(c.mod_loaded[j].sem, c.mod_loaded[j].at(16 * i + 16))
        for kt in range(lo, hi):
            for g in range(self.groups):
                w, acc = self.w[:, j, kt * 256:(kt + 1) * 256], self.acc[:, j, g * 256:(g + 1) * 256]
                scale = c.silu_c[:, kt, g:g + 1] if self.groups == 2 else c.silu_c2[:, kt:kt + 1]
                if kt == 0:
                    ins = nc.vector.tensor_scalar(acc, w, scale, None, ALU.mult)
                else:
                    dve.wait_ge(c.mod_step.sem, c.mod_step.at(self.steps * l + ((kt - 1) * self.groups + g + 1)))
                    ins = nc.vector.scalar_tensor_tensor(acc, w, scale, acc, ALU.mult, ALU.add)
                ins.then_inc(c.mod_step.sem, 1)

    def sum(self, pe, j, l):
        c, nc = self.chip, self.chip.nc
        pe.wait_ge(c.mod_step.sem, c.mod_step.at(self.steps * l + self.steps))
        n = 256 * self.groups
        nc.tensor.matmul(c.bank[6 + j][:, 0:n], c.ones[:, :], self.acc[:, j, 0:n], start=True, stop=True)\
            .then_inc(c.mod_summed.sem, 1)

    def keep(self, dve, j, l):
        c, nc = self.chip, self.chip.nc
        blocks = 2 * self.groups
        if not (static(l) and l == 0):
            dve.wait_ge(c.mod_diag.sem, c.mod_diag.at(2 * l))
        dve.wait_ge(c.mod_summed.sem, c.mod_summed.at(l + 1))
        nc.vector.tensor_tensor(self.diag, c.bank[6 + j][:, 0:blocks * P].rearrange("p (b m) -> p b m", m=P),
                                c.ident[:, :].unsqueeze(1).to_broadcast([P, blocks, P]), ALU.mult).then_inc(c.mod_diag.sem, 1)
        dve.wait_ge(c.mod_diag.sem, c.mod_diag.at(2 * l + 1))
        nc.vector.tensor_reduce(c.mod_sums[:, l + self.first, 0:blocks], self.diag, AX.X, ALU.add)\
            .then_inc(c.mod_diag.sem, 1)

    def end(self):
        c = self.chip
        for s in c.mod_loaded:
            s.passed(16 * (self.n // 2))
        c.mod_step.passed(self.steps * self.n)
        c.mod_summed.passed(self.n)
        c.mod_diag.passed(2 * self.n)


def finish_mod(chip, dve, layer, lo, hi):
    nc = chip.nc
    mod, gain, half_gate = chip.mods[layer], chip.gains[layer], chip.half_gates[layer]
    u0 = layer * LAYER_UNITS
    for b in range(2):
        src = chip.mod_sums[:, u0 + lo * KT // 2:u0 + hi * KT // 2, :].rearrange("p u (g b) -> p u g b", b=2)[:, :, :, b]
        bias = chip.col("b_mod", layer * N_MOD * KT + lo * KT + b, (hi - lo) * KT - b)[:, ::2]
        last = nc.vector.tensor_tensor(mod[:, lo * KT + b:hi * KT:2, :], src,
                                       bias.unsqueeze(2).to_broadcast([P, (hi - lo) * KT // 2, 2]), ALU.add)
    in_order(dve, chip.dve_step, last)
    for i in range(lo // 3, hi // 3):
        g = chip.col("norm_g", (layer * 3 + i) * KT, KT).unsqueeze(2).to_broadcast([P, KT, 2])
        last = nc.vector.scalar_tensor_tensor(gain[:, i, :, :], mod[:, (3 * i + 1) * KT:(3 * i + 2) * KT, :],
                                              1.0, g, ALU.add, ALU.mult)
        if i != 1:
            last = nc.vector.tensor_scalar(half_gate[:, i // 2, :, :], mod[:, (3 * i + 2) * KT:(3 * i + 3) * KT, :],
                                           0.5, None, ALU.mult)
    in_order(dve, chip.dve_step, last)


def finish_mod2(chip, dve):
    nc = chip.nc
    src = chip.mod_sums[:, LAYERS * LAYER_UNITS:MOD_UNITS, 0:2]
    in_order(dve, chip.dve_step, nc.vector.tensor_tensor(
        chip.mod2[:, :].rearrange("p (u b) -> p u b", b=2), src, chip.col("b_ada").rearrange("p (u b) -> p u b", b=2), ALU.add))
    for i, g in enumerate(("g_mix", "g_ffn")):
        in_order(dve, chip.dve_step, nc.vector.scalar_tensor_tensor(
            chip.gain2[:, i, :], chip.mod2[:, (3 * i + 1) * KT:(3 * i + 2) * KT], 1.0, chip.col(g), ALU.add, ALU.mult))


def stage_first_mod(chip):
    work = Modulation(chip, 0, 3 * KT // 2, 2)
    with chip.nc.Block() as block:
        block.gpsimd(work.load)

        @block.tensor
        def _(pe):
            for l in range(work.n):
                work.sum(pe, l % 2, l)

        @block.vector
        def _(dve):
            for l in range(work.n):
                work.accumulate(dve, l // 2, l % 2, l)
                if l:
                    work.keep(dve, (l - 1) % 2, l - 1)
            work.keep(dve, (work.n - 1) % 2, work.n - 1)
            dve.wait_ge(chip.mod_diag.sem, chip.mod_diag.at(2 * work.n))
            finish_mod(chip, dve, 0, 0, 3)
    work.end()


def norm1(chip, layer, i, width):
    groups = [(0, S), (S, T2)][:width // S]
    return Norm(chip, chip.part(A_X, KT, T2), chip.part(A_H, KT, T2), chip.part(A_RSTD + 512, 512), chip.part(A_RSTD, 512),
                lambda kt, g: chip.gains[layer][:, i, kt, g:g + 1],
                lambda kt, g: chip.mods[layer][:, 3 * i * KT + kt, g:g + 1],
                groups, width)


def take_for_ffn(chip, ctx, name):
    part = ([P, max(HIDDEN), T2], F32R)
    chip.take_more(ctx, name, A_FFN, hidden_hi=part, hidden_lo=part)


def stage_ffn(chip, stream, layer, which, width, work=None, finish=None):
    nc, t = chip.nc, width
    norm = norm1(chip, layer, 2 * which, width)
    x = chip.part(A_X, KT, T2)
    hid_hi, hid_lo = chip.extra["hidden_hi"], chip.extra["hidden_lo"]
    gate_buf = chip.part(A_GATE, 2, T2)
    beside = {None: (0, 0, 0), FT + 2: (0, 0, 2), FT + KT: (3, 3, 2)}[work.n if work else None]
    parts, u = [], 0
    for i, n in enumerate(HIDDEN):
        parts.append((sum(HIDDEN[:i]), n, u, i * KT, sum(beside[:i]), beside[i]))
        u += 2 * n + KT

    with nc.Block() as block:
        @block.sync
        def _(sp):
            stream.load_ahead(sp, FFN_UNITS)

        if work:
            block.gpsimd(work.load)

        @block.tensor
        def _(pe):
            norm.tensor(pe)
            pe.wait_ge(chip.split_in.sem, chip.split_in.at(KT))
            for n0, nh, u0, r0, extra, more in parts:
                def up(c, j):
                    n, half = 2 * c + (n0 + j // 2), j % 2
                    if half == 0 and not (static(c) and n < 2):
                        pe.wait_ge(chip.gated.sem, chip.gated.at(n - 1))
                    w_hi, w_lo = stream.operands(pe, c, u0 + j)
                    product(nc, chip.bank[2 * (j // 2) + half][:, 0:t],
                            [((w_hi[:, kt * P:(kt + 1) * P], w_lo[:, kt * P:(kt + 1) * P]),
                              (chip.hi[:, kt, 0:t], chip.lo[:, kt, 0:t])) for kt in range(KT)]).then_inc(stream.used, 1)
                    l = n + extra
                    if work and half and not (static(c) and l == 0):
                        work.sum(pe, (n0 + extra + j // 2 - 1) % 2, l - 1)
                over_units(pe, 2 * nh, up)
                pe.wait_ge(chip.gated.sem, chip.gated.at(n0 + nh))
                for n in range(KT):
                    r = r0 + n
                    if r >= 2:
                        pe.wait_ge(chip.added.sem, chip.added.at(r - 1))
                    w_hi, w_lo = stream.operands(pe, 0, u0 + 2 * nh + n)
                    product(nc, chip.bank[4 + n % 2][:, 0:t],
                            [((w_hi[:, kt * P:(kt + 1) * P], w_lo[:, kt * P:(kt + 1) * P]),
                              (hid_hi[:, kt, 0:t], hid_lo[:, kt, 0:t])) for kt in range(nh)]).then_inc(stream.used, 1)
                    if n % 3 == 1 and n // 3 < more:
                        l = n0 + nh + extra + n // 3
                        work.sum(pe, (l - 1) % 2, l - 1)
            if work:
                work.sum(pe, (work.n - 1) % 2, work.n - 1)

        @block.scalar
        def _(act):
            norm.scalar(act)
            for n0, nh, u0, r0, extra, more in parts:
                def silu(c, j):
                    if j % 2 == 0:
                        act.wait_ge(stream.used, stream.used_at(NS * c + (u0 + j)))
                        nc.scalar.activation(gate_buf[:, j // 2, 0:t], chip.bank[2 * (j // 2)][:, 0:t], ACT.Silu)\
                            .then_inc(chip.silu_done.sem, 1)
                    stream.round(act, c, u0 + j + 2)
                over_units(act, 2 * nh, silu)
                for n in range(KT):
                    stream.round(act, 0, u0 + 2 * nh + n + 2)

        @block.vector
        def _(dve):
            norm.vector(dve)
            for n0, nh, u0, r0, extra, more in parts:
                def gate(c, j):
                    i = j // 2
                    n = 2 * c + (n0 + i)
                    if j % 2:
                        g, hi, lo = gate_buf[:, i, 0:t], hid_hi[:, 2 * c + i, 0:t], hid_lo[:, 2 * c + i, 0:t]
                        dve.wait_ge(chip.silu_done.sem, chip.silu_done.at(n + 1))
                        dve.wait_ge(stream.used, stream.used_at(NS * c + (u0 + j)))
                        nc.vector.tensor_tensor(g, g, chip.bank[2 * i + 1][:, 0:t], ALU.mult).then_inc(chip.ffn_step.sem, 1)
                        dve.wait_ge(chip.ffn_step.sem, chip.ffn_step.at(2 * n + 1))
                        first, rest = split_activations(nc, hi, lo, g)
                        first.then_inc(chip.ffn_step.sem, 1)
                        dve.wait_ge(chip.ffn_step.sem, chip.ffn_step.at(2 * n + 2))
                        rest().then_inc(chip.gated.sem, 1)
                    stream.subtract(dve, c, u0 + j + 2)
                    if work:
                        e, l = n0 + extra + i, n + extra
                        work.accumulate(dve, c + e // 2, e % 2, l, KT // 2 * (j % 2), KT // 2 * (j % 2 + 1))
                        if j % 2 and not (static(c) and l == 0):
                            work.keep(dve, (e - 1) % 2, l - 1)
                over_units(dve, 2 * nh, gate)
                for n in range(KT):
                    r = r0 + n
                    dve.wait_ge(stream.used, stream.used_at(u0 + 2 * nh + n))
                    for g, (lo, hi) in enumerate(norm.groups):
                        last = nc.vector.scalar_tensor_tensor(x[:, n, lo:hi], chip.bank[4 + n % 2][:, lo:hi],
                                                              chip.half_gates[layer][:, which, n, g:g + 1], x[:, n, lo:hi],
                                                              ALU.mult, ALU.add)
                    last.then_inc(chip.added.sem, 1)
                    stream.subtract(dve, 0, u0 + 2 * nh + n + 2)
                    if n % 3 < 2 and n // 3 < more:
                        l = n0 + nh + extra + n // 3
                        work.accumulate(dve, l // 2, l % 2, l, KT // 2 * (n % 3), KT // 2 * (n % 3 + 1))
                        if n % 3 == 1:
                            work.keep(dve, (l - 1) % 2, l - 1)
            if work:
                work.keep(dve, (work.n - 1) % 2, work.n - 1)
                dve.wait_ge(chip.mod_diag.sem, chip.mod_diag.at(2 * work.n))
                finish(dve)
    if work:
        work.end()
    norm.end()
    chip.ffn_step.passed(2 * FT)
    chip.silu_done.passed(FT)
    chip.gated.passed(FT)
    chip.added.passed(3 * KT)
    stream.g0 += FFN_UNITS


def stage_mix_in(chip, stream, layer, last):
    nc, d = chip.nc, chip.dram
    norm = norm1(chip, layer, 1, T2)
    hi, lo = chip.hi, chip.lo
    u, v = chip.part(A_U, 16, T2), chip.part(A_V, 4, 512)
    bias = chip.part(A_BIAS, NA_H * BIAS_ROWS * GRID)
    width = [S if last and n < CH_K else T2 for n in range(16)]
    with nc.Block() as block:
        @block.sync
        def _(sp):
            sp.dma_start(bias, d["rel_bias"][layer]).then_inc(chip.table.sem, 16)
            sp.dma_start(chip.pool_w[:, :, :], d["pool_w"][layer]).then_inc(chip.table.sem, 16)
            sp.dma_start(chip.pool_inv[:, :, :], d["pool_inv"]).then_inc(chip.table.sem, 16)
            stream.load_ahead(sp, 20)

        @block.gpsimd
        def _(pool):
            pool.wait_ge(chip.table.sem, chip.table.at(48))
            for half in range(2):
                b = bias[half * GRID:(half + 1) * GRID, :].rearrange("p (r k) -> p r k", k=GRID)
                lo, hi = b[:, :, 0:GRID - 16], b[:, :, 16:GRID]
                in_order(pool, chip.pool_step, nc.gpsimd.affine_select(
                    out=lo, in_=lo, compare_op=ALU.is_ge, fill=NEG, base=8,
                    pattern=[[0, NA_H * BIAS_ROWS], [1, GRID - 16]], channel_multiplier=-1))
                in_order(pool, chip.pool_step, nc.gpsimd.affine_select(
                    out=hi, in_=hi, compare_op=ALU.is_ge, fill=NEG, base=7 - 16,
                    pattern=[[0, NA_H * BIAS_ROWS], [-1, GRID - 16]], channel_multiplier=1))

        @block.tensor
        def _(pe):
            norm.tensor(pe)
            pe.wait_ge(chip.split_in.sem, chip.split_in.at(KT))
            for n in range(16):
                if n >= 4:
                    pe.wait_ge(chip.copied.sem, chip.copied.at(n - 3))
                w_hi, w_lo = stream.operands(pe, 0, n)
                t = width[n]
                product(nc, chip.bank[n % 4][:, 0:t],
                        [((w_hi[:, kt * P:(kt + 1) * P], w_lo[:, kt * P:(kt + 1) * P]), (hi[:, kt, 0:t], lo[:, kt, 0:t]))
                         for kt in range(KT)]).then_inc(stream.used, 1)
            for n in range(4):
                w_hi, w_lo = stream.operands(pe, 0, 16 + n)
                for tt in range(4):
                    q = slice(tt * P, (tt + 1) * P)
                    mm = product(nc, chip.bank[4 + tt][:, :],
                                 [((hi[:, 2 * n + i, q], lo[:, 2 * n + i, q]),
                                   (w_hi[:, i * 512:(i + 1) * 512], w_lo[:, i * 512:(i + 1) * 512])) for i in range(2)],
                                 start=(n == 0), stop=(n == 3))
                mm.then_inc(stream.used, 1)

        @block.scalar
        def _(act):
            norm.scalar(act)
            for n in range(16):
                act.wait_ge(stream.used, stream.used_at(n))
                nc.scalar.activation(u[:, n, 0:width[n]], chip.bank[n % 4][:, 0:width[n]], ACT.Copy)\
                    .then_inc(chip.copied.sem, 1)
                stream.round(act, 0, n + 2)
            for n in range(4):
                stream.round(act, 0, 18 + n)
            act.wait_ge(stream.used, stream.used_at(19))
            for tt in range(4):
                nc.scalar.activation(v[:, tt, :], chip.bank[4 + tt][:, :], ACT.Copy)

        @block.vector
        def _(dve):
            norm.vector(dve)
            for n in range(20):
                stream.subtract(dve, 0, n + 2)
    norm.end()
    chip.table.passed(48)
    chip.copied.passed(16)
    stream.g0 += 20


def stage_mix(chip, stream, layer, last):
    nc = chip.nc
    u, v, y = chip.part(A_U, 16, T2), chip.part(A_V, 4, 512), chip.part(A_Y, KT, T2)
    bias = chip.part(A_BIAS, NA_H, BIAS_ROWS * GRID)
    sc, pt = chip.part(A_SC, 2, 512), chip.part(A_PT, 2, 4, S)
    ng = 1 if last else 2
    t = ng * S
    items = [(g, h, qt) for g in range(ng) for h in range(NA_H) for qt in range(2)]
    keys = lambda g: (0, T2) if g == 0 else (S, T2)

    with nc.Block() as block:
        @block.sync
        def _(sp):
            pass

        @block.gpsimd
        def _(pool):
            eng = nc.gpsimd
            step = lambda ins: in_order(pool, chip.pool_step, ins)
            z = chip.part(A_POOL, ng, S + 2)
            acc, tmp = chip.part(A_POOL + 544, ng, S), chip.part(A_POOL + 1088, ng, S)
            step(eng.memset(z, 0.0))
            for b in range(2):
                uu = lambda n: u[:, n + b, 0:t].rearrange("p (g s) -> p g s", s=S)
                w = lambda k: chip.col("conv_w", (layer * 3 + k) * 2 + b, 1)
                step(eng.tensor_tensor(z[:, :, 1:S + 1], uu(CH_C), uu(0), ALU.mult))
                step(eng.tensor_scalar(acc, z[:, :, 0:S], w(0), None, ALU.mult))
                for k in (1, 2):
                    step(eng.tensor_scalar(tmp, z[:, :, k:k + S], w(k), None, ALU.mult))
                    step(eng.tensor_tensor(acc, acc, tmp, ALU.add))
                step(eng.tensor_tensor(y[:, b, 0:t].rearrange("p (g s) -> p g s", s=S), acc, uu(CH_B), ALU.mult))
            wide = S + 16
            a, c = chip.part(A_POOL, ng, wide), chip.part(A_POOL + 544, ng, wide)
            for b in range(2):
                vv = u[:, CH_POOL + b, 0:t].rearrange("p (g s) -> p g s", s=S)
                out = y[:, 2 + b, 0:t].rearrange("p (g s) -> p g s", s=S)
                step(eng.memset(a, 0.0))
                step(eng.tensor_copy(a[:, :, 8:8 + S], vv))
                src, dst = a, c
                for n in range(2 + 2 * b):
                    gap, at = 1 << n, (2 << n) - 1
                    step(eng.tensor_tensor(dst[:, :, at:wide], src[:, :, at:wide], src[:, :, at - gap:wide - gap], ALU.add))
                    src, dst = dst, src
                    if n >= 2 * b:
                        half, lo = n - 2 * b, 8 + gap - 1
                        q = slice(64 * half, 64 * half + 64)
                        inv = chip.pool_inv[q, b, :].unsqueeze(1).to_broadcast([64, ng, S])
                        step(eng.tensor_tensor(out[q, :, :], src[q, :, lo:lo + S], inv, ALU.mult))
                step(eng.tensor_tensor(out, out, vv, ALU.subtract))
            eng.sem_inc(chip.mixed.sem, 1)

        @block.tensor
        def _(pe):
            def scores(w):
                g, h, qt = items[w]
                lo, hi = keys(g)
                po, q0 = 64 * (h % 2), g * S + qt * P
                if w >= 2:
                    pe.wait_ge(chip.scores_read.sem, chip.scores_read.at(w - 1))
                nc.tensor.matmul(chip.bank[w % 2][:, 0:hi - lo], u[po:po + 64, CH_Q + h // 2, q0:q0 + P],
                                 u[po:po + 64, CH_K + h // 2, lo:hi], start=True, stop=True)\
                    .then_inc(chip.scored.sem, 1)

            def transposes(w):
                g, h, qt = items[w]
                pe.wait_ge(chip.probs.sem, chip.probs.at(w + 1))
                if w >= 2:
                    pe.wait_ge(chip.copied.sem, chip.copied.at(w - 1))
                for kt in range((keys(g)[1] - keys(g)[0]) // P):
                    mm = nc.tensor.transpose(chip.bank[2 + w % 2][:, kt * P:(kt + 1) * P],
                                             sc[:, w % 2, kt * P:(kt + 1) * P], chip.ident[:, :])
                mm.then_inc(chip.turned.sem, 1)

            def values(n):
                g, h, _ = items[2 * n]
                po = 64 * (h % 2)
                pe.wait_ge(chip.copied.sem, chip.copied.at(2 * n + 2))
                if n >= 2:
                    pe.wait_ge(chip.moved.sem, chip.moved.at(n - 1))
                nkt = (keys(g)[1] - keys(g)[0]) // P
                for kt in range(nkt):
                    mm = nc.tensor.matmul(chip.bank[4 + n % 2][po:po + 64, 0:S],
                                          v[:, kt + 4 - nkt, h * DH:(h + 1) * DH], pt[:, n % 2, kt, :],
                                          start=(kt == 0), stop=(kt == nkt - 1))
                mm.then_inc(chip.product.sem, 1)

            scores(0)
            scores(1)
            for w in range(len(items)):
                transposes(w)
                if w + 2 < len(items):
                    scores(w + 2)
                if w >= 2 and w % 2 == 0:
                    values(w // 2 - 1)
            values(len(items) // 2 - 1)
            pe.wait_ge(chip.mixed.sem, chip.mixed.at(1))
            for b in range(2):
                mm = nc.tensor.matmul(chip.bank[6 + b][:, 0:t], chip.pool_w[:, b, :], y[:, 2 + b, 0:t],
                                      start=True, stop=True)
            mm.then_inc(chip.product.sem, 1)

        @block.scalar
        def _(act):
            def exps(w):
                g, h, qt = items[w]
                n = keys(g)[1] - keys(g)[0]
                act.wait_ge(chip.maxed.sem, chip.maxed.at(w + 1))
                nc.scalar.activation(sc[:, w % 2, 0:n], sc[:, w % 2, 0:n], ACT.Exp, bias=chip.nmax[:, w % 2:w % 2 + 1],
                                     accum_out=chip.rsum[:, w % 2:w % 2 + 1]).then_inc(chip.exped.sem, 1)

            def copies(w):
                g, h, qt = items[w]
                nkt = (keys(g)[1] - keys(g)[0]) // P
                n = w // 2
                act.wait_ge(chip.turned.sem, chip.turned.at(w + 1))
                if n >= 2:
                    act.wait_ge(chip.product.sem, chip.product.at(n - 1))
                nc.scalar.activation(pt[:, n % 2, 0:nkt, qt * P:(qt + 1) * P],
                                     chip.bank[2 + w % 2][:, 0:nkt * P].rearrange("p (k q) -> p k q", q=P), ACT.Copy)\
                    .then_inc(chip.copied.sem, 1)

            def move(n):
                g, h, _ = items[2 * n]
                po = 64 * (h % 2)
                act.wait_ge(chip.product.sem, chip.product.at(n + 1))
                nc.scalar.activation(y[po:po + 64, 4 + h // 2, g * S:(g + 1) * S], chip.bank[4 + n % 2][po:po + 64, 0:S],
                                     ACT.Copy).then_inc(chip.moved.sem, 1)

            exps(0)
            for w in range(len(items)):
                if w + 1 < len(items):
                    exps(w + 1)
                copies(w)
                if w >= 3 and w % 2 == 1:
                    move(w // 2 - 1)
            move(len(items) // 2 - 1)
            act.wait_ge(chip.product.sem, chip.product.at(len(items) // 2 + 1))
            for b in range(2):
                nc.scalar.activation(y[:, 2 + b, 0:t], chip.bank[6 + b][:, 0:t], ACT.Copy,
                                     scale=chip.col("pool_scale", layer * 2 + b, 1))

        @block.vector
        def _(dve):
            def scale(w):
                g, h, qt = items[w]
                n = keys(g)[1] - keys(g)[0]
                s, bank = sc[:, w % 2, :], chip.bank[w % 2]
                dve.wait_ge(chip.scored.sem, chip.scored.at(w + 1))
                if w >= 2:
                    dve.wait_ge(chip.turned.sem, chip.turned.at(w - 1))
                if g == 0:
                    r0 = (2 - 2 * qt) * GRID
                    nc.vector.scalar_tensor_tensor(s[:, 0:S], bank[:, 0:S], 0.125, bias[:, h, r0:r0 + S], ALU.mult, ALU.add)
                    nc.vector.tensor_scalar(s[:, S:T2], bank[:, S:T2], 0.125, None, ALU.mult)\
                        .then_inc(chip.scores_read.sem, 1)
                else:
                    nc.vector.tensor_scalar(s[:, 0:n], bank[:, 0:n], 0.125, None, ALU.mult)\
                        .then_inc(chip.scores_read.sem, 1)
                dve.wait_ge(chip.scores_read.sem, chip.scores_read.at(w + 1))
                nc.vector.tensor_reduce(chip.nmax[:, w % 2:w % 2 + 1], s[:, 0:n], AX.X, ALU.max, negate=True)\
                    .then_inc(chip.maxed.sem, 1)

            def normalise(w):
                g, h, qt = items[w]
                n = keys(g)[1] - keys(g)[0]
                dve.wait_ge(chip.exped.sem, chip.exped.at(w + 1))
                r = chip.rsum[:, w % 2:w % 2 + 1]
                in_order(dve, chip.dve_step, nc.vector.reciprocal(r, r))
                nc.vector.tensor_scalar(sc[:, w % 2, 0:n], sc[:, w % 2, 0:n], r, None, ALU.mult).then_inc(chip.probs.sem, 1)

            scale(0)
            for w in range(len(items)):
                if w + 1 < len(items):
                    scale(w + 1)
                normalise(w)
    n = len(items)
    for sig in (chip.scored, chip.scores_read, chip.maxed, chip.exped, chip.probs, chip.turned, chip.copied):
        sig.passed(n)
    chip.product.passed(n // 2 + 1)
    chip.moved.passed(n // 2)
    chip.mixed.passed(1)


def stage_add_product(chip, stream, x, y, gate, groups):
    nc, t = chip.nc, groups[-1][1]
    with nc.Block() as block:
        @block.sync
        def _(sp):
            stream.load_ahead(sp, KT)

        @block.tensor
        def _(pe):
            for n in range(KT):
                if n >= 4:
                    pe.wait_ge(chip.added.sem, chip.added.at(n - 3))
                w_hi, w_lo = stream.operands(pe, 0, n)
                for kt in range(KT):
                    if n == 0:
                        pe.wait_ge(chip.split_in.sem, chip.split_in.at(kt + 1))
                    mm = product(nc, chip.bank[n % 4][:, 0:t],
                                 [((w_hi[:, kt * P:(kt + 1) * P], w_lo[:, kt * P:(kt + 1) * P]),
                                   (chip.hi[:, kt, 0:t], chip.lo[:, kt, 0:t]))], start=(kt == 0), stop=(kt == KT - 1))
                mm.then_inc(stream.used, 1)

        @block.scalar
        def _(act):
            for kt in range(KT):
                nc.scalar.activation(chip.hi[:, kt, 0:t], y[:, kt, 0:t], ACT.Copy).then_inc(chip.copied.sem, 1)
            for n in range(KT):
                stream.round(act, 0, n + 2)

        @block.vector
        def _(dve):
            for kt in range(KT):
                dve.wait_ge(chip.copied.sem, chip.copied.at(kt + 1))
                nc.vector.tensor_tensor(chip.lo[:, kt, 0:t], y[:, kt, 0:t], chip.hi[:, kt, 0:t].bitcast(F32), ALU.subtract)\
                    .then_inc(chip.split_in.sem, 1)
            for n in range(KT):
                dve.wait_ge(stream.used, stream.used_at(n))
                for g, (lo, hi) in enumerate(groups):
                    last = nc.vector.scalar_tensor_tensor(x[:, n, lo:hi], chip.bank[n % 4][:, lo:hi], gate(n, g),
                                                          x[:, n, lo:hi], ALU.mult, ALU.add)
                last.then_inc(chip.added.sem, 1)
                stream.subtract(dve, 0, n + 2)
    chip.copied.passed(KT)
    chip.split_in.passed(KT)
    chip.added.passed(KT)
    stream.g0 += KT


B_U, B_TAB = 0, 5120
B_RV = B_TAB + N_TAB
B_VS = B_RV + 1024
B_Y = B_VS + 512
B_SR = B_Y + 2048
B_RY, B_T1, B_T2 = B_SR + 768, B_SR + 768 + 1024, B_SR + 768 + 2048
B_W1 = B_T2 + 1024
B_W2 = B_W1 + 8192
B_K2 = B_W2 + 256
B_BLK = B_K2 + 1024
B_HID = B_BLK + 960
B_SC, B_PTS, B_PTC = B_HID + 128, B_HID + 128 + 1024, B_HID + 128 + 1024 + 1536
B_C = B_PTC + 2048
E_Q, E_SC, E_SC2, E_V, E_I, E_IF, E_TV, E_TJ = 0, 4096, 8192, 8704, 9216, 9728, 10240, 10496
E_J, E_JF, E_EQ, E_N, E_W, E_CAND = 10752, 11264, 11776, 13824, 14592, 15104
E_KEYS = 20480
E_WORK = 256 * 128
E_SLOT = E_WORK
E_HOT = E_WORK + 3 * 256
B_WORDS = E_HOT + 1024


def stage_final_norm(chip):
    norm = Norm(chip, chip.part(A_X, KT, T2), chip.x2, chip.part(A_RSTD + 512, 512), chip.part(A_RSTD, 512),
                lambda kt, g: chip.col("final_g", kt, 1), None, [(0, S)], S, split=False)
    with chip.nc.Block() as block:
        block.tensor(norm.tensor)
        block.scalar(norm.scalar)
        block.vector(norm.vector)
    norm.end()


def norm2(chip, i, at, scratch):
    return Norm(chip, chip.x2, chip.part(scratch, KT, S), chip.part(at, S), chip.part(at + S, S),
                lambda kt, g: chip.gain2[:, i, kt:kt + 1], lambda kt, g: chip.mod2[:, 3 * i * KT + kt:3 * i * KT + kt + 1],
                [(0, S)], S)


def stage_proj(chip, stream):
    nc, d = chip.nc, chip.dram
    norm = norm2(chip, 0, B_T2, B_Y)
    hi, lo, u = chip.hi, chip.lo, chip.part(B_U, N_PROJ, S)
    rv, vs = chip.part(B_RV, 2, 512), chip.part(B_VS, 2, S)
    with nc.Block() as block:
        @block.sync
        def _(sp):
            sp.dma_start(chip.part(B_TAB, N_TAB), d["tables"]).then_inc(chip.table.sem, 16)
            for n, k in enumerate("kv"):
                sp.dma_start(chip.part(B_W1 + 4096 * n, 16, 256), d[f"cmp_{k}1"]).then_inc(chip.table.sem, 16)
                sp.dma_start(chip.part(B_W2 + 128 * n, 2, 64), d[f"cmp_{k}2"]).then_inc(chip.table.sem, 16)
            stream.load_ahead(sp, 28)
            sp.wait_ge(chip.table.sem, chip.table.at(80))

        @block.tensor
        def _(pe):
            norm.tensor(pe)
            pe.wait_ge(chip.split_in.sem, chip.split_in.at(KT))
            for n in range(N_PROJ):
                k = n // 2
                if n >= 4 and n % 2 == 0:
                    pe.wait_ge(chip.copied.sem, chip.copied.at(k - 1))
                w_hi, w_lo = stream.operands(pe, 0, n)
                product(nc, chip.bank[k % 2][:, n % 2 * S:(n % 2 + 1) * S],
                        [((w_hi[:, kt * P:(kt + 1) * P], w_lo[:, kt * P:(kt + 1) * P]), (hi[:, kt, :], lo[:, kt, :]))
                         for kt in range(KT)]).then_inc(stream.used, 1)
            for i, width in enumerate((512, 2 * P + 24)):
                for n in range(4):
                    w_hi, w_lo = stream.operands(pe, 0, N_PROJ + 4 * i + n)
                    for tt in range(2):
                        q = slice(tt * P, (tt + 1) * P)
                        mm = product(nc, chip.bank[2 + 2 * i + tt][:, 0:width],
                                     [((hi[:, 2 * n + m, q], lo[:, 2 * n + m, q]),
                                       (w_hi[:, m * 512:m * 512 + width], w_lo[:, m * 512:m * 512 + width])) for m in range(2)],
                                     start=(n == 0), stop=(n == 3))
                    mm.then_inc(stream.used, 1)

        @block.scalar
        def _(act):
            norm.scalar(act)
            for k in range(N_PROJ // 2):
                stream.round(act, 0, 2 * k + 2)
                act.wait_ge(stream.used, stream.used_at(2 * k + 1))
                nc.scalar.activation(u[:, 2 * k:2 * k + 2, :].rearrange("p a b -> p (a b)"), chip.bank[k % 2][:, :], ACT.Copy)\
                    .then_inc(chip.copied.sem, 1)
                stream.round(act, 0, 2 * k + 3)
            for n in range(8):
                stream.round(act, 0, N_PROJ + n + 2)
            act.wait_ge(stream.used, stream.used_at(27))
            for tt in range(2):
                nc.scalar.activation(rv[:, tt, :], chip.bank[2 + tt][:, :], ACT.Copy)
                nc.scalar.activation(vs[:, tt, :], chip.bank[4 + tt][:, 0:S], ACT.Copy)
                nc.scalar.activation(chip.gates[:, tt, :], chip.bank[4 + tt][:, S:S + 24], ACT.Sigmoid)

        @block.vector
        def _(dve):
            norm.vector(dve)
            for n in range(28):
                stream.subtract(dve, 0, n + 2)
    norm.end()
    chip.table.passed(80)
    chip.copied.passed(N_PROJ // 2)
    stream.g0 += 28


def table(chip, name, *shape):
    at, n = TAB[name]
    return chip.part(B_TAB + at, *(shape or (n,)))


def stage_rope(chip):
    nc, u = chip.nc, chip.part(B_U, N_PROJ, S)
    pairs = [(n, min(n + 2, ROPE_ALL)) for n in range(0, ROPE_ALL, 2)]
    with nc.Block() as block:
        @block.tensor
        def _(pe):
            for k, (lo, hi) in enumerate(pairs):
                perm = table(chip, "perm128" if lo < ROPE_WIDE else "perm64")
                mm = nc.tensor.matmul(chip.bank[k][:, 0:(hi - lo) * S], perm,
                                      u[:, lo:hi, :].rearrange("p a b -> p (a b)"), start=True, stop=True)
                mm.then_inc(chip.turned.sem, 1)

        @block.vector
        def _(dve):
            for k, (lo, hi) in enumerate(pairs):
                size = "128" if lo < ROPE_WIDE else "64"
                n = hi - lo
                cos, sin = (table(chip, x + size).unsqueeze(1).to_broadcast([P, n, S]) for x in ("cos", "sin"))
                tmp = chip.part(B_RY if k % 2 else B_T1, n, S)
                rot = chip.bank[k][:, 0:n * S].rearrange("p (a b) -> p a b", b=S)
                dve.wait_ge(chip.turned.sem, chip.turned.at(k + 1))
                nc.vector.tensor_tensor(tmp, rot, sin, ALU.mult)
                in_order(dve, chip.dve_step, nc.vector.tensor_tensor(u[:, lo:hi, :], u[:, lo:hi, :], cos, ALU.mult))
                nc.vector.tensor_tensor(u[:, lo:hi, :], u[:, lo:hi, :], tmp, ALU.add)
    chip.turned.passed(len(pairs))


def stage_retention(chip):
    nc = chip.nc
    u, rv, y = chip.part(B_U, N_PROJ, S), chip.part(B_RV, 2, 512), chip.part(B_Y, KT, S)
    sr, ry = chip.part(B_SR, 2, 384), chip.part(B_RY, RET_H * S)
    t1, t2 = chip.part(B_T1, RET_H * S), chip.part(B_T2, RET_H * S)
    decay = table(chip, "decay", RET_H, S)
    halves = [slice(0, 512), slice(512, 1024)]
    with nc.Block() as block:
        @block.tensor
        def _(pe):
            def scores(h):
                if h >= 2:
                    pe.wait_ge(chip.probs.sem, chip.probs.at(h - 1))
                q, k, b = u[:, R_Q + h, :], u[:, R_K + h, :], chip.bank[h % 2]
                nc.tensor.matmul(b[:, 0:S], k[:, 0:P], q, start=True, stop=True)
                nc.tensor.matmul(b[:, S:384], k[:, P:S], q[:, P:S], start=True, stop=True).then_inc(chip.scored.sem, 1)

            scores(0)
            for h in range(RET_H):
                if h + 1 < RET_H:
                    scores(h + 1)
                pe.wait_ge(chip.probs.sem, chip.probs.at(h + 1))
                o = chip.bank[2 + h // 2][:, (h % 2) * S:(h % 2 + 1) * S]
                nc.tensor.matmul(o, rv[:, 0, h * P:(h + 1) * P], sr[:, h % 2, 0:S], start=True, stop=False)
                nc.tensor.matmul(o[:, P:S], rv[:, 1, h * P:(h + 1) * P], sr[:, h % 2, S:384], start=False, stop=True)\
                    .then_inc(chip.product.sem, 1)
            pe.wait_ge(chip.copied.sem, chip.copied.at(2))
            for n, part in enumerate(halves):
                nc.tensor.matmul(chip.bank[4 + n][:, :], chip.ones[:, :], ry[:, part], start=True, stop=True)\
                    .then_inc(chip.summed.sem, 1)
            pe.wait_ge(chip.squared.sem, chip.squared.at(1))
            for n, part in enumerate(halves):
                nc.tensor.matmul(chip.bank[6 + n][:, :], chip.ones[:, :], t1[:, part], start=True, stop=True)\
                    .then_inc(chip.summed.sem, 1)

        @block.scalar
        def _(act):
            nc.scalar.activation(u[:, R_G:R_G + RET_H, :], u[:, R_G:R_G + RET_H, :], ACT.Silu).then_inc(chip.silu_done.sem, 1)
            for n, part in enumerate(halves):
                act.wait_ge(chip.product.sem, chip.product.at(2 * n + 2))
                nc.scalar.activation(ry[:, part], chip.bank[2 + n][:, :], ACT.Copy).then_inc(chip.copied.sem, 1)
            act.wait_ge(chip.scaled.sem, chip.scaled.at(1))
            nc.scalar.activation(t1, ry, ACT.Square).then_inc(chip.squared.sem, 1)
            for n, part in enumerate(halves):
                act.wait_ge(chip.summed.sem, chip.summed.at(3 + n))
                last = nc.scalar.activation(t2[:, part], chip.bank[6 + n][:, :], ACT.Sqrt, bias=chip.eps[:, 0:1], scale=1.0 / P)
            last.then_inc(chip.rooted.sem, 1)

        @block.vector
        def _(dve):
            for h in range(RET_H):
                dve.wait_ge(chip.scored.sem, chip.scored.at(h + 1))
                if h >= 2:
                    dve.wait_ge(chip.product.sem, chip.product.at(h - 1))
                b = chip.bank[h % 2]
                nc.vector.tensor_tensor(sr[:, h % 2, 0:S], b[:, 0:S], decay[:, h, :], ALU.mult)
                nc.vector.tensor_tensor(sr[:, h % 2, S:384], b[:, S:384], decay[:, h, 0:P], ALU.mult).then_inc(chip.probs.sem, 1)
            dve.wait_ge(chip.copied.sem, chip.copied.at(2))
            dve.wait_ge(chip.summed.sem, chip.summed.at(2))
            for n, part in enumerate(halves):
                last = nc.vector.scalar_tensor_tensor(ry[:, part], chip.bank[4 + n][:, :], -1.0 / P, ry[:, part], ALU.mult, ALU.add)
            last.then_inc(chip.scaled.sem, 1)
            dve.wait_ge(chip.rooted.sem, chip.rooted.at(1))
            dve.wait_ge(chip.silu_done.sem, chip.silu_done.at(1))
            in_order(dve, chip.dve_step, nc.vector.reciprocal(t2, t2))
            in_order(dve, chip.dve_step, nc.vector.tensor_tensor(ry, ry, t2, ALU.mult))
            nc.vector.tensor_tensor(y[:, 0:RET_H, :].rearrange("p a b -> p (a b)"), ry,
                                    u[:, R_G:R_G + RET_H, :].rearrange("p a b -> p (a b)"), ALU.mult)
    for sig, n in ((chip.scored, 4), (chip.probs, 4), (chip.product, 4), (chip.copied, 2), (chip.summed, 4),
                   (chip.squared, 1), (chip.rooted, 1), (chip.scaled, 1), (chip.silu_done, 1)):
        sig.passed(n)


def stage_compress(chip):
    nc = chip.nc
    u = chip.part(B_U, N_PROJ, S)
    w1 = [chip.part(B_W1 + 4096 * n, 16, 256) for n in range(2)]
    w2 = [chip.part(B_W2 + 128 * n, 2, 64) for n in range(2)]
    k2 = [chip.part(B_K2 + 512 * n, 2, S) for n in range(2)]
    blk = [chip.part(B_BLK + 480 * n, 16, 30) for n in range(2)]
    hid = [chip.part(B_HID + 60 * n, 2, 30) for n in range(2)]
    ptc = chip.part(B_PTC, NSA_H, S)
    s_c, mask01, add = chip.part(B_C, 16, 16), table(chip, "cmp_mask", 2, 16), table(chip, "cmp_add", 2, 16)
    top, tot = chip.part(B_C + 256, 16), chip.part(B_C + 272, 16)
    kc, vc = chip.part(B_C + 288, 16), chip.part(B_C + 304, 2, 64)
    sc = s_c[:, :, 0:NCB]
    with nc.Block() as block:
        @block.vector
        def _(dve):
            for n, chunk in enumerate((N_KC, N_VC)):
                for g in range(2):
                    src = u[64 * g:64 * g + 64, chunk, :]
                    nc.vector.tensor_copy(k2[n][0:64, g, :], src)
                    last = nc.vector.tensor_copy(k2[n][64:128, g, 0:S - 1], src[:, 1:S])
            nc.vector.memset(k2[0][64:128, :, S - 1:S], 0.0)
            in_order(dve, chip.dve_step, nc.vector.memset(k2[1][64:128, :, S - 1:S], 0.0))
            for n, pe_col in enumerate(("pe_k", "pe_v")):
                for g in range(2):
                    v = k2[n][:, g, :].rearrange("p (n l) -> p l n", l=CMP_STRIDE)
                    for j0 in (0, 8):
                        out = blk[n][:, j0:j0 + 8, g * NCB:(g + 1) * NCB]
                        pos = chip.col(pe_col, j0, 8).unsqueeze(2).to_broadcast([P, 8, NCB])
                        at = j0 // 8
                        last = nc.vector.tensor_tensor(out, v[:, 0:CMP_STRIDE:2, at:at + NCB], pos, ALU.add)
            last.then_inc(chip.gated.sem, 1)
            dve.wait_ge(chip.scored.sem, chip.scored.at(1))
            for qt in range(2):
                for g in range(2):
                    last = nc.vector.scalar_tensor_tensor(
                        s_c[:, 8 * qt + g:8 * qt + 8:2, 0:NCB],
                        chip.bank[6 + g][:, 64 * qt:64 * qt + 64].rearrange("p (h n) -> p h n", n=16)[:, :, 0:NCB], 0.125,
                        add[:, qt, 0:NCB].unsqueeze(1).to_broadcast([P, 4, NCB]), ALU.mult, ALU.add)
            in_order(dve, chip.dve_step, last)
            in_order(dve, chip.dve_step, nc.vector.tensor_reduce(top, sc, AX.X, ALU.max))
            nc.vector.tensor_tensor(sc, sc, top.unsqueeze(2).to_broadcast([P, 16, NCB]), ALU.subtract).then_inc(chip.maxed.sem, 1)
            dve.wait_ge(chip.exped.sem, chip.exped.at(1))
            for qt in range(2):
                last = nc.vector.tensor_tensor(s_c[:, 8 * qt:8 * qt + 8, 0:NCB], s_c[:, 8 * qt:8 * qt + 8, 0:NCB],
                                               mask01[:, qt, 0:NCB].unsqueeze(1).to_broadcast([P, 8, NCB]), ALU.mult)
            in_order(dve, chip.dve_step, last)
            in_order(dve, chip.dve_step, nc.vector.tensor_reduce(tot, sc, AX.X, ALU.add))
            in_order(dve, chip.dve_step, nc.vector.tensor_scalar(tot, tot, TINY, None, ALU.max))
            in_order(dve, chip.dve_step, nc.vector.reciprocal(tot, tot))
            gate = chip.gates[:, :, :].rearrange("p t (h b) -> p (t h) b", b=3)[:, :, 0]
            in_order(dve, chip.dve_step, nc.vector.tensor_tensor(tot, tot, gate, ALU.mult))
            nc.vector.tensor_tensor(sc, sc, tot.unsqueeze(2).to_broadcast([P, 16, NCB]), ALU.mult).then_inc(chip.probs.sem, 1)

        @block.tensor
        def _(pe):
            pe.wait_ge(chip.gated.sem, chip.gated.at(1))
            for n in range(2):
                for m in range(2):
                    for j in range(16):
                        mm = nc.tensor.matmul(chip.bank[2 * n + m][:, 0:2 * NCB], w1[n][:, j, m * P:(m + 1) * P],
                                              blk[n][:, j, :], start=(j == 0), stop=(j == 15))
                    mm.then_inc(chip.product.sem, 1)
            pe.wait_ge(chip.silu_done.sem, chip.silu_done.at(4))
            for g in range(2):
                for m in range(2):
                    nc.tensor.matmul(chip.bank[4][64 * g:64 * g + 64, 0:NCB], w2[0][:, m, :],
                                     hid[0][:, m, g * NCB:(g + 1) * NCB], start=(m == 0), stop=(m == 1))
                for m in range(2):
                    mm = nc.tensor.matmul(chip.bank[5][0:NCB, 64 * g:64 * g + 64], hid[1][:, m, g * NCB:(g + 1) * NCB],
                                          w2[1][:, m, :], start=(m == 0), stop=(m == 1))
            mm.then_inc(chip.product.sem, 1)
            pe.wait_ge(chip.copied.sem, chip.copied.at(1))
            for qt in range(2):
                for hh in range(NSA_H):
                    po, n = 64 * (hh % 2), 4 * qt + hh // 2
                    mm = nc.tensor.matmul(chip.bank[6 + hh % 2][:, n * 16:n * 16 + NCB], u[po:po + 64, N_Q + hh // 2, qt * P:(qt + 1) * P],
                                          kc[po:po + 64, 0:NCB], start=True, stop=True)
            mm.then_inc(chip.scored.sem, 1)
            pe.wait_ge(chip.probs.sem, chip.probs.at(1))
            for hh in range(NSA_H):
                for qt in range(2):
                    n = 2 * hh + qt
                    mm = nc.tensor.matmul(chip.bank[n // 4][0:NCB, (n % 4) * P:(n % 4 + 1) * P], s_c[:, 8 * qt + hh, 0:NCB],
                                          chip.ident[:, :], start=True, stop=True)
            mm.then_inc(chip.turned.sem, 1)

        @block.scalar
        def _(act):
            for n in range(2):
                for m in range(2):
                    act.wait_ge(chip.product.sem, chip.product.at(2 * n + m + 1))
                    nc.scalar.activation(hid[n][:, m, :], chip.bank[2 * n + m][:, 0:2 * NCB], ACT.Gelu_apprx_tanh,
                                         bias=chip.col(("b_cmp_k", "b_cmp_v")[n], m, 1)).then_inc(chip.silu_done.sem, 1)
            act.wait_ge(chip.product.sem, chip.product.at(5))
            nc.scalar.activation(kc[:, 0:NCB], chip.bank[4][:, 0:NCB], ACT.Copy)
            nc.scalar.activation(vc[0:NCB, :, :].rearrange("p a b -> p (a b)"), chip.bank[5][0:NCB, 0:P], ACT.Copy).then_inc(chip.copied.sem, 1)
            act.wait_ge(chip.maxed.sem, chip.maxed.at(1))
            nc.scalar.activation(sc, sc, ACT.Exp).then_inc(chip.exped.sem, 1)
            act.wait_ge(chip.turned.sem, chip.turned.at(1))
            for b in range(4):
                nc.scalar.activation(ptc[0:NCB, 2 * b:2 * b + 2, :].rearrange("p a b -> p (a b)"), chip.bank[b][0:NCB, :], ACT.Copy)
    for sig, n in ((chip.gated, 1), (chip.scored, 1), (chip.maxed, 1), (chip.exped, 1), (chip.probs, 1), (chip.product, 5),
                   (chip.silu_done, 4), (chip.copied, 1), (chip.turned, 1)):
        sig.passed(n)


def stage_sparse(chip):
    nc = chip.nc
    u, vs, y = chip.part(B_U, N_PROJ, S), chip.part(B_VS, 2, S), chip.part(B_Y, KT, S)
    sc, pts, ptc = chip.part(B_SC, 2, 2, S), chip.part(B_PTS, 2, 2, 384), chip.part(B_PTC, NSA_H, S)
    vc, causal = chip.part(B_C + 304, 2, 64), table(chip, "causal")
    items = [(hh, qt) for hh in range(NSA_H) for qt in range(2)]

    with nc.Block() as block:
        @block.tensor
        def _(pe):
            def scores(w):
                hh, qt = items[w]
                po, nk = 64 * (hh % 2), P * (qt + 1)
                if w >= 2:
                    pe.wait_ge(chip.scores_read.sem, chip.scores_read.at(w - 1))
                for br, chunk in enumerate((N_KS, N_KW)):
                    mm = nc.tensor.matmul(chip.bank[w % 2][:, br * S:br * S + nk], u[po:po + 64, N_Q + hh // 2, qt * P:(qt + 1) * P],
                                          u[po:po + 64, chunk, 0:nk], start=True, stop=True)
                mm.then_inc(chip.scored.sem, 1)

            def transposes(w):
                hh, qt = items[w]
                pe.wait_ge(chip.probs.sem, chip.probs.at(w + 1))
                if w >= 2:
                    pe.wait_ge(chip.copied.sem, chip.copied.at(w - 1))
                for br in range(2):
                    for kt in range(qt + 1):
                        mm = nc.tensor.transpose(chip.bank[2 + w % 2][:, (2 * br + kt) * P:(2 * br + kt + 1) * P],
                                                 sc[:, w % 2, br, kt * P:(kt + 1) * P], chip.ident[:, :])
                mm.then_inc(chip.turned.sem, 1)

            def values(hh):
                g = hh % 2
                pe.wait_ge(chip.copied.sem, chip.copied.at(2 * hh + 2))
                if hh >= 2:
                    pe.wait_ge(chip.moved.sem, chip.moved.at(hh - 1))
                o = chip.bank[4 + hh % 2][64 * g:64 * g + 64, :]
                for br in range(2):
                    v = slice(br * P + g * 64, br * P + g * 64 + 64)
                    nc.tensor.matmul(o[:, 0:S], vs[:, 0, v], pts[:, hh % 2, br, 0:S], start=(br == 0), stop=False)
                    nc.tensor.matmul(o[:, P:S], vs[:, 1, v], pts[:, hh % 2, br, S:384], start=False, stop=False)
                nc.tensor.matmul(o[:, 0:S], vc[0:NCB, g, :], ptc[0:NCB, hh, :], start=False, stop=True).then_inc(chip.product.sem, 1)

            scores(0)
            scores(1)
            for w in range(len(items)):
                transposes(w)
                if w + 2 < len(items):
                    scores(w + 2)
                if w >= 2 and w % 2 == 0:
                    values(w // 2 - 1)
            values(NSA_H - 1)

        @block.scalar
        def _(act):
            def exps(w):
                hh, qt = items[w]
                nk = P * (qt + 1)
                act.wait_ge(chip.maxed.sem, chip.maxed.at(w + 1))
                for br in range(2):
                    last = nc.scalar.activation(sc[:, w % 2, br, 0:nk], sc[:, w % 2, br, 0:nk], ACT.Exp,
                                                bias=chip.nmax4[:, w % 2, br:br + 1], accum_out=chip.rsum4[:, w % 2, br:br + 1])
                last.then_inc(chip.exped.sem, 1)

            def copies(w):
                hh, qt = items[w]
                act.wait_ge(chip.turned.sem, chip.turned.at(w + 1))
                if hh >= 2:
                    act.wait_ge(chip.product.sem, chip.product.at(hh - 1))
                src = chip.bank[2 + w % 2][:, :].rearrange("p (b k) -> p b k", b=2)
                nc.scalar.activation(pts[:, hh % 2, :, P * qt:P * qt + P * (qt + 1)], src[:, :, 0:P * (qt + 1)], ACT.Copy)\
                    .then_inc(chip.copied.sem, 1)

            def move(hh):
                po = 64 * (hh % 2)
                act.wait_ge(chip.product.sem, chip.product.at(hh + 1))
                nc.scalar.activation(y[po:po + 64, 4 + hh // 2, :], chip.bank[4 + hh % 2][po:po + 64, 0:S], ACT.Copy)\
                    .then_inc(chip.moved.sem, 1)

            exps(0)
            for w in range(len(items)):
                if w + 1 < len(items):
                    exps(w + 1)
                copies(w)
                if w >= 3 and w % 2 == 1:
                    move(w // 2 - 1)
            move(NSA_H - 1)

        @block.vector
        def _(dve):
            def scale(w):
                hh, qt = items[w]
                nk = P * (qt + 1)
                s = sc[:, w % 2, :, 0:nk]
                dve.wait_ge(chip.scored.sem, chip.scored.at(w + 1))
                if w >= 2:
                    dve.wait_ge(chip.turned.sem, chip.turned.at(w - 1))
                nc.vector.scalar_tensor_tensor(s, chip.bank[w % 2][:, :].rearrange("p (b k) -> p b k", b=2)[:, :, 0:nk], 0.125,
                                               causal[:, S - nk:S].unsqueeze(1).to_broadcast([P, 2, nk]), ALU.mult, ALU.add)\
                    .then_inc(chip.scores_read.sem, 1)
                dve.wait_ge(chip.scores_read.sem, chip.scores_read.at(w + 1))
                nc.vector.tensor_reduce(chip.nmax4[:, w % 2, :], s, AX.X, ALU.max, negate=True).then_inc(chip.maxed.sem, 1)

            def normalise(w):
                hh, qt = items[w]
                nk = P * (qt + 1)
                s, r = sc[:, w % 2, :, 0:nk], chip.rsum4[:, w % 2, :]
                dve.wait_ge(chip.exped.sem, chip.exped.at(w + 1))
                in_order(dve, chip.dve_step, nc.vector.reciprocal(r, r))
                in_order(dve, chip.dve_step, nc.vector.tensor_tensor(r, r, chip.gates[:, qt, 3 * hh + 1:3 * hh + 3], ALU.mult))
                nc.vector.tensor_tensor(s, s, r.unsqueeze(2).to_broadcast([P, 2, nk]), ALU.mult).then_inc(chip.probs.sem, 1)

            scale(0)
            for w in range(len(items)):
                if w + 1 < len(items):
                    scale(w + 1)
                normalise(w)
    n = len(items)
    for sig in (chip.scored, chip.scores_read, chip.maxed, chip.exped, chip.probs, chip.turned, chip.copied):
        sig.passed(n)
    chip.product.passed(NSA_H)
    chip.moved.passed(NSA_H)


def stage_expert_scores(chip, stream):
    nc = chip.nc
    norm = norm2(chip, 1, E_SC2, E_KEYS + UNIT * 2)
    keys = chip.part(E_KEYS, 16 * NK)
    q, s = chip.part(E_Q, 16, S), chip.part(E_SC, 2, 16, NK)
    with nc.Block() as block:
        @block.sync
        def _(sp):
            sp.dma_start(keys, chip.dram["subkeys"]).then_inc(chip.table.sem, 16)
            stream.load_ahead(sp, 16)

        @block.tensor
        def _(pe):
            norm.tensor(pe)
            pe.wait_ge(chip.split_in.sem, chip.split_in.at(KT))
            for n in range(16):
                k = n // 2
                if n >= 4 and n % 2 == 0:
                    pe.wait_ge(chip.copied.sem, chip.copied.at(k - 1))
                w_hi, w_lo = stream.operands(pe, 0, n)
                product(nc, chip.bank[k % 2][:, n % 2 * S:(n % 2 + 1) * S],
                        [((w_hi[:, kt * P:(kt + 1) * P], w_lo[:, kt * P:(kt + 1) * P]), (chip.hi[:, kt, :], chip.lo[:, kt, :]))
                         for kt in range(KT)]).then_inc(stream.used, 1)
            pe.wait_ge(chip.table.sem, chip.table.at(16))
            pe.wait_ge(chip.copied.sem, chip.copied.at(8))
            for tt in range(2):
                for n in range(16):
                    mm = nc.tensor.matmul(chip.bank[4 * tt + n // 4][:, (n % 4) * NK:(n % 4 + 1) * NK],
                                          q[:, n, tt * P:(tt + 1) * P], keys[:, n * NK:(n + 1) * NK], start=True, stop=True)
            mm.then_inc(chip.scored.sem, 1)

        @block.scalar
        def _(act):
            norm.scalar(act)
            for k in range(8):
                stream.round(act, 0, 2 * k + 2)
                act.wait_ge(stream.used, stream.used_at(2 * k + 1))
                nc.scalar.activation(q[:, 2 * k:2 * k + 2, :].rearrange("p a b -> p (a b)"), chip.bank[k % 2][:, :], ACT.Copy)\
                    .then_inc(chip.copied.sem, 1)
                stream.round(act, 0, 2 * k + 3)
            act.wait_ge(chip.scored.sem, chip.scored.at(1))
            for b in range(8):
                nc.scalar.activation(s[:, b // 4, 4 * (b % 4):4 * (b % 4) + 4, :].rearrange("p a b -> p (a b)"),
                                     chip.bank[b][:, :], ACT.Copy)

        @block.vector
        def _(dve):
            norm.vector(dve)
            for n in range(16):
                stream.subtract(dve, 0, n + 2)
    norm.end()
    chip.copied.passed(8)
    chip.table.passed(16)
    chip.scored.passed(1)
    stream.g0 += 16


def stage_retrieve(chip):
    nc = chip.nc
    s = chip.part(E_SC, 2, 16, NK)
    rest = [chip.part(E_SC2 + 256 * n, 256) for n in range(2)]
    v, ix = chip.part(E_V, 2, 16, TOPK), chip.part(E_I, 2, 16, TOPK).bitcast(U32)
    ixf = chip.part(E_IF, 2, 16, TOPK)
    tv, tj = chip.part(E_TV, 2, SLOTS), chip.part(E_TJ, 2, SLOTS).bitcast(U32)
    jj, jf = chip.part(E_J, 2, SLOTS).bitcast(U32), chip.part(E_JF, 2, SLOTS)
    eq = chip.part(E_EQ, PH * TOPK, TOPK)
    slots = chip.part(E_N, 3, SLOTS)
    small = chip.part(E_W, 64)
    cand = chip.part(E_CAND, 2, PH, TOPK * TOPK)
    iota16, iota = chip.iota[:, 0:TOPK], chip.iota

    with nc.Block() as block:
        @block.gpsimd
        def _(pool):
            nc.gpsimd.iota(iota[:, :], [[1, P]], base=0, channel_multiplier=0, allow_small_or_imprecise_dtypes=True)\
                .then_inc(chip.table.sem, 1)

        @block.vector
        def _(dve):
            step = lambda ins: in_order(dve, chip.dve_step, ins)

            def best(values, index, source, spare):
                both = list(zip(values, index, source, spare))
                for lo in (0, 8):
                    src = [x[2] if lo == 0 else x[3] for x in both]
                    for x, sr in zip(both, src):
                        last = nc.vector.max(x[0][:, lo:lo + 8], sr)
                    step(last)
                    for x, sr in zip(both, src):
                        last = nc.vector.max_index(x[1][:, lo:lo + 8], x[0][:, lo:lo + 8], sr)
                        if lo == 0:
                            last = nc.vector.match_replace(x[3], x[0][:, 0:8], sr, -3e38)
                    step(last)

            for tt in range(2):
                for n in range(0, 16, 2):
                    best([v[:, tt, n + i, :] for i in range(2)], [ix[:, tt, n + i, :] for i in range(2)],
                         [s[:, tt, n + i, :] for i in range(2)], [rest[i][:, 0:NK] for i in range(2)])
            step(nc.vector.tensor_copy(ixf, ix))
            for tt in range(2):
                vp = v[:, tt, :, :].rearrange("p (h two) k -> p h two k", two=2)
                for h in range(PH):
                    last = nc.vector.tensor_tensor(
                        cand[:, tt, h, :].rearrange("p (a b) -> p a b", b=TOPK),
                        vp[:, h, 0, :].unsqueeze(2).to_broadcast([P, TOPK, TOPK]),
                        vp[:, h, 1, :].unsqueeze(1).to_broadcast([P, TOPK, TOPK]), ALU.add)
            step(last)
            for tt in range(2):
                for h in range(0, PH, 2):
                    at = lambda x: [x[:, tt, (h + i) * TOPK:(h + i + 1) * TOPK] for i in range(2)]
                    best(at(tv), at(tj), [cand[:, tt, h + i, :] for i in range(2)], rest)
            dve.wait_ge(chip.table.sem, chip.table.at(1))
            for tt in range(2):
                for half in range(2):
                    step(nc.vector.tensor_scalar(jj[:, half, :], tj[:, tt, :], 4 if half == 0 else 15, None,
                                                 ALU.logical_shift_right if half == 0 else ALU.bitwise_and))
                    step(nc.vector.tensor_copy(jf[:, half, :], jj[:, half, :]))
                    step(nc.vector.tensor_tensor(eq, iota16.unsqueeze(1).to_broadcast([P, SLOTS, TOPK]),
                                                 jf[:, half, :].unsqueeze(2).to_broadcast([P, SLOTS, TOPK]), ALU.is_equal))
                    e4 = eq.rearrange("p (h k) i -> p h k i", h=PH)
                    sub = ixf[:, tt, :, :].rearrange("p (h two) k -> p h two k", two=2)[:, :, half, :]
                    step(nc.vector.tensor_tensor(e4, e4, sub.unsqueeze(2).to_broadcast([P, PH, TOPK, TOPK]), ALU.mult))
                    if tt == 1 and half == 0:
                        dve.wait_ge(chip.turned.sem, chip.turned.at(1))
                    step(nc.vector.tensor_reduce(slots[:, half, :], eq, AX.X, ALU.add))
                w = slots[:, 2, :].rearrange("p (h k) -> p h k", h=PH)
                t3 = tv[:, tt, :].rearrange("p (h k) -> p h k", h=PH)
                nc.vector.tensor_tensor(w, t3, t3[:, :, 0:1].to_broadcast([P, PH, TOPK]), ALU.subtract)\
                    .then_inc(chip.maxed.sem, 1)
                dve.wait_ge(chip.exped.sem, chip.exped.at(tt + 1))
                step(nc.vector.tensor_reduce(small[:, 0:PH], w, AX.X, ALU.add))
                step(nc.vector.reciprocal(small[:, 0:PH], small[:, 0:PH]))
                nc.vector.tensor_tensor(w, w, small[:, 0:PH].unsqueeze(2).to_broadcast([P, PH, TOPK]), ALU.mult)\
                    .then_inc(chip.probs.sem, 1)

        @block.scalar
        def _(act):
            for tt in range(2):
                act.wait_ge(chip.maxed.sem, chip.maxed.at(tt + 1))
                nc.scalar.activation(slots[:, 2, :], slots[:, 2, :], ACT.Exp).then_inc(chip.exped.sem, 1)
                act.wait_ge(chip.turned.sem, chip.turned.at(tt + 1))
                nc.scalar.activation(chip.part(E_SLOT, 3, S)[:, :, tt * P:(tt + 1) * P],
                                     chip.bank[tt][:, 0:3 * P].rearrange("p (a b) -> p a b", b=P), ACT.Copy)

        @block.tensor
        def _(pe):
            for tt in range(2):
                pe.wait_ge(chip.probs.sem, chip.probs.at(tt + 1))
                for n in range(3):
                    mm = nc.tensor.transpose(chip.bank[tt][:, n * P:(n + 1) * P], slots[:, n, :], chip.ident[:, :])
                mm.then_inc(chip.turned.sem, 1)
    for sig in (chip.maxed, chip.exped, chip.probs, chip.turned):
        sig.passed(2)
    chip.table.passed(1)


def stage_spread(chip):
    nc = chip.nc
    weight = chip.part(0, S, NK)
    work = chip.part(E_HOT, 4, 2 * P)
    a, b = work[:, :, 0:P], work[:, :, P:2 * P]
    with nc.Block() as block:
        @block.vector
        def _(dve):
            def onehots(c, j):
                t = NS * c + j
                if not static(c):
                    dve.wait_ge(chip.product.sem, chip.product.at(t - 3))
                col = lambda n: chip.part(E_SLOT, 3, S)[:, n, bass.ds(t, 1)]
                nc.vector.tensor_scalar(a[:, j, :], chip.iota[:, :], col(0), col(2), ALU.is_equal, ALU.mult)
                nc.vector.tensor_scalar(b[:, j, :], chip.iota[:, :], col(1), None, ALU.is_equal).then_inc(chip.probs.sem, 1)
            over_units(dve, S, onehots)

        @block.tensor
        def _(pe):
            def spread(c, j):
                t = NS * c + j
                if not static(c) and j % 2 == 0:
                    pe.wait_ge(chip.copied.sem, chip.copied.at(2 * c + (j // 2 - 1)))
                pe.wait_ge(chip.probs.sem, chip.probs.at(t + 1))
                nc.tensor.matmul(chip.bank[j // 2][:, (j % 2) * P:(j % 2 + 1) * P], a[:, j, :], b[:, j, :],
                                 start=True, stop=True).then_inc(chip.product.sem, 1)
            over_units(pe, S, spread)

        @block.scalar
        def _(act):
            with act.Fori(0, S // NS) as c:
                for j in range(2):
                    act.wait_ge(chip.product.sem, chip.product.at(NS * c + (2 * j + 2)))
                    nc.scalar.activation(weight[:, bass.ds(NS * c + 2 * j, 2), :].rearrange("p a b -> p (a b)"),
                                         chip.bank[j][:, 0:2 * P], ACT.Copy).then_inc(chip.copied.sem, 1)
    chip.product.passed(S)
    chip.probs.passed(S)
    chip.copied.passed(S // 2)


def stage_experts(chip, stream):
    nc = chip.nc
    weight, f = chip.part(0, S, NK), chip.part(E_HOT, 2, S)
    g_hi, g_lo = chip.extra["act_hi"], chip.extra["act_lo"]
    steps = NK
    with nc.Block() as block:
        @block.sync
        def _(sp):
            stream.load_ahead(sp, 2 * steps)

        @block.tensor
        def _(pe):
            def down(c, j, at):
                w_hi, w_lo = stream.operands(pe, c, j)
                product(nc, chip.bank[at][:, 0:S],
                        [((w_hi[:, kt * P:(kt + 1) * P], w_lo[:, kt * P:(kt + 1) * P]), (chip.hi[:, kt, :], chip.lo[:, kt, :]))
                         for kt in range(KT)]).then_inc(stream.used, 1)

            def up(c, j, k, at, first=False, last=False):
                pe.wait_ge(chip.gated.sem, chip.gated.at(k + 1))
                w_hi, w_lo = stream.operands(pe, c, j)
                for tt in range(2):
                    for half in range(2):
                        q, n = slice(tt * P, (tt + 1) * P), slice(half * 512, (half + 1) * 512)
                        mm = product(nc, chip.bank[4 + 2 * tt + half][:, :],
                                     [((g_hi[:, at, q], g_lo[:, at, q]), (w_hi[:, n], w_lo[:, n]))], start=first, stop=last)
                mm.then_inc(stream.used, 1)

            down(0, 0, 0)
            down(0, 1, 1)
            up(0, 2, 0, 0, first=True)
            down(0, 3, 0)
            up(1, 0, 1, 1)
            down(1, 1, 1)
            with pe.Fori(1, steps // 2 - 1) as c:
                up(c, 2, 2 * c, 0)
                down(c, 3, 0)
                up(c, 4, 2 * c + 1, 1)
                down(c, 5, 1)
            c = steps // 2 - 1
            up(c, 2, 2 * c, 0)
            up(c, 3, 2 * c + 1, 1, last=True)

        @block.scalar
        def _(act):
            def gelu(c, j, at):
                act.wait_ge(stream.used, stream.used_at(NS * c + j))
                nc.scalar.activation(f[:, at, :], chip.bank[at][:, 0:S], ACT.Gelu_apprx_tanh).then_inc(chip.gelu_done.sem, 1)
                stream.round(act, c, j + 2)

            gelu(0, 0, 0)
            gelu(0, 1, 1)
            with act.Fori(0, steps // 2 - 1) as c:
                stream.round(act, c, 4)
                gelu(c, 3, 0)
                stream.round(act, c, 6)
                gelu(c, 5, 1)

        @block.vector
        def _(dve):
            def weigh(k, at):
                dve.wait_ge(chip.gelu_done.sem, chip.gelu_done.at(k + 1))
                nc.vector.tensor_tensor(f[:, at, :], f[:, at, :], weight[:, :, k], ALU.mult).then_inc(chip.ffn_step.sem, 1)
                dve.wait_ge(chip.ffn_step.sem, chip.ffn_step.at(2 * k + 1))
                first, rest = split_activations(nc, g_hi[:, at, :], g_lo[:, at, :], f[:, at, :])
                first.then_inc(chip.ffn_step.sem, 1)
                dve.wait_ge(chip.ffn_step.sem, chip.ffn_step.at(2 * k + 2))
                rest().then_inc(chip.gated.sem, 1)

            for k in range(2):
                weigh(k, k)
                stream.subtract(dve, 0, k + 2)
            with dve.Fori(0, steps // 2 - 1) as c:
                stream.subtract(dve, c, 4)
                weigh(2 * c + 2, 0)
                stream.subtract(dve, c, 5)
                stream.subtract(dve, c, 6)
                weigh(2 * c + 3, 1)
                stream.subtract(dve, c, 7)
    chip.gelu_done.passed(steps)
    chip.ffn_step.passed(2 * steps)
    chip.gated.passed(steps)
    stream.g0 += 2 * steps


def stage_finish(chip, out):
    nc = chip.nc
    o = chip.part(0, 2, D)
    norm = Norm(chip, chip.x2, chip.part(8192, KT, S), chip.part(4096, S), chip.part(4096 + S, S),
                lambda kt, g: chip.col("g_final", kt, 1), None, [(0, S)], S, split=False)
    with nc.Block() as block:
        @block.scalar
        def _(act):
            for n in range(4):
                nc.scalar.activation(o[:, n // 2, (n % 2) * 512:(n % 2 + 1) * 512], chip.bank[4 + n][:, :], ACT.Copy)\
                    .then_inc(chip.copied.sem, 1)

        @block.tensor
        def _(pe):
            pe.wait_ge(chip.copied.sem, chip.copied.at(4))
            for kt in range(KT):
                for tt in range(2):
                    mm = nc.tensor.transpose(chip.bank[kt // 2][:, (kt % 2) * S + tt * P:(kt % 2) * S + (tt + 1) * P],
                                             o[:, tt, kt * P:(kt + 1) * P], chip.ident[:, :])
                mm.then_inc(chip.turned.sem, 1)

        @block.vector
        def _(dve):
            for kt in range(KT):
                dve.wait_ge(chip.turned.sem, chip.turned.at(2 * (kt // 2) + 2))
                nc.vector.scalar_tensor_tensor(chip.x2[:, kt, :], chip.bank[kt // 2][:, (kt % 2) * S:(kt % 2 + 1) * S],
                                               chip.mod2[:, 5 * KT + kt:5 * KT + kt + 1], chip.x2[:, kt, :], ALU.mult, ALU.add)
    chip.copied.passed(4)
    chip.turned.passed(KT)
    with nc.Block() as block:
        block.tensor(norm.tensor)
        block.scalar(norm.scalar)
        block.vector(norm.vector)

        @block.sync
        def _(sp):
            sp.wait_ge(chip.h_ready.sem, chip.h_ready.at(KT))
            sp.dma_start(out, norm.h).then_inc(chip.table.sem, 16)
            sp.wait_ge(chip.table.sem, chip.table.at(16))


def build(nc, dram, out):
    with ExitStack() as ctx:
        chip = Chip(ctx, nc, dram)
        segments = []
        for l in range(LAYERS):
            segments += [(dram["ffn"][l][0], FFN_UNITS), (dram["w_mix"][l], 28), (dram["ffn"][l][1], FFN_UNITS)]
        segments += [(dram["w_second"], 28 + KT + 16), (dram["experts"], 2 * NK)]
        stream = Stream(ctx, nc, segments)
        with ExitStack() as first:
            chip.take(first, T2, A_WORDS)
            stage_setup(chip, stream)
            for l in range(LAYERS):
                last = l == LAYERS - 1
                width = S if last else T2
                groups = [(0, S)] if last else [(0, S), (S, T2)]
                with ExitStack() as sublayer:
                    take_for_ffn(chip, sublayer, f"ffn{l}0")
                    if l == 0:
                        stage_first_mod(chip)
                        work = Modulation(chip, 12, 30, 2)
                        stage_ffn(chip, stream, l, 0, T2, work, lambda dve: finish_mod(chip, dve, 0, 3, 9))
                    else:
                        work = Modulation(chip, 72, 24, 1)
                        stage_ffn(chip, stream, l, 0, T2, work, lambda dve: finish_mod2(chip, dve))
                with ExitStack() as sublayer:
                    chip.take_more(sublayer, f"mixer{l}", A_MIXER)
                    stage_mix_in(chip, stream, l, last)
                    stage_mix(chip, stream, l, last)
                    stage_add_product(chip, stream, chip.part(A_X, KT, T2), chip.part(A_Y, KT, T2),
                                      lambda n, g: chip.mods[l][:, 5 * KT + n, g:g + 1], groups)
                with ExitStack() as sublayer:
                    take_for_ffn(chip, sublayer, f"ffn{l}1")
                    work = Modulation(chip, 42, 30, 2) if l == 0 else None
                    stage_ffn(chip, stream, l, 1, width, work, lambda dve: finish_mod(chip, dve, 1, 0, 9))
            stage_final_norm(chip)
        with ExitStack() as second:
            chip.take(second, S, B_WORDS)
            chip.take_more(second, "experts", act_hi=([P, 2, S], F32R), act_lo=([P, 2, S], F32R))
            stage_proj(chip, stream)
            stage_rope(chip)
            stage_retention(chip)
            stage_compress(chip)
            stage_sparse(chip)
            stage_add_product(chip, stream, chip.x2, chip.part(B_Y, KT, S),
                              lambda n, g: chip.mod2[:, 2 * KT + n:2 * KT + n + 1], [(0, S)])
            stage_expert_scores(chip, stream)
            stage_retrieve(chip)
            stage_spread(chip)
            stage_experts(chip, stream)
            stage_finish(chip, out)


def _layout(inp):
    def blocks(w):
        n = w.shape[1]
        return w.reshape(KT, P, n // P, P).transpose(2, 1, 0, 3).reshape(n // P, P, UNIT)

    def rows(w):
        return w.reshape(4, 2, P, 512).transpose(0, 2, 1, 3).reshape(4, P, UNIT)

    def pack(w):
        k, n = w.shape
        return w.reshape(k // P, P, n // 256, 256).transpose(2, 1, 0, 3).reshape(n // 256, P, k // P * 256)

    def vec(v):
        return v.reshape(-1, P).T

    f = np.float32
    a = {}
    a["w_mods"] = np.concatenate([pack(w) for w in inp["w_mod"]] + [pack(inp["w_ada_2"][0])])
    ffn = []
    for l in range(LAYERS):
        for k in range(2):
            a_b = blocks(inp["ffn_w_in"][l, k])
            w2 = inp["ffn_w_out"][l, k].reshape(FT, P, KT, P)
            n0 = 0
            for nh in HIDDEN:
                for n in range(n0, n0 + nh):
                    ffn += [a_b[n], a_b[FT + n]]
                part = np.zeros((KT, P, KT, P), w2.dtype)
                part[:, :, 0:nh] = w2[n0:n0 + nh].transpose(2, 1, 0, 3)
                ffn += list(part.reshape(KT, P, UNIT))
                n0 += nh
    a["ffn"] = np.stack(ffn).reshape(LAYERS, 2, FFN_UNITS, P, UNIT)
    a["w_mix"] = np.stack([np.concatenate([blocks(inp["w_in"][l][:, 0:2 * D]), rows(inp["w_in"][l][:, 2 * D:]),
                                           blocks(inp["w_out"][l])]) for l in range(LAYERS)])
    x = np.concatenate([inp["x"][0], inp["ctx"][0]])
    a["x"] = x.T.reshape(KT, P, T2).transpose(1, 0, 2)
    cc = np.stack([vec(inp["c"][0]), vec(inp["c_ctx"])], axis=2).reshape(P, KT * 2)
    parts = {"cc": cc, "c2": vec(inp["c_2"][0]), "b_mod": vec(inp["b_mod"]), "norm_g": vec(inp["norm_g"]),
             "final_g": vec(inp["final_g"]), "conv_w": vec(inp["conv_w"]), "pool_scale": vec(inp["pool_scale"]),
             "b_ada": vec(inp["b_ada_2"]), "g_mix": vec(inp["g_norm_mix_2"]), "g_ffn": vec(inp["g_norm_ffn_2"]),
             "g_final": vec(inp["g_norm_final_2"]), "b_cmp_k": vec(inp["b_cmp_k1_2"]), "b_cmp_v": vec(inp["b_cmp_v1_2"]),
             "pe_k": vec(inp["pe_cmp_k_2"]), "pe_v": vec(inp["pe_cmp_v_2"])}
    a["cols"] = np.concatenate([parts[n] for n in COLS], axis=1)
    assert a["cols"].shape[1] == N_COLS
    rpb = np.zeros((LAYERS, NA_H, 7, 2 * GRID - 1), inp["rpb"].dtype)
    rpb[..., GRID - 16:GRID + 15] = inp["rpb"][:, :, 4:11, :]
    t = np.stack([rpb[..., GRID - 1 - q:2 * GRID - 1 - q] for q in range(GRID)], axis=1)
    a["rel_bias"] = np.concatenate([t[:, :, :, 1:7], t[:, :, :, 0:6]], axis=1).reshape(LAYERS, P, NA_H * BIAS_ROWS * GRID)
    pw = np.zeros((LAYERS, 2, 2, 64, 2, 64), inp["pool_w"].dtype)
    for g in range(4):
        pw[:, g // 2, g % 2, :, g % 2, :] = inp["pool_w"][:, g]
    a["pool_w"] = pw.reshape(LAYERS, 2, P, P).transpose(0, 2, 1, 3)
    cnt = np.zeros((4, S), f)
    for g, w in enumerate((2, 4, 8, 16)):
        tt = np.arange(S)
        cnt[g] = np.clip(tt + w - w // 2, 0, S) - np.clip(tt - w // 2, 0, S)
    a["pool_inv"] = np.repeat((f(1) / cnt).reshape(2, 2, 1, S), 64, axis=2).reshape(2, P, S).transpose(1, 0, 2)

    w = inp["w_in_2"][0]
    cut = np.split(w, np.cumsum([512, 512, 512, 512, 512, 128, 128, 128, 128, 128, 128, 24])[:-1], axis=1)
    rq, rk, rv, rg, nq, kc, vc, ks, vs, kw, vw, gate = cut
    nq = nq.reshape(D, 2, 4, 64).transpose(0, 2, 1, 3).reshape(D, 512)
    gate = np.concatenate([gate.reshape(D, 2, 4, 3).transpose(0, 2, 1, 3).reshape(D, 24), np.zeros((D, 232), w.dtype)], axis=1)
    fm = np.concatenate([rq, rk, nq, kc, ks, kw, vc, rg], axis=1)
    tm = rows(np.concatenate([vs, vw, gate], axis=1))
    wo = inp["w_out_2"][0]
    wo = np.concatenate([wo[:512], wo[512:].reshape(2, 4, 64, D).transpose(1, 0, 2, 3).reshape(512, D)])
    a["subkeys"] = inp["peer_subkeys_2"][0].reshape(16, NK, P).transpose(2, 0, 1).reshape(P, 16 * NK)
    a["w_second"] = np.concatenate([blocks(fm), rows(rv), tm, blocks(wo), blocks(inp["w_peer_q_2"][0])])
    down = inp["peer_down_2"][0].reshape(NK, NK, KT, P).transpose(1, 3, 2, 0).reshape(NK, P, UNIT)
    up = inp["peer_up_2"][0].reshape(NK, NK, D).transpose(1, 0, 2)
    order = [down[0], down[1]]
    for k in range(NK):
        order += [up[k]] + ([down[k + 2]] if k + 2 < NK else [])
    a["experts"] = np.stack(order)
    for k, nm in (("k", "w_cmp_k"), ("v", "w_cmp_v")):
        w1 = inp[f"{nm}1_2"][0].reshape(16, P, 256).transpose(1, 0, 2)
        w2 = inp[f"{nm}2_2"][0].reshape(2, P, 64).transpose(1, 0, 2)
        a[f"cmp_{k}1"], a[f"cmp_{k}2"] = w1, w2

    tab = {}
    for dim, name in ((128, "128"), (64, "64")):
        inv = f(10000.0) ** (-np.arange(0, dim, 2, dtype=f) / f(dim))
        ang = np.arange(S, dtype=f)[None, :] * inv[:, None]
        tab["cos" + name] = np.tile(np.cos(ang).astype(f), (P // (dim // 2), 1))
        tab["sin" + name] = np.tile(np.sin(ang).astype(f), (P // (dim // 2), 1))
        perm = np.zeros((P, P), f)
        for m in range(P):
            half = dim // 2
            if m % dim < half:
                perm[m + half, m] = -1
            else:
                perm[m - half, m] = 1
        tab["perm" + name] = perm
    log_g = np.log1p(-np.exp2(f(-5.0) - np.arange(RET_H, dtype=f))).astype(f)
    diff = np.arange(S, dtype=f)[None, :] - np.arange(P, dtype=f)[:, None]
    dec = np.where(diff >= 0, np.exp(np.where(diff >= 0, diff, 0)[None] * log_g[:, None, None]), 0).astype(f)
    tab["decay"] = (dec * f(128 ** -0.5)).transpose(1, 0, 2).reshape(P, RET_H * S)
    q = np.arange(P)
    tab["causal"] = np.concatenate([np.zeros((P, P), f), np.where(q[None, :] <= q[:, None], 0, NEG).astype(f)], axis=1)
    n = np.arange(16)
    ok = np.stack([(CMP_STRIDE * n[None, :] + CMP_LEN - 1 <= q[:, None] + P * qt) & (n[None, :] < NCB) for qt in range(2)], axis=1)
    tab["cmp_add"] = np.where(ok, 0, NEG).astype(f).reshape(P, 32)
    tab["cmp_mask"] = ok.astype(f).reshape(P, 32)
    a["tables"] = np.concatenate([tab[n] for n in TAB], axis=1)
    assert a["tables"].shape[1] == N_TAB
    return {k: np.ascontiguousarray(v) for k, v in a.items()}


def kernel(**inputs):
    import concourse.bacc as bacc
    from concourse.bass_utils import run_bass_kernel_spmd

    arrays = _layout({k: np.asarray(v) for k, v in inputs.items()})
    nc = bacc.Bacc("TRN2", target_bir_lowering=False, num_devices=1)
    dram = {k: nc.dram_tensor(f"in_{k}", v.shape, mybir.dt.from_np(v.dtype), kind="ExternalInput").ap()
            for k, v in arrays.items()}
    out = nc.dram_tensor("out_x", (P, KT, S), F32, kind="ExternalOutput").ap()
    build(nc, dram, out)
    r = run_bass_kernel_spmd(nc, [{f"in_{k}": v for k, v in arrays.items()}], core_ids=[0])
    return r.results[0]["out_x"].transpose(2, 1, 0).reshape(1, S, D)
```

```python
from contextlib import ExitStack

import numpy as np

import concourse.bass as bass
from concourse import mybir

F32 = mybir.dt.float32
F32R = mybir.dt.float32r
U32 = mybir.dt.uint32
ALU = mybir.AluOpType
ACT = mybir.ActivationFunctionType
AX = mybir.AxisListType.X

P = 128
D = 1024
KT = D // P
S = 256
T2 = 2 * S
LAYERS = 2
D_FF = 2816
FT = D_FF // P
N_MOD = 9
LAYER_UNITS = N_MOD * KT // 2
MOD_UNITS = LAYERS * LAYER_UNITS + 6 * KT // 2
EPS = 1e-6
NEG = -1e30
TINY = float(np.finfo(np.float32).tiny)
NS = 4
UNIT = KT * P
HALF = UNIT // 2
MOD_UNIT = 2 * UNIT
HIDDEN = (8, 8, 6)
FFN_UNITS = 2 * FT + KT * len(HIDDEN)

CH_B, CH_C, CH_POOL, CH_Q, CH_K = 2, 4, 6, 8, 12
NA_H, DH = 8, 64
GRID = 64
BIAS_ROWS = 6
R_Q, R_K, N_Q, N_KC, N_KS, N_KW, N_VC, R_G = 0, 4, 8, 12, 13, 14, 15, 16
N_PROJ = 20
ROPE_WIDE, ROPE_ALL = 8, 15
RET_H = 4
NSA_H, NSA_G = 8, 2
CMP_LEN, CMP_STRIDE = 32, 16
NCB = (S - CMP_LEN) // CMP_STRIDE + 1
PH, TOPK, NK = 8, 16, 128
SLOTS = PH * TOPK

COLS = {}


def _columns():
    at = 0
    for name, n in [("cc", KT * 2), ("c2", KT), ("b_mod", LAYERS * N_MOD * KT), ("norm_g", LAYERS * 3 * KT),
                    ("final_g", KT), ("conv_w", LAYERS * 3 * 2), ("pool_scale", LAYERS * 2),
                    ("b_ada", 6 * KT), ("g_mix", KT), ("g_ffn", KT), ("g_final", KT),
                    ("b_cmp_k", 2), ("b_cmp_v", 2), ("pe_k", CMP_LEN // 2), ("pe_v", CMP_LEN // 2)]:
        COLS[name] = (at, n)
        at += n
    return at


N_COLS = _columns()
TAB = {}


def _tables():
    at = 0
    for name, n in [("cos128", S), ("sin128", S), ("cos64", S), ("sin64", S), ("perm128", P), ("perm64", P),
                    ("decay", RET_H * S), ("causal", S), ("cmp_add", 2 * 16), ("cmp_mask", 2 * 16)]:
        TAB[name] = (at, n)
        at += n
    return at


N_TAB = _tables()


class Signal:

    def __init__(self, ctx, nc, name):
        self.sem = ctx.enter_context(nc.semaphore(name))
        self.base = 0

    def at(self, n):
        return n + self.base

    def passed(self, n):
        self.base += n


class Stream:

    def __init__(self, ctx, nc, segments):
        self.nc, self.segments = nc, segments
        self.ring = ctx.enter_context(nc.sbuf_tensor("weight_ring", [P, NS, UNIT], F32))
        self.hi = ctx.enter_context(nc.sbuf_tensor("weight_hi", [P, 2, UNIT], F32R))
        self.lo = ctx.enter_context(nc.sbuf_tensor("weight_lo", [P, 2, UNIT], F32R))
        self.loaded = [ctx.enter_context(nc.semaphore(f"unit_loaded{s}")) for s in range(NS)]
        self.rounded = ctx.enter_context(nc.semaphore("unit_rounded"))
        self.split = ctx.enter_context(nc.semaphore("unit_split"))
        self.used = ctx.enter_context(nc.semaphore("unit_used"))
        self.total = sum(n for _, n in segments)
        self.g0 = 0

    def used_at(self, k):
        return 2 * k + 2 * (self.g0 + 1)

    def round(self, act, c, j, halves=(0, 1)):
        g = self.g0 + j
        for i in halves:
            if i == 0:
                act.wait_ge(self.loaded[g % NS], 16 * (c + (g // NS + 1)))
            if not (static(c) and NS * c + g < 2):
                act.wait_ge(self.used, 2 * NS * c + (2 * g + i - 3))
            h = slice(i * HALF, (i + 1) * HALF)
            nc = self.nc
            nc.scalar.activation(self.hi[:, g % 2, h], self.ring[:, g % NS, h], ACT.Copy).then_inc(self.rounded, 1)

    def subtract(self, dve, c, j, halves=(0, 1)):
        g = self.g0 + j
        for i in halves:
            dve.wait_ge(self.rounded, 2 * NS * c + (2 * g + i + 1))
            h = slice(i * HALF, (i + 1) * HALF)
            self.nc.vector.tensor_tensor(self.lo[:, g % 2, h], self.ring[:, g % NS, h], self.hi[:, g % 2, h].bitcast(F32),
                                         ALU.subtract).then_inc(self.split, 1)

    def half(self, pe, c, j, i):
        g = self.g0 + j
        pe.wait_ge(self.split, 2 * NS * c + (2 * g + i + 1))
        h = slice(i * HALF, (i + 1) * HALF)
        return self.hi[:, g % 2, h], self.lo[:, g % 2, h]

    def chunk(self, pe, c, j, out, x, n=KT, ready=None, before=0):
        for i in range(2):
            w_hi, w_lo = self.half(pe, c, j, i)
            for kt in range(KT // 2 * i, min(KT // 2 * (i + 1), n)):
                if ready:
                    pe.wait_ge(ready.sem, ready.at(before + kt + 1))
                b = slice(kt * P - i * HALF, (kt + 1) * P - i * HALF)
                last = product(self.nc, out, [((w_hi[:, b], w_lo[:, b]), x(kt))], start=(kt == 0), stop=(kt == n - 1))
            last.then_inc(self.used, 1)

    def load(self, eng, lo, hi):
        hi = min(hi, self.total)
        first = 0
        for src, n in self.segments:
            a, b = max(lo, first), min(hi, first + n)
            if a < b:
                cycles = (b - a) // NS if a >= NS and (b - a) // NS >= 2 else 0
                if cycles:
                    with eng.Fori(0, cycles) as i:
                        for j in range(NS):
                            eng.wait_ge(self.split, 2 * NS * i + 2 * (a + j - NS + 1))
                            eng.dma_start(self.ring[:, (a + j) % NS, :], src[NS * i + (a + j - first)])\
                               .then_inc(self.loaded[(a + j) % NS], 16)
                for g in range(a + NS * cycles, b):
                    if g >= NS:
                        eng.wait_ge(self.split, 2 * (g - NS + 1))
                    eng.dma_start(self.ring[:, g % NS, :], src[g - first]).then_inc(self.loaded[g % NS], 16)
            first += n

    def load_ahead(self, eng, n):
        self.load(eng, NS if self.g0 == 0 else self.g0 + NS + 2, self.g0 + n + NS + 2)


def product(nc, out, pairs, start=True, stop=True):
    for n, ((a_hi, a_lo), (b_hi, b_lo)) in enumerate(pairs):
        nc.tensor.matmul(out, a_hi, b_hi, start=start and n == 0, stop=False)
        nc.tensor.matmul(out, a_hi, b_lo, start=False, stop=False)
        last = nc.tensor.matmul(out, a_lo, b_hi, start=False, stop=stop and n == len(pairs) - 1)
    return last


def split_activations(nc, hi, lo, x):
    first = nc.vector.tensor_copy(hi, x)
    return first, lambda: nc.vector.tensor_tensor(lo, x, hi.bitcast(F32), ALU.subtract)


def over_units(eng, n, body):
    for j in range(min(NS, n)):
        body(0, j)
    whole = n // NS
    if whole > 1:
        with eng.Fori(1, whole) as c:
            for j in range(NS):
                body(c, j)
    if whole:
        for j in range(n - whole * NS):
            body(whole, j)


def static(c):
    return isinstance(c, int)


class Chip:

    def __init__(self, ctx, nc, dram):
        def sb(name, shape, dt=F32):
            return ctx.enter_context(nc.sbuf_tensor(name, shape, dt))

        def sig(name):
            return Signal(ctx, nc, name)

        self.nc, self.dram, self.extra = nc, dram, {}
        self.bank = [ctx.enter_context(nc.psum_tensor(f"bank{b}", [P, 512], F32)) for b in range(8)]
        self.x2 = sb("x2", [P, KT, S])
        self.cols = sb("cols", [P, N_COLS])
        self.silu_c = sb("silu_c", [P, KT, 2])
        self.silu_c2 = sb("silu_c2", [P, KT])
        self.mod_sums = sb("mod_sums", [P, MOD_UNITS, 4])
        self.mods = [sb(f"mod{l}", [P, N_MOD * KT, 2]) for l in range(LAYERS)]
        self.gains = [sb(f"gain{l}", [P, 3, KT, 2]) for l in range(LAYERS)]
        self.half_gates = [sb(f"half_gate{l}", [P, 2, KT, 2]) for l in range(LAYERS)]
        self.mod2 = sb("mod2", [P, 6 * KT])
        self.gain2 = sb("gain2", [P, 2, KT])
        self.ident = sb("ident", [P, P])
        self.ones = sb("ones", [P, P])
        self.eps = sb("eps", [P, 1])

        self.squared, self.summed, self.rooted = sig("squared"), sig("summed"), sig("rooted")
        self.scaled, self.h_ready = sig("scaled"), sig("h_ready")
        self.dve_step, self.act_step, self.pool_step = sig("dve_step"), sig("act_step"), sig("pool_step")
        self.table = sig("table")
        self.product, self.copied, self.added = sig("product"), sig("copied"), sig("added")
        self.silu_done, self.gated = sig("silu_done"), sig("gated")
        self.mod_loaded = [sig("mod_loaded0"), sig("mod_loaded1")]
        self.hot0, self.hot1, self.spread, self.kept = sig("hot0"), sig("hot1"), sig("spread"), sig("kept")
        self.columns_there = sig("columns_there")
        self.mod_first = [sig(f"mod_first{n}") for n in range(4)]
        self.mod_step, self.mod_summed, self.mod_diag = sig("mod_step"), sig("mod_summed"), sig("mod_diag")
        self.nmax, self.rsum = sb("nmax", [P, 4]), sb("rsum", [P, 4])
        self.gates = sb("gates", [P, 2, 24])
        self.nmax4, self.rsum4 = sb("nmax4", [P, 4, 2]), sb("rsum4", [P, 4, 2])
        self.iota = sb("iota", [P, P])
        self.split_in = sig("split_in")
        self.ffn_step = sig("ffn_step")
        self.gelu_done = sig("gelu_done")
        self.scored, self.scores_read, self.maxed = sig("scored"), sig("scores_read"), sig("maxed")
        self.exped, self.probs, self.turned = sig("exped"), sig("probs"), sig("turned")
        self.moved, self.mixed = sig("moved"), sig("mixed")

    def col(self, name, at=0, n=None):
        lo, size = COLS[name]
        return self.cols[:, lo + at:lo + (size if n is None else at + n)]

    def take(self, ctx, width, words):
        sb = lambda name, shape, dt: ctx.enter_context(self.nc.sbuf_tensor(f"{name}_{width}", shape, dt))
        self.hi, self.lo = sb("operand_hi", [P, KT, width], F32R), sb("operand_lo", [P, KT, width], F32R)
        self.arena, self.words = sb("arena", [P, words], F32), words

    def take_more(self, ctx, name, words=0, **more):
        sb = lambda n, shape, dt: ctx.enter_context(self.nc.sbuf_tensor(f"{n}_{name}", shape, dt))
        if words:
            self.extension = sb("extension", [P, words], F32)
        for buffer, (shape, dt) in more.items():
            self.extra[buffer] = sb(buffer, shape, dt)

    def part(self, at, *shape):
        n = int(np.prod(shape))
        if at < self.words:
            assert at + n <= self.words
            flat = self.arena[:, at:at + n]
        else:
            flat = self.extension[:, at - self.words:at - self.words + n]
        if len(shape) == 1:
            return flat
        if len(shape) == 2:
            return flat.rearrange("p (a b) -> p a b", b=shape[1])
        return flat.rearrange("p (a b c) -> p a b c", b=shape[1], c=shape[2])


A_X, A_H, A_RSTD = 0, 4096, 8192
A_Y = A_H
A_WORDS = A_RSTD + 1024
A_U = A_WORDS
A_V = A_U + 8192
A_BIAS = A_V + 2048
A_SC = A_BIAS + NA_H * BIAS_ROWS * GRID
A_PT = A_SC + 2048
A_POOL = A_PT + 2048
A_MIXER = A_POOL + 2048 - A_WORDS
A_MOD = A_WORDS
A_GATE = A_MOD + 2 * MOD_UNIT + 1024 + 4 * P
A_FFN = A_GATE + 2 * T2 - A_WORDS


def in_order(eng, signal, instruction):
    signal.passed(1)
    instruction.then_inc(signal.sem, 1)
    eng.wait_ge(signal.sem, signal.base)


class Norm:
    def __init__(self, chip, x, h, root, rstd, gain, shift, groups, width, split=True):
        self.chip, self.x, self.h, self.root, self.rstd = chip, x, h, root, rstd
        self.gain, self.shift, self.groups, self.t = gain, shift, groups, width
        self.split = split

    def scalar(self, act):
        c, nc, t = self.chip, self.chip.nc, self.t
        for kt in range(KT):
            nc.scalar.activation(self.h[:, kt, 0:t], self.x[:, kt, 0:t], ACT.Square).then_inc(c.squared.sem, 1)
        act.wait_ge(c.summed.sem, c.summed.at(1))
        nc.scalar.activation(self.root[:, 0:t], c.bank[7][:, 0:t], ACT.Sqrt, bias=self.chip.eps[:, 0:1], scale=1.0 / D)\
            .then_inc(c.rooted.sem, 1)
        for kt in range(KT):
            act.wait_ge(c.scaled.sem, c.scaled.at(kt + 1))
            for g, (lo, hi) in enumerate(self.groups):
                shift = 0.0 if self.shift is None else self.shift(kt, g)
                last = nc.scalar.activation(self.h[:, kt, lo:hi], self.h[:, kt, lo:hi], ACT.Identity,
                                            bias=shift, scale=self.gain(kt, g))
            last.then_inc(c.h_ready.sem, 1)

    def tensor(self, pe):
        c, nc, t = self.chip, self.chip.nc, self.t
        for kt in range(KT):
            pe.wait_ge(c.squared.sem, c.squared.at(kt + 1))
            last = nc.tensor.matmul(c.bank[7][:, 0:t], c.ones[:, :], self.h[:, kt, 0:t],
                                    start=(kt == 0), stop=(kt == KT - 1))
        last.then_inc(c.summed.sem, 1)

    def vector(self, dve):
        c, nc, t = self.chip, self.chip.nc, self.t
        dve.wait_ge(c.rooted.sem, c.rooted.at(1))
        in_order(dve, c.dve_step, nc.vector.reciprocal(self.rstd[:, 0:t], self.root[:, 0:t]))
        for kt in range(KT):
            nc.vector.tensor_tensor(self.h[:, kt, 0:t], self.x[:, kt, 0:t], self.rstd[:, 0:t], ALU.mult)\
                .then_inc(c.scaled.sem, 1)
            if self.split and kt:
                self.parts(dve, kt - 1)
        if self.split:
            self.parts(dve, KT - 1)

    def parts(self, dve, kt):
        c, nc, t = self.chip, self.chip.nc, self.t
        dve.wait_ge(c.h_ready.sem, c.h_ready.at(kt + 1))
        first, rest = split_activations(nc, c.hi[:, kt, 0:t], c.lo[:, kt, 0:t], self.h[:, kt, 0:t])
        in_order(dve, c.dve_step, first)
        rest().then_inc(c.split_in.sem, 1)

    def end(self):
        c = self.chip
        c.squared.passed(KT)
        c.summed.passed(1)
        c.rooted.passed(1)
        c.scaled.passed(KT)
        c.h_ready.passed(KT)
        if self.split:
            c.split_in.passed(KT)


def stage_setup(chip, stream):
    nc, d = chip.nc, chip.dram
    x = chip.part(A_X, KT, T2)
    with nc.Block() as block:
        @block.sync
        def _(sp):
            sp.dma_start(chip.cols[:, :], d["cols"]).then_inc(chip.table.sem, 16)
            sp.dma_start(x, d["x"]).then_inc(chip.table.sem, 16)
            stream.load(sp, 0, NS)
            sp.wait_ge(chip.table.sem, 32)

        @block.gpsimd
        def _(pool):
            nc.gpsimd.memset(chip.ones[:, :], 1.0)
            nc.gpsimd.memset(chip.eps[:, :], EPS)
            in_order(pool, chip.pool_step, nc.gpsimd.memset(chip.ident[:, :], 0.0))
            in_order(pool, chip.pool_step, nc.gpsimd.affine_select(
                out=chip.ident[:, :], in_=chip.ident[:, :], compare_op=ALU.not_equal, fill=1.0, base=0,
                pattern=[[-1, P]], channel_multiplier=1))

        @block.scalar
        def _(act):
            act.wait_ge(chip.table.sem, 32)
            nc.scalar.activation(chip.silu_c[:, :, :].rearrange("p a b -> p (a b)"), chip.col("cc"), ACT.Silu)\
                .then_inc(chip.act_step.sem, 1)
            nc.scalar.activation(chip.silu_c2[:, :], chip.col("c2"), ACT.Silu).then_inc(chip.act_step.sem, 1)
            act.wait_ge(chip.act_step.sem, 2)
            for j in range(2):
                stream.round(act, 0, j)

        @block.vector
        def _(dve):
            for j in range(2):
                stream.subtract(dve, 0, j)
    chip.table.passed(32)
    chip.act_step.passed(2)


class Modulation:

    def __init__(self, chip, first, n, groups, at=A_MOD):
        self.chip, self.first, self.n, self.groups = chip, first, n, groups
        self.steps = KT * groups
        self.w = chip.part(at, 2, MOD_UNIT)
        self.acc = chip.part(at + 2 * MOD_UNIT, 2, 512)
        self.diag = chip.part(at + 2 * MOD_UNIT + 1024, 2 * groups, P)

    def load(self, eng):
        c = self.chip
        for l in range(2):
            eng.dma_start(self.w[:, l, :], c.dram["w_mods"][self.first + l]).then_inc(c.mod_loaded[l].sem, 16)
        with eng.Fori(1, self.n // 2) as i:
            for j in range(2):
                eng.wait_ge(c.mod_step.sem, c.mod_step.at(2 * self.steps * i + self.steps * (j - 1)))
                eng.dma_start(self.w[:, j, :], c.dram["w_mods"][2 * i + (self.first + j)]).then_inc(c.mod_loaded[j].sem, 16)

    def accumulate(self, dve, i, j, l, lo=0, hi=KT):
        c, nc = self.chip, self.chip.nc
        if lo == 0:
            dve.wait_ge(c.mod_loaded[j].sem, c.mod_loaded[j].at(16 * i + 16))
        for kt in range(lo, hi):
            for g in range(self.groups):
                w, acc = self.w[:, j, kt * 256:(kt + 1) * 256], self.acc[:, j, g * 256:(g + 1) * 256]
                scale = c.silu_c[:, kt, g:g + 1] if self.groups == 2 else c.silu_c2[:, kt:kt + 1]
                if kt == 0:
                    ins = nc.vector.tensor_scalar(acc, w, scale, None, ALU.mult)
                else:
                    dve.wait_ge(c.mod_step.sem, c.mod_step.at(self.steps * l + ((kt - 1) * self.groups + g + 1)))
                    ins = nc.vector.scalar_tensor_tensor(acc, w, scale, acc, ALU.mult, ALU.add)
                ins.then_inc(c.mod_step.sem, 1)

    def sum(self, pe, j, l):
        c, nc = self.chip, self.chip.nc
        pe.wait_ge(c.mod_step.sem, c.mod_step.at(self.steps * l + self.steps))
        n = 256 * self.groups
        nc.tensor.matmul(c.bank[6 + j][:, 0:n], c.ones[:, :], self.acc[:, j, 0:n], start=True, stop=True)\
            .then_inc(c.mod_summed.sem, 1)

    def keep(self, dve, j, l):
        c, nc = self.chip, self.chip.nc
        blocks = 2 * self.groups
        if not (static(l) and l == 0):
            dve.wait_ge(c.mod_diag.sem, c.mod_diag.at(2 * l))
        dve.wait_ge(c.mod_summed.sem, c.mod_summed.at(l + 1))
        nc.vector.tensor_tensor(self.diag, c.bank[6 + j][:, 0:blocks * P].rearrange("p (b m) -> p b m", m=P),
                                c.ident[:, :].unsqueeze(1).to_broadcast([P, blocks, P]), ALU.mult).then_inc(c.mod_diag.sem, 1)
        dve.wait_ge(c.mod_diag.sem, c.mod_diag.at(2 * l + 1))
        nc.vector.tensor_reduce(c.mod_sums[:, l + self.first, 0:blocks], self.diag, AX.X, ALU.add)\
            .then_inc(c.mod_diag.sem, 1)

    def end(self):
        c = self.chip
        for s in c.mod_loaded:
            s.passed(16 * (self.n // 2))
        c.mod_step.passed(self.steps * self.n)
        c.mod_summed.passed(self.n)
        c.mod_diag.passed(2 * self.n)


def finish_mod(chip, dve, layer, lo, hi):
    nc = chip.nc
    mod, gain, half_gate = chip.mods[layer], chip.gains[layer], chip.half_gates[layer]
    u0 = layer * LAYER_UNITS
    for b in range(2):
        src = chip.mod_sums[:, u0 + lo * KT // 2:u0 + hi * KT // 2, :].rearrange("p u (g b) -> p u g b", b=2)[:, :, :, b]
        bias = chip.col("b_mod", layer * N_MOD * KT + lo * KT + b, (hi - lo) * KT - b)[:, ::2]
        last = nc.vector.tensor_tensor(mod[:, lo * KT + b:hi * KT:2, :], src,
                                       bias.unsqueeze(2).to_broadcast([P, (hi - lo) * KT // 2, 2]), ALU.add)
    in_order(dve, chip.dve_step, last)
    for i in range(lo // 3, hi // 3):
        g = chip.col("norm_g", (layer * 3 + i) * KT, KT).unsqueeze(2).to_broadcast([P, KT, 2])
        last = nc.vector.scalar_tensor_tensor(gain[:, i, :, :], mod[:, (3 * i + 1) * KT:(3 * i + 2) * KT, :],
                                              1.0, g, ALU.add, ALU.mult)
        if i != 1:
            last = nc.vector.tensor_scalar(half_gate[:, i // 2, :, :], mod[:, (3 * i + 2) * KT:(3 * i + 3) * KT, :],
                                           0.5, None, ALU.mult)
    in_order(dve, chip.dve_step, last)


def finish_mod2(chip, dve):
    nc = chip.nc
    src = chip.mod_sums[:, LAYERS * LAYER_UNITS:MOD_UNITS, 0:2]
    in_order(dve, chip.dve_step, nc.vector.tensor_tensor(
        chip.mod2[:, :].rearrange("p (u b) -> p u b", b=2), src, chip.col("b_ada").rearrange("p (u b) -> p u b", b=2), ALU.add))
    for i, g in enumerate(("g_mix", "g_ffn")):
        in_order(dve, chip.dve_step, nc.vector.scalar_tensor_tensor(
            chip.gain2[:, i, :], chip.mod2[:, (3 * i + 1) * KT:(3 * i + 2) * KT], 1.0, chip.col(g), ALU.add, ALU.mult))


def stage_first_mod(chip):
    nc, units, slots = chip.nc, 3 * KT // 2, 4
    w = [chip.part(at + MOD_UNIT * i, MOD_UNIT) for at in (A_H, A_MOD) for i in range(2)]
    rows = chip.part(A_GATE, 2, 256)
    with nc.Block() as block:
        @block.gpsimd
        def _(pool):
            for l in range(units):
                if l >= slots:
                    pool.wait_ge(chip.mod_summed.sem, chip.mod_summed.at(l - slots + 1))
                pool.dma_start(w[l % slots], chip.dram["w_mods"][l]).then_inc(chip.mod_first[l % slots].sem, 16)

        @block.tensor
        def _(pe):
            def turn(l):
                pe.wait_ge(chip.copied.sem, chip.copied.at(l + 1))
                for b in range(2):
                    last = nc.tensor.transpose(chip.bank[2][:, 4 * l + 2 * b:4 * l + 2 * b + 2],
                                               rows[0:2, l % 2, b * P:(b + 1) * P], chip.ident[0:2, 0:2])
                last.then_inc(chip.turned.sem, 1)

            for l in range(units):
                pe.wait_ge(chip.mod_first[l % slots].sem, chip.mod_first[l % slots].at(16 * (l // slots + 1)))
                if l >= 2:
                    pe.wait_ge(chip.copied.sem, chip.copied.at(l - 1))
                for kt in range(KT):
                    last = nc.tensor.matmul(chip.bank[l % 2][0:2, 0:256], chip.silu_c[:, kt, :],
                                            w[l % slots][:, kt * 256:(kt + 1) * 256], start=(kt == 0), stop=(kt == KT - 1))
                last.then_inc(chip.mod_summed.sem, 1)
                if l:
                    turn(l - 1)
            turn(units - 1)

        @block.scalar
        def _(act):
            for l in range(units):
                act.wait_ge(chip.mod_summed.sem, chip.mod_summed.at(l + 1))
                if l >= 2:
                    act.wait_ge(chip.turned.sem, chip.turned.at(l - 1))
                nc.scalar.activation(rows[0:2, l % 2, :], chip.bank[l % 2][0:2, 0:256], ACT.Copy)\
                    .then_inc(chip.copied.sem, 1)

        @block.vector
        def _(dve):
            dve.wait_ge(chip.turned.sem, chip.turned.at(units))
            for b in range(2):
                dst = chip.mod_sums[:, 0:units, :].rearrange("p u (g b) -> p u g b", b=2)[:, :, :, b]
                src = chip.bank[2][:, 0:4 * units].rearrange("p (u b g) -> p u b g", b=2, g=2)[:, :, b, :]
                last = nc.vector.tensor_copy(dst, src)
            in_order(dve, chip.dve_step, last)
            finish_mod(chip, dve, 0, 0, 3)
    for signal in chip.mod_first:
        signal.passed(16 * units // slots)
    for signal in (chip.mod_summed, chip.copied, chip.turned):
        signal.passed(units)


def norm1(chip, layer, i, width):
    groups = [(0, S), (S, T2)][:width // S]
    return Norm(chip, chip.part(A_X, KT, T2), chip.part(A_H, KT, T2), chip.part(A_RSTD + 512, 512), chip.part(A_RSTD, 512),
                lambda kt, g: chip.gains[layer][:, i, kt, g:g + 1],
                lambda kt, g: chip.mods[layer][:, 3 * i * KT + kt, g:g + 1],
                groups, width)


def take_for_ffn(chip, ctx, name):
    part = ([P, max(HIDDEN), T2], F32R)
    chip.take_more(ctx, name, A_FFN, hidden_hi=part, hidden_lo=part)


def stage_ffn(chip, stream, layer, which, width, work=None, finish=None):
    nc, t = chip.nc, width
    norm = norm1(chip, layer, 2 * which, width)
    x = chip.part(A_X, KT, T2)
    hid_hi, hid_lo = chip.extra["hidden_hi"], chip.extra["hidden_lo"]
    gate_buf = chip.part(A_GATE, 2, T2)
    beside = {None: (0, 0, 0), FT + 2: (0, 0, 2), FT + KT: (3, 3, 2)}[work.n if work else None]
    parts, u = [], 0
    for i, n in enumerate(HIDDEN):
        parts.append((sum(HIDDEN[:i]), n, u, i * KT, sum(beside[:i]), beside[i]))
        u += 2 * n + KT

    with nc.Block() as block:
        @block.sync
        def _(sp):
            stream.load_ahead(sp, FFN_UNITS)

        if work:
            block.gpsimd(work.load)

        @block.tensor
        def _(pe):
            norm.tensor(pe)
            for n0, nh, u0, r0, extra, more in parts:
                def up(c, j):
                    n, half = 2 * c + (n0 + j // 2), j % 2
                    if half == 0 and not (static(c) and n < 2):
                        pe.wait_ge(chip.gated.sem, chip.gated.at(n - 1))
                    first = static(c) and u0 + NS * c + j == 0
                    stream.chunk(pe, c, u0 + j, chip.bank[2 * (j // 2) + half][:, 0:t],
                                 lambda kt: (chip.hi[:, kt, 0:t], chip.lo[:, kt, 0:t]), ready=chip.split_in if first else None)
                    l = n + extra
                    if work and half and not (static(c) and l == 0):
                        work.sum(pe, (n0 + extra + j // 2 - 1) % 2, l - 1)
                over_units(pe, 2 * nh, up)
                for n in range(KT):
                    r = r0 + n
                    if r >= 2:
                        pe.wait_ge(chip.added.sem, chip.added.at(r - 1))
                    stream.chunk(pe, 0, u0 + 2 * nh + n, chip.bank[4 + n % 2][:, 0:t],
                                 lambda kt: (hid_hi[:, kt, 0:t], hid_lo[:, kt, 0:t]), n=nh,
                                 ready=None if n else chip.gated, before=n0)
                    if n % 3 == 1 and n // 3 < more:
                        l = n0 + nh + extra + n // 3
                        work.sum(pe, (l - 1) % 2, l - 1)
            if work:
                work.sum(pe, (work.n - 1) % 2, work.n - 1)

        @block.scalar
        def _(act):
            norm.scalar(act)
            for n0, nh, u0, r0, extra, more in parts:
                def silu(c, j):
                    stream.round(act, c, u0 + j + 2, [0])
                    if j % 2 == 0:
                        act.wait_ge(stream.used, stream.used_at(NS * c + (u0 + j)))
                        nc.scalar.activation(gate_buf[:, j // 2, 0:t], chip.bank[2 * (j // 2)][:, 0:t], ACT.Silu)\
                            .then_inc(chip.silu_done.sem, 1)
                    stream.round(act, c, u0 + j + 2, [1])
                over_units(act, 2 * nh, silu)
                for n in range(KT):
                    stream.round(act, 0, u0 + 2 * nh + n + 2)

        @block.vector
        def _(dve):
            norm.vector(dve)
            for n0, nh, u0, r0, extra, more in parts:
                def gate(c, j):
                    i = j // 2
                    n = 2 * c + (n0 + i)
                    stream.subtract(dve, c, u0 + j + 2, [0])
                    if j % 2:
                        g, hi, lo = gate_buf[:, i, 0:t], hid_hi[:, 2 * c + i, 0:t], hid_lo[:, 2 * c + i, 0:t]
                        dve.wait_ge(chip.silu_done.sem, chip.silu_done.at(n + 1))
                        dve.wait_ge(stream.used, stream.used_at(NS * c + (u0 + j)))
                        nc.vector.tensor_tensor(g, g, chip.bank[2 * i + 1][:, 0:t], ALU.mult).then_inc(chip.ffn_step.sem, 1)
                        dve.wait_ge(chip.ffn_step.sem, chip.ffn_step.at(2 * n + 1))
                        first, rest = split_activations(nc, hi, lo, g)
                        first.then_inc(chip.ffn_step.sem, 1)
                        dve.wait_ge(chip.ffn_step.sem, chip.ffn_step.at(2 * n + 2))
                        rest().then_inc(chip.gated.sem, 1)
                        stream.subtract(dve, c, u0 + j + 2, [1])
                    if work:
                        e, l = n0 + extra + i, n + extra
                        work.accumulate(dve, c + e // 2, e % 2, l, KT // 2 * (j % 2), KT // 2 * (j % 2 + 1))
                        if j % 2 and not (static(c) and l == 0):
                            work.keep(dve, (e - 1) % 2, l - 1)
                    if j % 2 == 0:
                        stream.subtract(dve, c, u0 + j + 2, [1])
                over_units(dve, 2 * nh, gate)
                for n in range(KT):
                    r = r0 + n
                    stream.subtract(dve, 0, u0 + 2 * nh + n + 2, [0])
                    dve.wait_ge(stream.used, stream.used_at(u0 + 2 * nh + n))
                    for g, (lo, hi) in enumerate(norm.groups):
                        last = nc.vector.scalar_tensor_tensor(x[:, n, lo:hi], chip.bank[4 + n % 2][:, lo:hi],
                                                              chip.half_gates[layer][:, which, n, g:g + 1], x[:, n, lo:hi],
                                                              ALU.mult, ALU.add)
                    last.then_inc(chip.added.sem, 1)
                    stream.subtract(dve, 0, u0 + 2 * nh + n + 2, [1])
                    if n % 3 < 2 and n // 3 < more:
                        l = n0 + nh + extra + n // 3
                        work.accumulate(dve, l // 2, l % 2, l, KT // 2 * (n % 3), KT // 2 * (n % 3 + 1))
                        if n % 3 == 1:
                            work.keep(dve, (l - 1) % 2, l - 1)
            if work:
                work.keep(dve, (work.n - 1) % 2, work.n - 1)
                dve.wait_ge(chip.mod_diag.sem, chip.mod_diag.at(2 * work.n))
                finish(dve)
    if work:
        work.end()
    norm.end()
    chip.ffn_step.passed(2 * FT)
    chip.silu_done.passed(FT)
    chip.gated.passed(FT)
    chip.added.passed(3 * KT)
    stream.g0 += FFN_UNITS


def stage_mix_in(chip, stream, layer, last):
    nc, d = chip.nc, chip.dram
    norm = norm1(chip, layer, 1, T2)
    hi, lo = chip.hi, chip.lo
    u, v = chip.part(A_U, 16, T2), chip.part(A_V, 4, 512)
    bias = chip.part(A_BIAS, NA_H * BIAS_ROWS * GRID)
    width = [S if last and n < CH_K else T2 for n in range(16)]
    with nc.Block() as block:
        @block.sync
        def _(sp):
            sp.dma_start(bias, d["rel_bias"][layer]).then_inc(chip.table.sem, 16)
            sp.dma_start(chip.extra["pool_w"][:, :, :], d["pool_w"][layer]).then_inc(chip.table.sem, 16)
            sp.dma_start(chip.extra["pool_inv"][:, :, :], d["pool_inv"]).then_inc(chip.table.sem, 16)
            stream.load_ahead(sp, 20)

        @block.gpsimd
        def _(pool):
            pool.wait_ge(chip.table.sem, chip.table.at(48))
            for half in range(2):
                b = bias[half * GRID:(half + 1) * GRID, :].rearrange("p (r k) -> p r k", k=GRID)
                lo, hi = b[:, :, 0:GRID - 16], b[:, :, 16:GRID]
                in_order(pool, chip.pool_step, nc.gpsimd.affine_select(
                    out=lo, in_=lo, compare_op=ALU.is_ge, fill=NEG, base=8,
                    pattern=[[0, NA_H * BIAS_ROWS], [1, GRID - 16]], channel_multiplier=-1))
                in_order(pool, chip.pool_step, nc.gpsimd.affine_select(
                    out=hi, in_=hi, compare_op=ALU.is_ge, fill=NEG, base=7 - 16,
                    pattern=[[0, NA_H * BIAS_ROWS], [-1, GRID - 16]], channel_multiplier=1))

        @block.tensor
        def _(pe):
            norm.tensor(pe)
            for n in range(16):
                if n >= 4:
                    pe.wait_ge(chip.copied.sem, chip.copied.at(n - 3))
                t = width[n]
                stream.chunk(pe, 0, n, chip.bank[n % 4][:, 0:t], lambda kt: (hi[:, kt, 0:t], lo[:, kt, 0:t]),
                             ready=chip.split_in if n == 0 else None)
            for n in range(4):
                for i in range(2):
                    w = stream.half(pe, 0, 16 + n, i)
                    for tt in range(4):
                        q, kt = slice(tt * P, (tt + 1) * P), 2 * n + i
                        mm = product(nc, chip.bank[4 + tt][:, :], [((hi[:, kt, q], lo[:, kt, q]), w)],
                                     start=(kt == 0), stop=(kt == KT - 1))
                    mm.then_inc(stream.used, 1)

        @block.scalar
        def _(act):
            norm.scalar(act)
            for n in range(16):
                stream.round(act, 0, n + 2, [0])
                act.wait_ge(stream.used, stream.used_at(n))
                nc.scalar.activation(u[:, n, 0:width[n]], chip.bank[n % 4][:, 0:width[n]], ACT.Copy)\
                    .then_inc(chip.copied.sem, 1)
                stream.round(act, 0, n + 2, [1])
            for n in range(4):
                stream.round(act, 0, 18 + n)
            act.wait_ge(stream.used, stream.used_at(19))
            for tt in range(4):
                nc.scalar.activation(v[:, tt, :], chip.bank[4 + tt][:, :], ACT.Copy)

        @block.vector
        def _(dve):
            norm.vector(dve)
            for n in range(20):
                stream.subtract(dve, 0, n + 2)
    norm.end()
    chip.table.passed(48)
    chip.copied.passed(16)
    stream.g0 += 20


def stage_mix(chip, stream, layer, last):
    nc = chip.nc
    u, v, y = chip.part(A_U, 16, T2), chip.part(A_V, 4, 512), chip.part(A_Y, KT, T2)
    bias = chip.part(A_BIAS, NA_H, BIAS_ROWS * GRID)
    sc, pt = chip.part(A_SC, 4, 512), chip.part(A_PT, 2, 4, S)
    ng = 1 if last else 2
    t = ng * S
    items = [(g, h, qt) for g in range(ng) for h in range(NA_H) for qt in range(2)]
    keys = lambda g: (0, T2) if g == 0 else (S, T2)

    with nc.Block() as block:
        @block.gpsimd
        def _(pool):
            eng = nc.gpsimd
            step = lambda ins: in_order(pool, chip.pool_step, ins)
            z = chip.part(A_POOL, ng, S + 2)
            acc, tmp = chip.part(A_POOL + 544, ng, S), chip.part(A_POOL + 1088, ng, S)
            step(eng.memset(z, 0.0))
            for b in range(2):
                uu = lambda n: u[:, n + b, 0:t].rearrange("p (g s) -> p g s", s=S)
                w = lambda k: chip.col("conv_w", (layer * 3 + k) * 2 + b, 1)
                step(eng.tensor_tensor(z[:, :, 1:S + 1], uu(CH_C), uu(0), ALU.mult))
                step(eng.tensor_scalar(acc, z[:, :, 0:S], w(0), None, ALU.mult))
                for k in (1, 2):
                    step(eng.tensor_scalar(tmp, z[:, :, k:k + S], w(k), None, ALU.mult))
                    step(eng.tensor_tensor(acc, acc, tmp, ALU.add))
                step(eng.tensor_tensor(y[:, b, 0:t].rearrange("p (g s) -> p g s", s=S), acc, uu(CH_B), ALU.mult))
            wide = S + 16
            a, c = chip.part(A_POOL, ng, wide), chip.part(A_POOL + 544, ng, wide)
            for b in range(2):
                vv = u[:, CH_POOL + b, 0:t].rearrange("p (g s) -> p g s", s=S)
                out = y[:, 2 + b, 0:t].rearrange("p (g s) -> p g s", s=S)
                step(eng.memset(a, 0.0))
                step(eng.tensor_copy(a[:, :, 8:8 + S], vv))
                src, dst = a, c
                for n in range(2 + 2 * b):
                    gap, at = 1 << n, (2 << n) - 1
                    step(eng.tensor_tensor(dst[:, :, at:wide], src[:, :, at:wide], src[:, :, at - gap:wide - gap], ALU.add))
                    src, dst = dst, src
                    if n >= 2 * b:
                        half, lo = n - 2 * b, 8 + gap - 1
                        q = slice(64 * half, 64 * half + 64)
                        inv = chip.extra["pool_inv"][q, b, :].unsqueeze(1).to_broadcast([64, ng, S])
                        step(eng.tensor_tensor(out[q, :, :], src[q, :, lo:lo + S], inv, ALU.mult))
                step(eng.tensor_tensor(out, out, vv, ALU.subtract))
            eng.sem_inc(chip.mixed.sem, 1)

        @block.tensor
        def _(pe):
            def scores(w):
                g, h, qt = items[w]
                lo, hi = keys(g)
                po, q0 = 64 * (h % 2), g * S + qt * P
                if w >= 2:
                    pe.wait_ge(chip.scores_read.sem, chip.scores_read.at(w - 1))
                nc.tensor.matmul(chip.bank[w % 2][:, 0:hi - lo], u[po:po + 64, CH_Q + h // 2, q0:q0 + P],
                                 u[po:po + 64, CH_K + h // 2, lo:hi], start=True, stop=True)\
                    .then_inc(chip.scored.sem, 1)

            def transposes(w):
                g, h, qt = items[w]
                pe.wait_ge(chip.probs.sem, chip.probs.at(w + 1))
                if w >= 2:
                    pe.wait_ge(chip.copied.sem, chip.copied.at(w - 1))
                for kt in range((keys(g)[1] - keys(g)[0]) // P):
                    mm = nc.tensor.transpose(chip.bank[2 + w % 2][:, kt * P:(kt + 1) * P],
                                             sc[:, w % 4, kt * P:(kt + 1) * P], chip.ident[:, :])
                mm.then_inc(chip.turned.sem, 1)

            def values(n):
                g, h, _ = items[2 * n]
                po = 64 * (h % 2)
                pe.wait_ge(chip.copied.sem, chip.copied.at(2 * n + 2))
                if n >= 2:
                    pe.wait_ge(chip.moved.sem, chip.moved.at(n - 1))
                nkt = (keys(g)[1] - keys(g)[0]) // P
                for kt in range(nkt):
                    mm = nc.tensor.matmul(chip.bank[4 + n % 2][po:po + 64, 0:S],
                                          v[:, kt + 4 - nkt, h * DH:(h + 1) * DH], pt[:, n % 2, kt, :],
                                          start=(kt == 0), stop=(kt == nkt - 1))
                mm.then_inc(chip.product.sem, 1)

            for w in range(3):
                scores(w)
            for w in range(len(items)):
                if w + 3 < len(items):
                    scores(w + 3)
                transposes(w)
                if w >= 2 and w % 2 == 0:
                    values(w // 2 - 1)
            values(len(items) // 2 - 1)
            pe.wait_ge(chip.mixed.sem, chip.mixed.at(1))
            for b in range(2):
                mm = nc.tensor.matmul(chip.bank[6 + b][:, 0:t], chip.extra["pool_w"][:, b, :], y[:, 2 + b, 0:t],
                                      start=True, stop=True)
            mm.then_inc(chip.product.sem, 1)

        @block.scalar
        def _(act):
            def exps(w):
                g, h, qt = items[w]
                n = keys(g)[1] - keys(g)[0]
                act.wait_ge(chip.maxed.sem, chip.maxed.at(w + 1))
                nc.scalar.activation(sc[:, w % 4, 0:n], sc[:, w % 4, 0:n], ACT.Exp, bias=chip.nmax[:, w % 4:w % 4 + 1],
                                     accum_out=chip.rsum[:, w % 4:w % 4 + 1]).then_inc(chip.exped.sem, 1)

            def copies(w):
                g, h, qt = items[w]
                nkt = (keys(g)[1] - keys(g)[0]) // P
                n = w // 2
                act.wait_ge(chip.turned.sem, chip.turned.at(w + 1))
                if n >= 2:
                    act.wait_ge(chip.product.sem, chip.product.at(n - 1))
                nc.scalar.activation(pt[:, n % 2, 0:nkt, qt * P:(qt + 1) * P],
                                     chip.bank[2 + w % 2][:, 0:nkt * P].rearrange("p (k q) -> p k q", q=P), ACT.Copy)\
                    .then_inc(chip.copied.sem, 1)

            def move(n):
                g, h, _ = items[2 * n]
                po = 64 * (h % 2)
                act.wait_ge(chip.product.sem, chip.product.at(n + 1))
                nc.scalar.activation(y[po:po + 64, 4 + h // 2, g * S:(g + 1) * S], chip.bank[4 + n % 2][po:po + 64, 0:S],
                                     ACT.Copy).then_inc(chip.moved.sem, 1)

            exps(0)
            exps(1)
            for w in range(len(items)):
                if w + 2 < len(items):
                    exps(w + 2)
                copies(w)
                if w >= 3 and w % 2 == 1:
                    move(w // 2 - 1)
            move(len(items) // 2 - 1)
            act.wait_ge(chip.product.sem, chip.product.at(len(items) // 2 + 1))
            for b in range(2):
                nc.scalar.activation(y[:, 2 + b, 0:t], chip.bank[6 + b][:, 0:t], ACT.Copy,
                                     scale=chip.col("pool_scale", layer * 2 + b, 1))

        @block.vector
        def _(dve):
            def scale(w):
                g, h, qt = items[w]
                n = keys(g)[1] - keys(g)[0]
                s, bank = sc[:, w % 4, :], chip.bank[w % 2]
                dve.wait_ge(chip.scored.sem, chip.scored.at(w + 1))
                if w >= 4:
                    dve.wait_ge(chip.turned.sem, chip.turned.at(w - 3))
                if g == 0:
                    r0 = (2 - 2 * qt) * GRID
                    nc.vector.scalar_tensor_tensor(s[:, 0:S], bank[:, 0:S], 0.125, bias[:, h, r0:r0 + S], ALU.mult, ALU.add)
                    nc.vector.tensor_scalar(s[:, S:T2], bank[:, S:T2], 0.125, None, ALU.mult)\
                        .then_inc(chip.scores_read.sem, 1)
                else:
                    nc.vector.tensor_scalar(s[:, 0:n], bank[:, 0:n], 0.125, None, ALU.mult)\
                        .then_inc(chip.scores_read.sem, 1)
                dve.wait_ge(chip.scores_read.sem, chip.scores_read.at(w + 1))
                nc.vector.tensor_reduce(chip.nmax[:, w % 4:w % 4 + 1], s[:, 0:n], AX.X, ALU.max, negate=True)\
                    .then_inc(chip.maxed.sem, 1)

            def normalise(w):
                g, h, qt = items[w]
                n = keys(g)[1] - keys(g)[0]
                dve.wait_ge(chip.exped.sem, chip.exped.at(w + 1))
                r = chip.rsum[:, w % 4:w % 4 + 1]
                in_order(dve, chip.dve_step, nc.vector.reciprocal(r, r))
                nc.vector.tensor_scalar(sc[:, w % 4, 0:n], sc[:, w % 4, 0:n], r, None, ALU.mult).then_inc(chip.probs.sem, 1)

            scale(0)
            scale(1)
            for w in range(len(items)):
                if w + 2 < len(items):
                    scale(w + 2)
                normalise(w)
    n = len(items)
    for sig in (chip.scored, chip.scores_read, chip.maxed, chip.exped, chip.probs, chip.turned, chip.copied):
        sig.passed(n)
    chip.product.passed(n // 2 + 1)
    chip.moved.passed(n // 2)
    chip.mixed.passed(1)


def stage_add_product(chip, stream, x, y, gate, groups):
    nc, t = chip.nc, groups[-1][1]
    with nc.Block() as block:
        @block.sync
        def _(sp):
            stream.load_ahead(sp, KT)

        @block.tensor
        def _(pe):
            for n in range(KT):
                if n >= 4:
                    pe.wait_ge(chip.added.sem, chip.added.at(n - 3))
                stream.chunk(pe, 0, n, chip.bank[n % 4][:, 0:t], lambda kt: (chip.hi[:, kt, 0:t], chip.lo[:, kt, 0:t]),
                             ready=chip.split_in if n == 0 else None)

        @block.scalar
        def _(act):
            for kt in range(KT):
                nc.scalar.activation(chip.hi[:, kt, 0:t], y[:, kt, 0:t], ACT.Copy).then_inc(chip.copied.sem, 1)
            for n in range(KT):
                stream.round(act, 0, n + 2)

        @block.vector
        def _(dve):
            for kt in range(KT):
                dve.wait_ge(chip.copied.sem, chip.copied.at(kt + 1))
                nc.vector.tensor_tensor(chip.lo[:, kt, 0:t], y[:, kt, 0:t], chip.hi[:, kt, 0:t].bitcast(F32), ALU.subtract)\
                    .then_inc(chip.split_in.sem, 1)
            for n in range(KT):
                stream.subtract(dve, 0, n + 2, [0])
                dve.wait_ge(stream.used, stream.used_at(n))
                for g, (lo, hi) in enumerate(groups):
                    last = nc.vector.scalar_tensor_tensor(x[:, n, lo:hi], chip.bank[n % 4][:, lo:hi], gate(n, g),
                                                          x[:, n, lo:hi], ALU.mult, ALU.add)
                last.then_inc(chip.added.sem, 1)
                stream.subtract(dve, 0, n + 2, [1])
    chip.copied.passed(KT)
    chip.split_in.passed(KT)
    chip.added.passed(KT)
    stream.g0 += KT


B_U, B_TAB = 0, 5120
B_RV = B_TAB + N_TAB
B_VS = B_RV + 1024
B_Y = B_VS + 512
B_SR = B_Y + 2048
B_RY, B_T1, B_T2 = B_SR + 768, B_SR + 768 + 1024, B_SR + 768 + 2048
B_W1 = B_T2 + 1024
B_W2 = B_W1 + 8192
B_K2 = B_W2 + 256
B_BLK = B_K2 + 1024
B_HID = B_BLK + 960
B_SC, B_PTS, B_PTC = B_HID + 128, B_HID + 128 + 2048, B_HID + 128 + 2048 + 1536
B_C = B_PTC + 2048
E_Q, E_KEYS, E_H = 0, 4096, 4096 + 16 * NK
E_SC = P * NK
E_SC2, E_V, E_I, E_IF, E_TV, E_TJ = (E_SC + 4096 + n for n in (0, 512, 1024, 1536, 2048, 2304))
E_J, E_JF, E_EQ, E_N, E_W, E_CAND = (E_SC + 4096 + n for n in (2560, 3072, 3584, 5632, 6400, 6912))
E_WORK = S * NK
E_SLOT = E_WORK
E_HOT = E_WORK + 3 * S
HOTS = 8
B_WORDS = E_HOT + HOTS * 2 * P


def stage_final_norm(chip):
    norm = Norm(chip, chip.part(A_X, KT, T2), chip.x2, chip.part(A_RSTD + 512, 512), chip.part(A_RSTD, 512),
                lambda kt, g: chip.col("final_g", kt, 1), None, [(0, S)], S, split=False)
    with chip.nc.Block() as block:
        block.tensor(norm.tensor)
        block.scalar(norm.scalar)
        block.vector(norm.vector)
    norm.end()


def norm2(chip, i, at, scratch):
    return Norm(chip, chip.x2, chip.part(scratch, KT, S), chip.part(at, S), chip.part(at + S, S),
                lambda kt, g: chip.gain2[:, i, kt:kt + 1], lambda kt, g: chip.mod2[:, 3 * i * KT + kt:3 * i * KT + kt + 1],
                [(0, S)], S)


def stage_proj(chip, stream):
    nc, d = chip.nc, chip.dram
    norm = norm2(chip, 0, B_T2, B_Y)
    hi, lo, u = chip.hi, chip.lo, chip.part(B_U, N_PROJ, S)
    rv, vs = chip.part(B_RV, 2, 512), chip.part(B_VS, 2, S)
    with nc.Block() as block:
        @block.sync
        def _(sp):
            sp.dma_start(chip.part(B_TAB, N_TAB), d["tables"]).then_inc(chip.table.sem, 16)
            for n, k in enumerate("kv"):
                sp.dma_start(chip.part(B_W1 + 4096 * n, 16, 256), d[f"cmp_{k}1"]).then_inc(chip.table.sem, 16)
                sp.dma_start(chip.part(B_W2 + 128 * n, 2, 64), d[f"cmp_{k}2"]).then_inc(chip.table.sem, 16)
            stream.load_ahead(sp, 28)
            sp.wait_ge(chip.table.sem, chip.table.at(80))

        @block.tensor
        def _(pe):
            norm.tensor(pe)
            for n in range(N_PROJ):
                k = n // 2
                if n >= 4 and n % 2 == 0:
                    pe.wait_ge(chip.copied.sem, chip.copied.at(k - 1))
                stream.chunk(pe, 0, n, chip.bank[k % 2][:, n % 2 * S:(n % 2 + 1) * S], lambda kt: (hi[:, kt, :], lo[:, kt, :]),
                             ready=chip.split_in if n == 0 else None)
            for i, width in enumerate((512, 2 * P + 24)):
                for n in range(4):
                    for m in range(2):
                        w_hi, w_lo = stream.half(pe, 0, N_PROJ + 4 * i + n, m)
                        for tt in range(2):
                            q, kt = slice(tt * P, (tt + 1) * P), 2 * n + m
                            mm = product(nc, chip.bank[2 + 2 * i + tt][:, 0:width],
                                         [((hi[:, kt, q], lo[:, kt, q]), (w_hi[:, 0:width], w_lo[:, 0:width]))],
                                         start=(kt == 0), stop=(kt == KT - 1))
                        mm.then_inc(stream.used, 1)

        @block.scalar
        def _(act):
            norm.scalar(act)
            for k in range(N_PROJ // 2):
                stream.round(act, 0, 2 * k + 2)
                stream.round(act, 0, 2 * k + 3, [0])
                act.wait_ge(stream.used, stream.used_at(2 * k + 1))
                nc.scalar.activation(u[:, 2 * k:2 * k + 2, :].rearrange("p a b -> p (a b)"), chip.bank[k % 2][:, :], ACT.Copy)\
                    .then_inc(chip.copied.sem, 1)
                stream.round(act, 0, 2 * k + 3, [1])
            for n in range(8):
                stream.round(act, 0, N_PROJ + n + 2)
            act.wait_ge(stream.used, stream.used_at(27))
            for tt in range(2):
                nc.scalar.activation(rv[:, tt, :], chip.bank[2 + tt][:, :], ACT.Copy)
                nc.scalar.activation(vs[:, tt, :], chip.bank[4 + tt][:, 0:S], ACT.Copy)
                nc.scalar.activation(chip.gates[:, tt, :], chip.bank[4 + tt][:, S:S + 24], ACT.Sigmoid)

        @block.vector
        def _(dve):
            norm.vector(dve)
            for n in range(28):
                stream.subtract(dve, 0, n + 2)
    norm.end()
    chip.table.passed(80)
    chip.copied.passed(N_PROJ // 2)
    stream.g0 += 28


def table(chip, name, *shape):
    at, n = TAB[name]
    return chip.part(B_TAB + at, *(shape or (n,)))


def stage_rope(chip):
    nc, u = chip.nc, chip.part(B_U, N_PROJ, S)
    pairs = [(n, min(n + 2, ROPE_ALL)) for n in range(0, ROPE_ALL, 2)]
    with nc.Block() as block:
        @block.tensor
        def _(pe):
            for k, (lo, hi) in enumerate(pairs):
                perm = table(chip, "perm128" if lo < ROPE_WIDE else "perm64")
                mm = nc.tensor.matmul(chip.bank[k][:, 0:(hi - lo) * S], perm,
                                      u[:, lo:hi, :].rearrange("p a b -> p (a b)"), start=True, stop=True)
                mm.then_inc(chip.turned.sem, 1)

        @block.vector
        def _(dve):
            for k, (lo, hi) in enumerate(pairs):
                size = "128" if lo < ROPE_WIDE else "64"
                n = hi - lo
                cos, sin = (table(chip, x + size).unsqueeze(1).to_broadcast([P, n, S]) for x in ("cos", "sin"))
                tmp = chip.part(B_RY if k % 2 else B_T1, n, S)
                rot = chip.bank[k][:, 0:n * S].rearrange("p (a b) -> p a b", b=S)
                dve.wait_ge(chip.turned.sem, chip.turned.at(k + 1))
                nc.vector.tensor_tensor(tmp, rot, sin, ALU.mult)
                in_order(dve, chip.dve_step, nc.vector.tensor_tensor(u[:, lo:hi, :], u[:, lo:hi, :], cos, ALU.mult))
                nc.vector.tensor_tensor(u[:, lo:hi, :], u[:, lo:hi, :], tmp, ALU.add)
    chip.turned.passed(len(pairs))


def stage_retention(chip):
    nc = chip.nc
    u, rv, y = chip.part(B_U, N_PROJ, S), chip.part(B_RV, 2, 512), chip.part(B_Y, KT, S)
    sr, ry = chip.part(B_SR, 2, 384), chip.part(B_RY, RET_H * S)
    t1, t2 = chip.part(B_T1, RET_H * S), chip.part(B_T2, RET_H * S)
    decay = table(chip, "decay", RET_H, S)
    halves = [slice(0, 512), slice(512, 1024)]
    with nc.Block() as block:
        @block.tensor
        def _(pe):
            def scores(h):
                if h >= 2:
                    pe.wait_ge(chip.probs.sem, chip.probs.at(h - 1))
                q, k, b = u[:, R_Q + h, :], u[:, R_K + h, :], chip.bank[h % 2]
                nc.tensor.matmul(b[:, 0:S], k[:, 0:P], q, start=True, stop=True)
                nc.tensor.matmul(b[:, S:384], k[:, P:S], q[:, P:S], start=True, stop=True).then_inc(chip.scored.sem, 1)

            scores(0)
            for h in range(RET_H):
                if h + 1 < RET_H:
                    scores(h + 1)
                pe.wait_ge(chip.probs.sem, chip.probs.at(h + 1))
                o = chip.bank[2 + h // 2][:, (h % 2) * S:(h % 2 + 1) * S]
                nc.tensor.matmul(o, rv[:, 0, h * P:(h + 1) * P], sr[:, h % 2, 0:S], start=True, stop=False)
                nc.tensor.matmul(o[:, P:S], rv[:, 1, h * P:(h + 1) * P], sr[:, h % 2, S:384], start=False, stop=True)\
                    .then_inc(chip.product.sem, 1)
            pe.wait_ge(chip.copied.sem, chip.copied.at(2))
            for n, part in enumerate(halves):
                nc.tensor.matmul(chip.bank[4 + n][:, :], chip.ones[:, :], ry[:, part], start=True, stop=True)\
                    .then_inc(chip.summed.sem, 1)
            pe.wait_ge(chip.squared.sem, chip.squared.at(1))
            for n, part in enumerate(halves):
                nc.tensor.matmul(chip.bank[6 + n][:, :], chip.ones[:, :], t1[:, part], start=True, stop=True)\
                    .then_inc(chip.summed.sem, 1)

        @block.scalar
        def _(act):
            nc.scalar.activation(u[:, R_G:R_G + RET_H, :], u[:, R_G:R_G + RET_H, :], ACT.Silu).then_inc(chip.silu_done.sem, 1)
            for n, part in enumerate(halves):
                act.wait_ge(chip.product.sem, chip.product.at(2 * n + 2))
                nc.scalar.activation(ry[:, part], chip.bank[2 + n][:, :], ACT.Copy).then_inc(chip.copied.sem, 1)
            act.wait_ge(chip.scaled.sem, chip.scaled.at(1))
            nc.scalar.activation(t1, ry, ACT.Square).then_inc(chip.squared.sem, 1)
            for n, part in enumerate(halves):
                act.wait_ge(chip.summed.sem, chip.summed.at(3 + n))
                last = nc.scalar.activation(t2[:, part], chip.bank[6 + n][:, :], ACT.Sqrt, bias=chip.eps[:, 0:1], scale=1.0 / P)
            last.then_inc(chip.rooted.sem, 1)

        @block.vector
        def _(dve):
            for h in range(RET_H):
                dve.wait_ge(chip.scored.sem, chip.scored.at(h + 1))
                if h >= 2:
                    dve.wait_ge(chip.product.sem, chip.product.at(h - 1))
                b = chip.bank[h % 2]
                nc.vector.tensor_tensor(sr[:, h % 2, 0:S], b[:, 0:S], decay[:, h, :], ALU.mult)
                nc.vector.tensor_tensor(sr[:, h % 2, S:384], b[:, S:384], decay[:, h, 0:P], ALU.mult).then_inc(chip.probs.sem, 1)
            dve.wait_ge(chip.copied.sem, chip.copied.at(2))
            dve.wait_ge(chip.summed.sem, chip.summed.at(2))
            for n, part in enumerate(halves):
                last = nc.vector.scalar_tensor_tensor(ry[:, part], chip.bank[4 + n][:, :], -1.0 / P, ry[:, part], ALU.mult, ALU.add)
            last.then_inc(chip.scaled.sem, 1)
            dve.wait_ge(chip.rooted.sem, chip.rooted.at(1))
            dve.wait_ge(chip.silu_done.sem, chip.silu_done.at(1))
            in_order(dve, chip.dve_step, nc.vector.reciprocal(t2, t2))
            in_order(dve, chip.dve_step, nc.vector.tensor_tensor(ry, ry, t2, ALU.mult))
            nc.vector.tensor_tensor(y[:, 0:RET_H, :].rearrange("p a b -> p (a b)"), ry,
                                    u[:, R_G:R_G + RET_H, :].rearrange("p a b -> p (a b)"), ALU.mult)
    for sig, n in ((chip.scored, 4), (chip.probs, 4), (chip.product, 4), (chip.copied, 2), (chip.summed, 4),
                   (chip.squared, 1), (chip.rooted, 1), (chip.scaled, 1), (chip.silu_done, 1)):
        sig.passed(n)


def stage_compress(chip):
    nc = chip.nc
    u = chip.part(B_U, N_PROJ, S)
    w1 = [chip.part(B_W1 + 4096 * n, 16, 256) for n in range(2)]
    w2 = [chip.part(B_W2 + 128 * n, 2, 64) for n in range(2)]
    k2 = [chip.part(B_K2 + 512 * n, 2, S) for n in range(2)]
    blk = [chip.part(B_BLK + 480 * n, 16, 30) for n in range(2)]
    hid = [chip.part(B_HID + 60 * n, 2, 30) for n in range(2)]
    ptc = chip.part(B_PTC, NSA_H, S)
    s_c, mask01, add = chip.part(B_C, 16, 16), table(chip, "cmp_mask", 2, 16), table(chip, "cmp_add", 2, 16)
    top, tot = chip.part(B_C + 256, 16), chip.part(B_C + 272, 16)
    kc, vc = chip.part(B_C + 288, 16), chip.part(B_C + 304, 2, 64)
    sc = s_c[:, :, 0:NCB]
    with nc.Block() as block:
        @block.vector
        def _(dve):
            for n, chunk in enumerate((N_KC, N_VC)):
                for g in range(2):
                    src = u[64 * g:64 * g + 64, chunk, :]
                    nc.vector.tensor_copy(k2[n][0:64, g, :], src)
                    last = nc.vector.tensor_copy(k2[n][64:128, g, 0:S - 1], src[:, 1:S])
            nc.vector.memset(k2[0][64:128, :, S - 1:S], 0.0)
            in_order(dve, chip.dve_step, nc.vector.memset(k2[1][64:128, :, S - 1:S], 0.0))
            for n, pe_col in enumerate(("pe_k", "pe_v")):
                for g in range(2):
                    v = k2[n][:, g, :].rearrange("p (n l) -> p l n", l=CMP_STRIDE)
                    for j0 in (0, 8):
                        out = blk[n][:, j0:j0 + 8, g * NCB:(g + 1) * NCB]
                        pos = chip.col(pe_col, j0, 8).unsqueeze(2).to_broadcast([P, 8, NCB])
                        at = j0 // 8
                        last = nc.vector.tensor_tensor(out, v[:, 0:CMP_STRIDE:2, at:at + NCB], pos, ALU.add)
            last.then_inc(chip.gated.sem, 1)
            dve.wait_ge(chip.scored.sem, chip.scored.at(1))
            for qt in range(2):
                for g in range(2):
                    last = nc.vector.scalar_tensor_tensor(
                        s_c[:, 8 * qt + g:8 * qt + 8:2, 0:NCB],
                        chip.bank[6 + g][:, 64 * qt:64 * qt + 64].rearrange("p (h n) -> p h n", n=16)[:, :, 0:NCB], 0.125,
                        add[:, qt, 0:NCB].unsqueeze(1).to_broadcast([P, 4, NCB]), ALU.mult, ALU.add)
            in_order(dve, chip.dve_step, last)
            in_order(dve, chip.dve_step, nc.vector.tensor_reduce(top, sc, AX.X, ALU.max))
            nc.vector.tensor_tensor(sc, sc, top.unsqueeze(2).to_broadcast([P, 16, NCB]), ALU.subtract).then_inc(chip.maxed.sem, 1)
            dve.wait_ge(chip.exped.sem, chip.exped.at(1))
            for qt in range(2):
                last = nc.vector.tensor_tensor(s_c[:, 8 * qt:8 * qt + 8, 0:NCB], s_c[:, 8 * qt:8 * qt + 8, 0:NCB],
                                               mask01[:, qt, 0:NCB].unsqueeze(1).to_broadcast([P, 8, NCB]), ALU.mult)
            in_order(dve, chip.dve_step, last)
            in_order(dve, chip.dve_step, nc.vector.tensor_reduce(tot, sc, AX.X, ALU.add))
            in_order(dve, chip.dve_step, nc.vector.tensor_scalar(tot, tot, TINY, None, ALU.max))
            in_order(dve, chip.dve_step, nc.vector.reciprocal(tot, tot))
            gate = chip.gates[:, :, :].rearrange("p t (h b) -> p (t h) b", b=3)[:, :, 0]
            in_order(dve, chip.dve_step, nc.vector.tensor_tensor(tot, tot, gate, ALU.mult))
            nc.vector.tensor_tensor(sc, sc, tot.unsqueeze(2).to_broadcast([P, 16, NCB]), ALU.mult).then_inc(chip.probs.sem, 1)

        @block.tensor
        def _(pe):
            pe.wait_ge(chip.gated.sem, chip.gated.at(1))
            for n in range(2):
                for m in range(2):
                    for j in range(16):
                        mm = nc.tensor.matmul(chip.bank[2 * n + m][:, 0:2 * NCB], w1[n][:, j, m * P:(m + 1) * P],
                                              blk[n][:, j, :], start=(j == 0), stop=(j == 15))
                    mm.then_inc(chip.product.sem, 1)
            pe.wait_ge(chip.silu_done.sem, chip.silu_done.at(4))
            for g in range(2):
                for m in range(2):
                    nc.tensor.matmul(chip.bank[4][64 * g:64 * g + 64, 0:NCB], w2[0][:, m, :],
                                     hid[0][:, m, g * NCB:(g + 1) * NCB], start=(m == 0), stop=(m == 1))
                for m in range(2):
                    mm = nc.tensor.matmul(chip.bank[5][0:NCB, 64 * g:64 * g + 64], hid[1][:, m, g * NCB:(g + 1) * NCB],
                                          w2[1][:, m, :], start=(m == 0), stop=(m == 1))
            mm.then_inc(chip.product.sem, 1)
            pe.wait_ge(chip.copied.sem, chip.copied.at(1))
            for qt in range(2):
                for hh in range(NSA_H):
                    po, n = 64 * (hh % 2), 4 * qt + hh // 2
                    mm = nc.tensor.matmul(chip.bank[6 + hh % 2][:, n * 16:n * 16 + NCB], u[po:po + 64, N_Q + hh // 2, qt * P:(qt + 1) * P],
                                          kc[po:po + 64, 0:NCB], start=True, stop=True)
            mm.then_inc(chip.scored.sem, 1)
            pe.wait_ge(chip.probs.sem, chip.probs.at(1))
            for hh in range(NSA_H):
                for qt in range(2):
                    n = 2 * hh + qt
                    mm = nc.tensor.matmul(chip.bank[n // 4][0:NCB, (n % 4) * P:(n % 4 + 1) * P], s_c[:, 8 * qt + hh, 0:NCB],
                                          chip.ident[:, :], start=True, stop=True)
            mm.then_inc(chip.turned.sem, 1)

        @block.scalar
        def _(act):
            for n in range(2):
                for m in range(2):
                    act.wait_ge(chip.product.sem, chip.product.at(2 * n + m + 1))
                    nc.scalar.activation(hid[n][:, m, :], chip.bank[2 * n + m][:, 0:2 * NCB], ACT.Gelu_apprx_tanh,
                                         bias=chip.col(("b_cmp_k", "b_cmp_v")[n], m, 1)).then_inc(chip.silu_done.sem, 1)
            act.wait_ge(chip.product.sem, chip.product.at(5))
            nc.scalar.activation(kc[:, 0:NCB], chip.bank[4][:, 0:NCB], ACT.Copy)
            nc.scalar.activation(vc[0:NCB, :, :].rearrange("p a b -> p (a b)"), chip.bank[5][0:NCB, 0:P], ACT.Copy).then_inc(chip.copied.sem, 1)
            act.wait_ge(chip.maxed.sem, chip.maxed.at(1))
            nc.scalar.activation(sc, sc, ACT.Exp).then_inc(chip.exped.sem, 1)
            act.wait_ge(chip.turned.sem, chip.turned.at(1))
            for b in range(4):
                nc.scalar.activation(ptc[0:NCB, 2 * b:2 * b + 2, :].rearrange("p a b -> p (a b)"), chip.bank[b][0:NCB, :], ACT.Copy)
    for sig, n in ((chip.gated, 1), (chip.scored, 1), (chip.maxed, 1), (chip.exped, 1), (chip.probs, 1), (chip.product, 5),
                   (chip.silu_done, 4), (chip.copied, 1), (chip.turned, 1)):
        sig.passed(n)


def stage_sparse(chip):
    nc = chip.nc
    u, vs, y = chip.part(B_U, N_PROJ, S), chip.part(B_VS, 2, S), chip.part(B_Y, KT, S)
    sc, pts, ptc = chip.part(B_SC, 4, 2, S), chip.part(B_PTS, 2, 2, 384), chip.part(B_PTC, NSA_H, S)
    vc, causal = chip.part(B_C + 304, 2, 64), table(chip, "causal")
    items = [(hh, qt) for hh in range(NSA_H) for qt in range(2)]

    with nc.Block() as block:
        @block.tensor
        def _(pe):
            def scores(w):
                hh, qt = items[w]
                po, nk = 64 * (hh % 2), P * (qt + 1)
                if w >= 2:
                    pe.wait_ge(chip.scores_read.sem, chip.scores_read.at(w - 1))
                for br, chunk in enumerate((N_KS, N_KW)):
                    mm = nc.tensor.matmul(chip.bank[w % 2][:, br * S:br * S + nk], u[po:po + 64, N_Q + hh // 2, qt * P:(qt + 1) * P],
                                          u[po:po + 64, chunk, 0:nk], start=True, stop=True)
                mm.then_inc(chip.scored.sem, 1)

            def transposes(w):
                hh, qt = items[w]
                pe.wait_ge(chip.probs.sem, chip.probs.at(w + 1))
                if w >= 2:
                    pe.wait_ge(chip.copied.sem, chip.copied.at(w - 1))
                for br in range(2):
                    for kt in range(qt + 1):
                        mm = nc.tensor.transpose(chip.bank[2 + w % 2][:, (2 * br + kt) * P:(2 * br + kt + 1) * P],
                                                 sc[:, w % 4, br, kt * P:(kt + 1) * P], chip.ident[:, :])
                mm.then_inc(chip.turned.sem, 1)

            def values(hh):
                g = hh % 2
                pe.wait_ge(chip.copied.sem, chip.copied.at(2 * hh + 2))
                if hh >= 2:
                    pe.wait_ge(chip.moved.sem, chip.moved.at(hh - 1))
                o = chip.bank[4 + hh % 2][64 * g:64 * g + 64, :]
                for br in range(2):
                    v = slice(br * P + g * 64, br * P + g * 64 + 64)
                    nc.tensor.matmul(o[:, 0:S], vs[:, 0, v], pts[:, hh % 2, br, 0:S], start=(br == 0), stop=False)
                    nc.tensor.matmul(o[:, P:S], vs[:, 1, v], pts[:, hh % 2, br, S:384], start=False, stop=False)
                nc.tensor.matmul(o[:, 0:S], vc[0:NCB, g, :], ptc[0:NCB, hh, :], start=False, stop=True).then_inc(chip.product.sem, 1)

            for w in range(3):
                scores(w)
            for w in range(len(items)):
                if w + 3 < len(items):
                    scores(w + 3)
                transposes(w)
                if w >= 2 and w % 2 == 0:
                    values(w // 2 - 1)
            values(NSA_H - 1)

        @block.scalar
        def _(act):
            def exps(w):
                hh, qt = items[w]
                nk = P * (qt + 1)
                act.wait_ge(chip.maxed.sem, chip.maxed.at(w + 1))
                for br in range(2):
                    last = nc.scalar.activation(sc[:, w % 4, br, 0:nk], sc[:, w % 4, br, 0:nk], ACT.Exp,
                                                bias=chip.nmax4[:, w % 4, br:br + 1], accum_out=chip.rsum4[:, w % 4, br:br + 1])
                last.then_inc(chip.exped.sem, 1)

            def copies(w):
                hh, qt = items[w]
                act.wait_ge(chip.turned.sem, chip.turned.at(w + 1))
                if hh >= 2:
                    act.wait_ge(chip.product.sem, chip.product.at(hh - 1))
                src = chip.bank[2 + w % 2][:, :].rearrange("p (b k) -> p b k", b=2)
                nc.scalar.activation(pts[:, hh % 2, :, P * qt:P * qt + P * (qt + 1)], src[:, :, 0:P * (qt + 1)], ACT.Copy)\
                    .then_inc(chip.copied.sem, 1)

            def move(hh):
                po = 64 * (hh % 2)
                act.wait_ge(chip.product.sem, chip.product.at(hh + 1))
                nc.scalar.activation(y[po:po + 64, 4 + hh // 2, :], chip.bank[4 + hh % 2][po:po + 64, 0:S], ACT.Copy)\
                    .then_inc(chip.moved.sem, 1)

            exps(0)
            exps(1)
            for w in range(len(items)):
                if w + 2 < len(items):
                    exps(w + 2)
                copies(w)
                if w >= 3 and w % 2 == 1:
                    move(w // 2 - 1)
            move(NSA_H - 1)

        @block.vector
        def _(dve):
            def scale(w):
                hh, qt = items[w]
                nk = P * (qt + 1)
                s = sc[:, w % 4, :, 0:nk]
                dve.wait_ge(chip.scored.sem, chip.scored.at(w + 1))
                if w >= 4:
                    dve.wait_ge(chip.turned.sem, chip.turned.at(w - 3))
                nc.vector.scalar_tensor_tensor(s, chip.bank[w % 2][:, :].rearrange("p (b k) -> p b k", b=2)[:, :, 0:nk], 0.125,
                                               causal[:, S - nk:S].unsqueeze(1).to_broadcast([P, 2, nk]), ALU.mult, ALU.add)\
                    .then_inc(chip.scores_read.sem, 1)
                dve.wait_ge(chip.scores_read.sem, chip.scores_read.at(w + 1))
                nc.vector.tensor_reduce(chip.nmax4[:, w % 4, :], s, AX.X, ALU.max, negate=True).then_inc(chip.maxed.sem, 1)

            def normalise(w):
                hh, qt = items[w]
                nk = P * (qt + 1)
                s, r = sc[:, w % 4, :, 0:nk], chip.rsum4[:, w % 4, :]
                dve.wait_ge(chip.exped.sem, chip.exped.at(w + 1))
                in_order(dve, chip.dve_step, nc.vector.reciprocal(r, r))
                in_order(dve, chip.dve_step, nc.vector.tensor_tensor(r, r, chip.gates[:, qt, 3 * hh + 1:3 * hh + 3], ALU.mult))
                nc.vector.tensor_tensor(s, s, r.unsqueeze(2).to_broadcast([P, 2, nk]), ALU.mult).then_inc(chip.probs.sem, 1)

            scale(0)
            scale(1)
            for w in range(len(items)):
                if w + 2 < len(items):
                    scale(w + 2)
                normalise(w)
    n = len(items)
    for sig in (chip.scored, chip.scores_read, chip.maxed, chip.exped, chip.probs, chip.turned, chip.copied):
        sig.passed(n)
    chip.product.passed(NSA_H)
    chip.moved.passed(NSA_H)


def stage_expert_scores(chip, stream):
    nc = chip.nc
    norm = norm2(chip, 1, E_SC2, E_H)
    keys = chip.part(E_KEYS, 16 * NK)
    q, s = chip.part(E_Q, 16, S), chip.part(E_SC, 2, 16, NK)
    with nc.Block() as block:
        @block.sync
        def _(sp):
            sp.dma_start(keys, chip.dram["subkeys"]).then_inc(chip.table.sem, 16)
            stream.load_ahead(sp, 16)

        @block.tensor
        def _(pe):
            norm.tensor(pe)
            for n in range(16):
                k = n // 2
                if n >= 4 and n % 2 == 0:
                    pe.wait_ge(chip.copied.sem, chip.copied.at(k - 1))
                stream.chunk(pe, 0, n, chip.bank[k % 2][:, n % 2 * S:(n % 2 + 1) * S], lambda kt: (chip.hi[:, kt, :], chip.lo[:, kt, :]),
                             ready=chip.split_in if n == 0 else None)
            pe.wait_ge(chip.table.sem, chip.table.at(16))
            pe.wait_ge(chip.copied.sem, chip.copied.at(8))
            for tt in range(2):
                for n in range(16):
                    mm = nc.tensor.matmul(chip.bank[4 * tt + n // 4][:, (n % 4) * NK:(n % 4 + 1) * NK],
                                          q[:, n, tt * P:(tt + 1) * P], keys[:, n * NK:(n + 1) * NK], start=True, stop=True)
            mm.then_inc(chip.scored.sem, 1)

        @block.scalar
        def _(act):
            norm.scalar(act)
            for k in range(8):
                stream.round(act, 0, 2 * k + 2)
                stream.round(act, 0, 2 * k + 3, [0])
                act.wait_ge(stream.used, stream.used_at(2 * k + 1))
                nc.scalar.activation(q[:, 2 * k:2 * k + 2, :].rearrange("p a b -> p (a b)"), chip.bank[k % 2][:, :], ACT.Copy)\
                    .then_inc(chip.copied.sem, 1)
                stream.round(act, 0, 2 * k + 3, [1])
            act.wait_ge(chip.scored.sem, chip.scored.at(1))
            for b in range(8):
                nc.scalar.activation(s[:, b // 4, 4 * (b % 4):4 * (b % 4) + 4, :].rearrange("p a b -> p (a b)"),
                                     chip.bank[b][:, :], ACT.Copy)

        @block.vector
        def _(dve):
            norm.vector(dve)
            for n in range(16):
                stream.subtract(dve, 0, n + 2)
    norm.end()
    chip.copied.passed(8)
    chip.table.passed(16)
    chip.scored.passed(1)
    stream.g0 += 16


def over_tokens(eng, tt, body):
    cycles = P // HOTS
    if tt == 0:
        for j in range(HOTS):
            body(0, j)
    with eng.Fori(max(1, tt * cycles), (tt + 1) * cycles) as c:
        for j in range(HOTS):
            body(c, j)


def stage_retrieve(chip):
    nc = chip.nc
    s = chip.part(E_SC, 2, 16, NK)
    rest = [chip.part(E_SC2 + 256 * n, 256) for n in range(2)]
    v, ix = chip.part(E_V, 2, 16, TOPK), chip.part(E_I, 2, 16, TOPK).bitcast(U32)
    ixf = chip.part(E_IF, 2, 16, TOPK)
    tv, tj = chip.part(E_TV, 2, SLOTS), chip.part(E_TJ, 2, SLOTS).bitcast(U32)
    jj, jf = chip.part(E_J, 2, SLOTS).bitcast(U32), chip.part(E_JF, 2, SLOTS)
    eq = chip.part(E_EQ, PH * TOPK, TOPK)
    slots = chip.part(E_N, 3, SLOTS)
    total = chip.part(E_W, PH)
    cand = chip.part(E_CAND, 2, PH, TOPK * TOPK)
    iota16, iota = chip.iota[:, 0:TOPK], chip.iota
    weight, columns = chip.part(0, S, NK), chip.part(E_SLOT, 3, S)
    hots = chip.part(E_HOT, HOTS, 2 * P)
    a, b = hots[:, :, 0:P], hots[:, :, P:2 * P]

    def free(eng, c, j):
        if not (static(c) and c == 0):
            eng.wait_ge(chip.spread.sem, chip.spread.at(HOTS * c + (j - HOTS + 1)))

    with nc.Block() as block:
        @block.gpsimd
        def _(pool):
            nc.gpsimd.iota(iota[:, :], [[1, P]], base=0, channel_multiplier=0, allow_small_or_imprecise_dtypes=True)\
                .then_inc(chip.table.sem, 1)
            pool.wait_ge(chip.table.sem, chip.table.at(1))

            for tt in range(2):
                pool.wait_ge(chip.columns_there.sem, chip.columns_there.at(tt + 1))
                for t in range(tt * P, (tt + 1) * P, tt + 1):
                    free(pool, t // HOTS, t % HOTS)
                    nc.gpsimd.tensor_scalar(b[:, t % HOTS, :], iota[:, :], columns[:, 1, t:t + 1], None, ALU.is_equal)\
                        .then_inc(chip.hot1.sem, 1)

        @block.vector
        def _(dve):
            step = lambda ins: in_order(dve, chip.dve_step, ins)

            def first(c, j, both=False):
                free(dve, c, j)
                col = lambda n: columns[:, n, bass.ds(HOTS * c + j, 1)]
                if both:
                    nc.vector.tensor_scalar(b[:, j, :], iota[:, :], col(1), None, ALU.is_equal)
                nc.vector.tensor_scalar(a[:, j, :], iota[:, :], col(0), col(2), ALU.is_equal, ALU.mult)\
                    .then_inc(chip.hot0.sem, 1)

            def beside(lo, hi):
                for t in range(lo, hi):
                    first(t // HOTS, t % HOTS)

            def best(values, index, source, spare, lo=0, hi=0):
                both = list(zip(values, index, source, spare))
                at = [lo + (hi - lo) * n // 4 for n in range(5)]
                for half in range(2):
                    k = slice(8 * half, 8 * half + 8)
                    src = [x[3] if half else x[2] for x in both]
                    for x, sr in zip(both, src):
                        last = nc.vector.max(x[0][:, k], sr)
                    chip.dve_step.passed(1)
                    last.then_inc(chip.dve_step.sem, 1)
                    beside(at[2 * half], at[2 * half + 1])
                    dve.wait_ge(chip.dve_step.sem, chip.dve_step.base)
                    for x, sr in zip(both, src):
                        last = nc.vector.max_index(x[1][:, k], x[0][:, k], sr)
                        if half == 0:
                            last = nc.vector.match_replace(x[3], x[0][:, k], sr, -3e38)
                    chip.dve_step.passed(1)
                    last.then_inc(chip.dve_step.sem, 1)
                    beside(at[2 * half + 1], at[2 * half + 2])
                    dve.wait_ge(chip.dve_step.sem, chip.dve_step.base)

            for tt in range(2):
                groups = 8 + PH // 2
                if tt:
                    dve.wait_ge(chip.columns_there.sem, chip.columns_there.at(1))
                upto = lambda n: P * n // groups if tt else 0
                for n in range(8):
                    best([v[:, tt, 2 * n + i, :] for i in range(2)], [ix[:, tt, 2 * n + i, :] for i in range(2)],
                         [s[:, tt, 2 * n + i, :] for i in range(2)], [rest[i][:, 0:NK] for i in range(2)],
                         upto(n), upto(n + 1))
                step(nc.vector.tensor_copy(ixf[:, tt, :, :], ix[:, tt, :, :]))
                vp = v[:, tt, :, :].rearrange("p (h two) k -> p h two k", two=2)
                for h in range(PH):
                    last = nc.vector.tensor_tensor(
                        cand[:, tt, h, :].rearrange("p (a b) -> p a b", b=TOPK),
                        vp[:, h, 0, :].unsqueeze(2).to_broadcast([P, TOPK, TOPK]),
                        vp[:, h, 1, :].unsqueeze(1).to_broadcast([P, TOPK, TOPK]), ALU.add)
                step(last)
                for h in range(0, PH, 2):
                    at = lambda x: [x[:, tt, (h + i) * TOPK:(h + i + 1) * TOPK] for i in range(2)]
                    best(at(tv), at(tj), [cand[:, tt, h + i, :] for i in range(2)], rest,
                         upto(8 + h // 2), upto(9 + h // 2))
                if tt == 0:
                    dve.wait_ge(chip.table.sem, chip.table.at(1))
                for half in range(2):
                    step(nc.vector.tensor_scalar(jj[:, half, :], tj[:, tt, :], 4 if half == 0 else 15, None,
                                                 ALU.logical_shift_right if half == 0 else ALU.bitwise_and))
                    step(nc.vector.tensor_copy(jf[:, half, :], jj[:, half, :]))
                    step(nc.vector.tensor_tensor(eq, iota16.unsqueeze(1).to_broadcast([P, SLOTS, TOPK]),
                                                 jf[:, half, :].unsqueeze(2).to_broadcast([P, SLOTS, TOPK]), ALU.is_equal))
                    e4 = eq.rearrange("p (h k) i -> p h k i", h=PH)
                    sub = ixf[:, tt, :, :].rearrange("p (h two) k -> p h two k", two=2)[:, :, half, :]
                    step(nc.vector.tensor_tensor(e4, e4, sub.unsqueeze(2).to_broadcast([P, PH, TOPK, TOPK]), ALU.mult))
                    step(nc.vector.tensor_reduce(slots[:, half, :], eq, AX.X, ALU.add))
                w = slots[:, 2, :].rearrange("p (h k) -> p h k", h=PH)
                t3 = tv[:, tt, :].rearrange("p (h k) -> p h k", h=PH)
                nc.vector.tensor_tensor(w, t3, t3[:, :, 0:1].to_broadcast([P, PH, TOPK]), ALU.subtract)\
                    .then_inc(chip.maxed.sem, 1)
                dve.wait_ge(chip.exped.sem, chip.exped.at(tt + 1))
                step(nc.vector.tensor_reduce(total, w, AX.X, ALU.add))
                step(nc.vector.reciprocal(total, total))
                nc.vector.tensor_tensor(w, w, total.unsqueeze(2).to_broadcast([P, PH, TOPK]), ALU.mult)\
                    .then_inc(chip.probs.sem, 1)
            dve.wait_ge(chip.columns_there.sem, chip.columns_there.at(2))
            over_tokens(dve, 1, lambda c, j: first(c, j, j % 2 == 1))

        @block.scalar
        def _(act):
            def keep(c, j):
                if j % 2:
                    act.wait_ge(chip.spread.sem, chip.spread.at(HOTS * c + (j + 1)))
                    nc.scalar.activation(weight[:, bass.ds(HOTS * c + (j - 1), 2), :].rearrange("p a b -> p (a b)"),
                                         chip.bank[4 + j // 2][:, 0:2 * P], ACT.Copy).then_inc(chip.kept.sem, 1)
            for tt in range(2):
                act.wait_ge(chip.maxed.sem, chip.maxed.at(tt + 1))
                nc.scalar.activation(slots[:, 2, :], slots[:, 2, :], ACT.Exp).then_inc(chip.exped.sem, 1)
                act.wait_ge(chip.turned.sem, chip.turned.at(tt + 1))
                nc.scalar.activation(columns[:, :, tt * P:(tt + 1) * P],
                                     chip.bank[tt][:, 0:3 * P].rearrange("p (a b) -> p a b", b=P), ACT.Copy)\
                    .then_inc(chip.columns_there.sem, 1)
                over_tokens(act, tt, keep)

        @block.tensor
        def _(pe):
            def spread(c, j, tt):
                if not (static(c) and c == 0) and j % 2 == 0:
                    pe.wait_ge(chip.kept.sem, chip.kept.at(HOTS // 2 * c + (j // 2 - HOTS // 2 + 1)))
                pe.wait_ge(chip.hot0.sem, chip.hot0.at(HOTS * c + (j + 1)))
                if tt == 0:
                    pe.wait_ge(chip.hot1.sem, chip.hot1.at(HOTS * c + (j + 1)))
                elif j % 2 == 0:
                    pe.wait_ge(chip.hot1.sem, chip.hot1.at(HOTS // 2 * c + (P // 2 + j // 2 + 1)))
                nc.tensor.matmul(chip.bank[4 + j // 2][:, (j % 2) * P:(j % 2 + 1) * P], a[:, j, :], b[:, j, :],
                                 start=True, stop=True).then_inc(chip.spread.sem, 1)
            for tt in range(2):
                pe.wait_ge(chip.probs.sem, chip.probs.at(tt + 1))
                for n in range(3):
                    mm = nc.tensor.transpose(chip.bank[tt][:, n * P:(n + 1) * P], slots[:, n, :], chip.ident[:, :])
                mm.then_inc(chip.turned.sem, 1)
                over_tokens(pe, tt, lambda c, j: spread(c, j, tt))
    for sig in (chip.maxed, chip.exped, chip.probs, chip.turned, chip.columns_there):
        sig.passed(2)
    for sig in (chip.hot0, chip.spread):
        sig.passed(S)
    chip.hot1.passed(P + P // 2)
    chip.kept.passed(S // 2)
    chip.table.passed(1)


def stage_experts(chip, stream):
    nc = chip.nc
    weight, f = chip.part(0, S, NK), chip.part(E_HOT, 2, S)
    g_hi, g_lo = chip.extra["act_hi"], chip.extra["act_lo"]
    steps = NK
    with nc.Block() as block:
        @block.sync
        def _(sp):
            stream.load_ahead(sp, 2 * steps)

        @block.tensor
        def _(pe):
            def down(c, j, at):
                stream.chunk(pe, c, j, chip.bank[at][:, 0:S], lambda kt: (chip.hi[:, kt, :], chip.lo[:, kt, :]))

            def up(c, j, k, at, first=False, last=False):
                pe.wait_ge(chip.gated.sem, chip.gated.at(k + 1))
                for half in range(2):
                    w = stream.half(pe, c, j, half)
                    for tt in range(2):
                        q = slice(tt * P, (tt + 1) * P)
                        mm = product(nc, chip.bank[4 + 2 * tt + half][:, :], [((g_hi[:, at, q], g_lo[:, at, q]), w)],
                                     start=first, stop=last)
                    mm.then_inc(stream.used, 1)

            down(0, 0, 0)
            down(0, 1, 1)
            up(0, 2, 0, 0, first=True)
            down(0, 3, 0)
            up(1, 0, 1, 1)
            down(1, 1, 1)
            with pe.Fori(1, steps // 2 - 1) as c:
                up(c, 2, 2 * c, 0)
                down(c, 3, 0)
                up(c, 4, 2 * c + 1, 1)
                down(c, 5, 1)
            c = steps // 2 - 1
            up(c, 2, 2 * c, 0)
            up(c, 3, 2 * c + 1, 1, last=True)

        @block.scalar
        def _(act):
            def gelu(c, j, at):
                stream.round(act, c, j + 2)
                act.wait_ge(stream.used, stream.used_at(NS * c + j))
                nc.scalar.activation(f[:, at, :], chip.bank[at][:, 0:S], ACT.Gelu_apprx_tanh).then_inc(chip.gelu_done.sem, 1)

            gelu(0, 0, 0)
            gelu(0, 1, 1)
            with act.Fori(0, steps // 2 - 1) as c:
                stream.round(act, c, 4)
                gelu(c, 3, 0)
                stream.round(act, c, 6)
                gelu(c, 5, 1)

        @block.vector
        def _(dve):
            def weigh(k, at):
                dve.wait_ge(chip.gelu_done.sem, chip.gelu_done.at(k + 1))
                nc.vector.tensor_tensor(f[:, at, :], f[:, at, :], weight[:, :, k], ALU.mult).then_inc(chip.ffn_step.sem, 1)
                dve.wait_ge(chip.ffn_step.sem, chip.ffn_step.at(2 * k + 1))
                first, rest = split_activations(nc, g_hi[:, at, :], g_lo[:, at, :], f[:, at, :])
                first.then_inc(chip.ffn_step.sem, 1)
                dve.wait_ge(chip.ffn_step.sem, chip.ffn_step.at(2 * k + 2))
                rest().then_inc(chip.gated.sem, 1)

            for k in range(2):
                stream.subtract(dve, 0, k + 2)
                weigh(k, k)
            with dve.Fori(0, steps // 2 - 1) as c:
                stream.subtract(dve, c, 4)
                stream.subtract(dve, c, 5)
                weigh(2 * c + 2, 0)
                stream.subtract(dve, c, 6)
                stream.subtract(dve, c, 7)
                weigh(2 * c + 3, 1)
    chip.gelu_done.passed(steps)
    chip.ffn_step.passed(2 * steps)
    chip.gated.passed(steps)
    stream.g0 += 2 * steps


def stage_finish(chip, out):
    nc = chip.nc
    o = chip.part(0, 2, D)
    norm = Norm(chip, chip.x2, chip.part(8192, KT, S), chip.part(4096, S), chip.part(4096 + S, S),
                lambda kt, g: chip.col("g_final", kt, 1), None, [(0, S)], S, split=False)
    with nc.Block() as block:
        @block.scalar
        def _(act):
            for n in range(4):
                nc.scalar.activation(o[:, n // 2, (n % 2) * 512:(n % 2 + 1) * 512], chip.bank[4 + n][:, :], ACT.Copy)\
                    .then_inc(chip.copied.sem, 1)

        @block.tensor
        def _(pe):
            pe.wait_ge(chip.copied.sem, chip.copied.at(4))
            for kt in range(KT):
                for tt in range(2):
                    mm = nc.tensor.transpose(chip.bank[kt // 2][:, (kt % 2) * S + tt * P:(kt % 2) * S + (tt + 1) * P],
                                             o[:, tt, kt * P:(kt + 1) * P], chip.ident[:, :])
                mm.then_inc(chip.turned.sem, 1)

        @block.vector
        def _(dve):
            for kt in range(KT):
                dve.wait_ge(chip.turned.sem, chip.turned.at(2 * (kt // 2) + 2))
                nc.vector.scalar_tensor_tensor(chip.x2[:, kt, :], chip.bank[kt // 2][:, (kt % 2) * S:(kt % 2 + 1) * S],
                                               chip.mod2[:, 5 * KT + kt:5 * KT + kt + 1], chip.x2[:, kt, :], ALU.mult, ALU.add)
    chip.copied.passed(4)
    chip.turned.passed(KT)
    with nc.Block() as block:
        block.tensor(norm.tensor)
        block.scalar(norm.scalar)
        block.vector(norm.vector)

        @block.sync
        def _(sp):
            sp.wait_ge(chip.h_ready.sem, chip.h_ready.at(KT))
            sp.dma_start(out, norm.h).then_inc(chip.table.sem, 16)
            sp.wait_ge(chip.table.sem, chip.table.at(16))


def build(nc, dram, out):
    with ExitStack() as ctx:
        chip = Chip(ctx, nc, dram)
        segments = []
        for l in range(LAYERS):
            segments += [(dram["ffn"][l][0], FFN_UNITS), (dram["w_mix"][l], 28), (dram["ffn"][l][1], FFN_UNITS)]
        segments += [(dram["w_second"], 28 + KT + 16), (dram["experts"], 2 * NK)]
        stream = Stream(ctx, nc, segments)
        with ExitStack() as first:
            chip.take(first, T2, A_WORDS)
            chip.take_more(first, "pooling", pool_w=([P, 2, P], F32), pool_inv=([P, 2, S], F32))
            stage_setup(chip, stream)
            for l in range(LAYERS):
                last = l == LAYERS - 1
                width = S if last else T2
                groups = [(0, S)] if last else [(0, S), (S, T2)]
                with ExitStack() as sublayer:
                    take_for_ffn(chip, sublayer, f"ffn{l}0")
                    if l == 0:
                        stage_first_mod(chip)
                        work = Modulation(chip, 12, 30, 2)
                        stage_ffn(chip, stream, l, 0, T2, work, lambda dve: finish_mod(chip, dve, 0, 3, 9))
                    else:
                        work = Modulation(chip, 72, 24, 1)
                        stage_ffn(chip, stream, l, 0, T2, work, lambda dve: finish_mod2(chip, dve))
                with ExitStack() as sublayer:
                    chip.take_more(sublayer, f"mixer{l}", A_MIXER)
                    stage_mix_in(chip, stream, l, last)
                    stage_mix(chip, stream, l, last)
                    stage_add_product(chip, stream, chip.part(A_X, KT, T2), chip.part(A_Y, KT, T2),
                                      lambda n, g: chip.mods[l][:, 5 * KT + n, g:g + 1], groups)
                with ExitStack() as sublayer:
                    take_for_ffn(chip, sublayer, f"ffn{l}1")
                    work = Modulation(chip, 42, 30, 2) if l == 0 else None
                    stage_ffn(chip, stream, l, 1, width, work, lambda dve: finish_mod(chip, dve, 1, 0, 9))
            stage_final_norm(chip)
        with ExitStack() as second:
            chip.take(second, S, B_WORDS)
            chip.take_more(second, "experts", act_hi=([P, 2, S], F32R), act_lo=([P, 2, S], F32R))
            stage_proj(chip, stream)
            stage_rope(chip)
            stage_retention(chip)
            stage_compress(chip)
            stage_sparse(chip)
            stage_add_product(chip, stream, chip.x2, chip.part(B_Y, KT, S),
                              lambda n, g: chip.mod2[:, 2 * KT + n:2 * KT + n + 1], [(0, S)])
            stage_expert_scores(chip, stream)
            stage_retrieve(chip)
            stage_experts(chip, stream)
            stage_finish(chip, out)


def _layout(inp):
    def blocks(w):
        n = w.shape[1]
        return w.reshape(KT, P, n // P, P).transpose(2, 1, 0, 3).reshape(n // P, P, UNIT)

    def rows(w):
        return w.reshape(4, 2, P, 512).transpose(0, 2, 1, 3).reshape(4, P, UNIT)

    def pack(w):
        k, n = w.shape
        return w.reshape(k // P, P, n // 256, 256).transpose(2, 1, 0, 3).reshape(n // 256, P, k // P * 256)

    def vec(v):
        return v.reshape(-1, P).T

    f = np.float32
    a = {}
    a["w_mods"] = np.concatenate([pack(w) for w in inp["w_mod"]] + [pack(inp["w_ada_2"][0])])
    ffn = []
    for l in range(LAYERS):
        for k in range(2):
            a_b = blocks(inp["ffn_w_in"][l, k])
            w2 = inp["ffn_w_out"][l, k].reshape(FT, P, KT, P)
            n0 = 0
            for nh in HIDDEN:
                for n in range(n0, n0 + nh):
                    ffn += [a_b[n], a_b[FT + n]]
                part = np.zeros((KT, P, KT, P), w2.dtype)
                part[:, :, 0:nh] = w2[n0:n0 + nh].transpose(2, 1, 0, 3)
                ffn += list(part.reshape(KT, P, UNIT))
                n0 += nh
    a["ffn"] = np.stack(ffn).reshape(LAYERS, 2, FFN_UNITS, P, UNIT)
    a["w_mix"] = np.stack([np.concatenate([blocks(inp["w_in"][l][:, 0:2 * D]), rows(inp["w_in"][l][:, 2 * D:]),
                                           blocks(inp["w_out"][l])]) for l in range(LAYERS)])
    x = np.concatenate([inp["x"][0], inp["ctx"][0]])
    a["x"] = x.T.reshape(KT, P, T2).transpose(1, 0, 2)
    cc = np.stack([vec(inp["c"][0]), vec(inp["c_ctx"])], axis=2).reshape(P, KT * 2)
    parts = {"cc": cc, "c2": vec(inp["c_2"][0]), "b_mod": vec(inp["b_mod"]), "norm_g": vec(inp["norm_g"]),
             "final_g": vec(inp["final_g"]), "conv_w": vec(inp["conv_w"]), "pool_scale": vec(inp["pool_scale"]),
             "b_ada": vec(inp["b_ada_2"]), "g_mix": vec(inp["g_norm_mix_2"]), "g_ffn": vec(inp["g_norm_ffn_2"]),
             "g_final": vec(inp["g_norm_final_2"]), "b_cmp_k": vec(inp["b_cmp_k1_2"]), "b_cmp_v": vec(inp["b_cmp_v1_2"]),
             "pe_k": vec(inp["pe_cmp_k_2"]), "pe_v": vec(inp["pe_cmp_v_2"])}
    a["cols"] = np.concatenate([parts[n] for n in COLS], axis=1)
    assert a["cols"].shape[1] == N_COLS
    rpb = np.zeros((LAYERS, NA_H, 7, 2 * GRID - 1), inp["rpb"].dtype)
    rpb[..., GRID - 16:GRID + 15] = inp["rpb"][:, :, 4:11, :]
    t = np.stack([rpb[..., GRID - 1 - q:2 * GRID - 1 - q] for q in range(GRID)], axis=1)
    a["rel_bias"] = np.concatenate([t[:, :, :, 1:7], t[:, :, :, 0:6]], axis=1).reshape(LAYERS, P, NA_H * BIAS_ROWS * GRID)
    pw = np.zeros((LAYERS, 2, 2, 64, 2, 64), inp["pool_w"].dtype)
    for g in range(4):
        pw[:, g // 2, g % 2, :, g % 2, :] = inp["pool_w"][:, g]
    a["pool_w"] = pw.reshape(LAYERS, 2, P, P).transpose(0, 2, 1, 3)
    cnt = np.zeros((4, S), f)
    for g, w in enumerate((2, 4, 8, 16)):
        tt = np.arange(S)
        cnt[g] = np.clip(tt + w - w // 2, 0, S) - np.clip(tt - w // 2, 0, S)
    a["pool_inv"] = np.repeat((f(1) / cnt).reshape(2, 2, 1, S), 64, axis=2).reshape(2, P, S).transpose(1, 0, 2)

    w = inp["w_in_2"][0]
    cut = np.split(w, np.cumsum([512, 512, 512, 512, 512, 128, 128, 128, 128, 128, 128, 24])[:-1], axis=1)
    rq, rk, rv, rg, nq, kc, vc, ks, vs, kw, vw, gate = cut
    nq = nq.reshape(D, 2, 4, 64).transpose(0, 2, 1, 3).reshape(D, 512)
    gate = np.concatenate([gate.reshape(D, 2, 4, 3).transpose(0, 2, 1, 3).reshape(D, 24), np.zeros((D, 232), w.dtype)], axis=1)
    fm = np.concatenate([rq, rk, nq, kc, ks, kw, vc, rg], axis=1)
    tm = rows(np.concatenate([vs, vw, gate], axis=1))
    wo = inp["w_out_2"][0]
    wo = np.concatenate([wo[:512], wo[512:].reshape(2, 4, 64, D).transpose(1, 0, 2, 3).reshape(512, D)])
    a["subkeys"] = inp["peer_subkeys_2"][0].reshape(16, NK, P).transpose(2, 0, 1).reshape(P, 16 * NK)
    a["w_second"] = np.concatenate([blocks(fm), rows(rv), tm, blocks(wo), blocks(inp["w_peer_q_2"][0])])
    down = inp["peer_down_2"][0].reshape(NK, NK, KT, P).transpose(1, 3, 2, 0).reshape(NK, P, UNIT)
    up = inp["peer_up_2"][0].reshape(NK, NK, D).transpose(1, 0, 2)
    order = [down[0], down[1]]
    for k in range(NK):
        order += [up[k]] + ([down[k + 2]] if k + 2 < NK else [])
    a["experts"] = np.stack(order)
    for k, nm in (("k", "w_cmp_k"), ("v", "w_cmp_v")):
        w1 = inp[f"{nm}1_2"][0].reshape(16, P, 256).transpose(1, 0, 2)
        w2 = inp[f"{nm}2_2"][0].reshape(2, P, 64).transpose(1, 0, 2)
        a[f"cmp_{k}1"], a[f"cmp_{k}2"] = w1, w2

    tab = {}
    for dim, name in ((128, "128"), (64, "64")):
        inv = f(10000.0) ** (-np.arange(0, dim, 2, dtype=f) / f(dim))
        ang = np.arange(S, dtype=f)[None, :] * inv[:, None]
        tab["cos" + name] = np.tile(np.cos(ang).astype(f), (P // (dim // 2), 1))
        tab["sin" + name] = np.tile(np.sin(ang).astype(f), (P // (dim // 2), 1))
        perm = np.zeros((P, P), f)
        for m in range(P):
            half = dim // 2
            if m % dim < half:
                perm[m + half, m] = -1
            else:
                perm[m - half, m] = 1
        tab["perm" + name] = perm
    log_g = np.log1p(-np.exp2(f(-5.0) - np.arange(RET_H, dtype=f))).astype(f)
    diff = np.arange(S, dtype=f)[None, :] - np.arange(P, dtype=f)[:, None]
    dec = np.where(diff >= 0, np.exp(np.where(diff >= 0, diff, 0)[None] * log_g[:, None, None]), 0).astype(f)
    tab["decay"] = (dec * f(128 ** -0.5)).transpose(1, 0, 2).reshape(P, RET_H * S)
    q = np.arange(P)
    tab["causal"] = np.concatenate([np.zeros((P, P), f), np.where(q[None, :] <= q[:, None], 0, NEG).astype(f)], axis=1)
    n = np.arange(16)
    ok = np.stack([(CMP_STRIDE * n[None, :] + CMP_LEN - 1 <= q[:, None] + P * qt) & (n[None, :] < NCB) for qt in range(2)], axis=1)
    tab["cmp_add"] = np.where(ok, 0, NEG).astype(f).reshape(P, 32)
    tab["cmp_mask"] = ok.astype(f).reshape(P, 32)
    a["tables"] = np.concatenate([tab[n] for n in TAB], axis=1)
    assert a["tables"].shape[1] == N_TAB
    return {k: np.ascontiguousarray(v) for k, v in a.items()}


def kernel(**inputs):
    import concourse.bacc as bacc
    from concourse.bass_utils import run_bass_kernel_spmd

    arrays = _layout({k: np.asarray(v) for k, v in inputs.items()})
    nc = bacc.Bacc("TRN2", target_bir_lowering=False, num_devices=1)
    dram = {k: nc.dram_tensor(f"in_{k}", v.shape, mybir.dt.from_np(v.dtype), kind="ExternalInput").ap()
            for k, v in arrays.items()}
    out = nc.dram_tensor("out_x", (P, KT, S), F32, kind="ExternalOutput").ap()
    build(nc, dram, out)
    r = run_bass_kernel_spmd(nc, [{f"in_{k}": v for k, v in arrays.items()}], core_ids=[0])
    return r.results[0]["out_x"].transpose(2, 1, 0).reshape(1, S, D)
```
